# Optimizing a Trainium2 kernel written in Bass

```python
import math
import jax, jax.numpy as jnp
from jax import lax
import numpy as np

D_MODEL = 1024
BATCH = 1
SEQ = 1024
DEPTH = 1

N_MIXERS = 2
N_ATTN_LAYERS = (DEPTH + N_MIXERS - 1) // N_MIXERS
N_SSM_LAYERS = DEPTH // N_MIXERS

ATTN_HEAD_DIM = 64
ATTN_HEADS = D_MODEL // ATTN_HEAD_DIM
Q_BLOCK = 128
SSM_EXPAND = 2
SSM_D_INNER = SSM_EXPAND * D_MODEL
SSM_HEAD_DIM = 64
SSM_HEADS = SSM_D_INNER // SSM_HEAD_DIM
SSM_GROUPS = 8
SSM_STATE = 128
SSM_CONV = 4
SSM_CHUNK = 128
SSM_XBC = SSM_D_INNER + 2 * SSM_GROUPS * SSM_STATE
FFN_DIM = 2816
FFN_CONV = 3
PLE_DIM = 256

LN_EPS = 1e-5
RMS_EPS = 1e-5
DEEPNORM_ALPHA = (2 * DEPTH) ** 0.25
DEEPNORM_BETA = (8 * DEPTH) ** -0.25


def layer_norm(x, g, b):
    xf = x.astype(jnp.float32)
    mu = jnp.mean(xf, axis=-1, keepdims=True)
    var = jnp.mean(jnp.square(xf - mu), axis=-1, keepdims=True)
    return ((xf - mu) * lax.rsqrt(var + LN_EPS) * g + b).astype(x.dtype)

def causal_dwconv(u, w, b):
    K = w.shape[0]
    S = u.shape[1]
    up = jnp.pad(u, ((0, 0), (K - 1, 0), (0, 0)))
    out = b
    for k in range(K):
        out = out + up[:, k:k + S] * w[k]
    return out

def fox_mixer(x, w_in, b_f, w_out):
    Bsz, S, _ = x.shape
    H, Dh = ATTN_HEADS, ATTN_HEAD_DIM
    proj = x @ w_in
    q, k, v, f_logit = jnp.split(proj, [D_MODEL, 2 * D_MODEL, 3 * D_MODEL], axis=-1)
    q = q.reshape(Bsz, S, H, Dh).transpose(0, 2, 1, 3)
    k = k.reshape(Bsz, S, H, Dh).transpose(0, 2, 1, 3)
    v = v.reshape(Bsz, S, H, Dh).transpose(0, 2, 1, 3)
    log_f = jax.nn.log_sigmoid(f_logit.astype(jnp.float32) + b_f)
    c = jnp.cumsum(log_f, axis=1).transpose(0, 2, 1)
    nb = S // Q_BLOCK
    qb = q.reshape(Bsz, H, nb, Q_BLOCK, Dh).transpose(2, 0, 1, 3, 4)
    cqb = c.reshape(Bsz, H, nb, Q_BLOCK).transpose(2, 0, 1, 3)
    kpos = jnp.arange(S)
    scale = 1.0 / math.sqrt(Dh)

    def block(args):
        qi, cqi, bi = args
        s = jnp.einsum('bhqd,bhkd->bhqk', qi, k).astype(jnp.float32) * scale
        s = s + cqi[..., None] - c[:, :, None, :]
        qpos = bi * Q_BLOCK + jnp.arange(Q_BLOCK)
        s = jnp.where(kpos[None, :] <= qpos[:, None], s, -jnp.inf)
        pr = jax.nn.softmax(s, axis=-1)
        return jnp.einsum('bhqk,bhkd->bhqd', pr.astype(v.dtype), v)

    o = lax.map(block, (qb, cqb, jnp.arange(nb)))
    o = o.transpose(1, 0, 3, 2, 4).reshape(Bsz, S, D_MODEL)
    return o @ w_out

def ssd_scan(xh, dt, A, Bm, Cm):
    Bsz, S = xh.shape[0], xh.shape[1]
    G, R, P, N, Q = SSM_GROUPS, SSM_HEADS // SSM_GROUPS, SSM_HEAD_DIM, SSM_STATE, SSM_CHUNK
    nc = S // Q

    def to_chunks(t):
        return jnp.moveaxis(t.reshape((Bsz, nc, Q) + t.shape[2:]), 1, 0)

    xc = to_chunks(xh.reshape(Bsz, S, G, R, P))
    dtc = to_chunks(dt.reshape(Bsz, S, G, R))
    Bc = to_chunks(Bm)
    Cc = to_chunks(Cm)
    A_g = A.reshape(G, R)
    tri = jnp.tril(jnp.ones((Q, Q), dtype=bool))[None, :, :, None, None]

    def step(state, inp):
        x_, dt_, B_, C_ = inp
        acum = jnp.cumsum(dt_ * A_g, axis=1)
        seg = acum[:, :, None] - acum[:, None, :]
        L = jnp.exp(jnp.where(tri, seg, -jnp.inf))
        CB = jnp.einsum('btgn,bsgn->btsg', C_, B_)
        y_intra = jnp.einsum('btsg,btsgr,bsgr,bsgrp->btgrp', CB, L, dt_, x_)
        y_inter = jnp.einsum('btgn,bgrpn,btgr->btgrp', C_, state, jnp.exp(acum))
        w_end = jnp.exp(acum[:, -1:] - acum) * dt_
        new_state = state * jnp.exp(acum[:, -1])[..., None, None] + \
            jnp.einsum('bsgn,bsgr,bsgrp->bgrpn', B_, w_end, x_)
        return new_state, (y_intra + y_inter).astype(jnp.float32)

    state0 = jnp.zeros((Bsz, G, R, P, N), jnp.float32)
    _, y = lax.scan(step, state0, (xc, dtc, Bc, Cc))
    return jnp.moveaxis(y, 0, 1).reshape(Bsz, S, SSM_HEADS, P)

def ssd_mixer(x, w_in, conv_w, conv_b, dt_bias, A_log, D_skip, norm_w, w_out):
    Bsz, S, _ = x.shape
    GN = SSM_GROUPS * SSM_STATE
    proj = x @ w_in
    z, xBC, dt_raw = jnp.split(proj, [SSM_D_INNER, SSM_D_INNER + SSM_XBC], axis=-1)
    xBC = jax.nn.silu(causal_dwconv(xBC, conv_w, conv_b))
    xs, Bm, Cm = jnp.split(xBC, [SSM_D_INNER, SSM_D_INNER + GN], axis=-1)
    dt = jax.nn.softplus(dt_raw.astype(jnp.float32) + dt_bias)
    A = -jnp.exp(A_log.astype(jnp.float32))
    xh = xs.reshape(Bsz, S, SSM_HEADS, SSM_HEAD_DIM)
    y = ssd_scan(xh, dt, A,
                 Bm.reshape(Bsz, S, SSM_GROUPS, SSM_STATE),
                 Cm.reshape(Bsz, S, SSM_GROUPS, SSM_STATE))
    y = y + D_skip[:, None] * xh
    y = y.reshape(Bsz, S, SSM_D_INNER) * jax.nn.silu(z.astype(jnp.float32))
    yg = y.reshape(Bsz, S, SSM_GROUPS, SSM_D_INNER // SSM_GROUPS)
    yg = yg * lax.rsqrt(jnp.mean(jnp.square(yg), axis=-1, keepdims=True) + RMS_EPS)
    y = yg.reshape(Bsz, S, SSM_D_INNER) * norm_w
    return y.astype(x.dtype) @ w_out

def conv_ffn(x, w_up, conv_w, conv_b, w_down):
    u, g = jnp.split(x @ w_up, [FFN_DIM], axis=-1)
    g = causal_dwconv(g, conv_w, conv_b)
    return (jax.nn.gelu(g, approximate=False) * u) @ w_down

def first_inputs(seed: int = 0) -> dict:
    key = jax.random.key(seed)
    ks = iter(jax.random.split(key, 40))

    def nrm(shape, scale):
        return jax.random.normal(next(ks), shape, jnp.float32) * scale

    D, H = D_MODEL, ATTN_HEADS
    NA, NB = N_ATTN_LAYERS, N_SSM_LAYERS
    beta = DEEPNORM_BETA
    x = nrm((BATCH, SEQ, D), 1.0)
    p = nrm((DEPTH, BATCH, SEQ, PLE_DIM), 1.0)
    attn_w_in = nrm((NA, D, 3 * D + H), D ** -0.5)
    attn_w_in = attn_w_in.at[:, :, 2 * D:3 * D].multiply(beta)
    attn_b_f = jax.random.uniform(next(ks), (NA, H), jnp.float32, 1.0, 6.0)
    attn_w_out = nrm((NA, D, D), beta * D ** -0.5)
    ssm_in_dim = 2 * SSM_D_INNER + 2 * SSM_GROUPS * SSM_STATE + SSM_HEADS
    ssm_w_in = nrm((NB, D, ssm_in_dim), D ** -0.5)
    ssm_conv_w = nrm((NB, SSM_CONV, SSM_XBC), SSM_CONV ** -0.5)
    ssm_conv_b = nrm((NB, SSM_XBC), 0.02)
    dt0 = jnp.exp(jax.random.uniform(next(ks), (NB, SSM_HEADS), jnp.float32,
                                     math.log(1e-3), math.log(1e-1)))
    ssm_dt_bias = dt0 + jnp.log(-jnp.expm1(-dt0))
    ssm_A_log = jnp.log(jax.random.uniform(next(ks), (NB, SSM_HEADS), jnp.float32, 1.0, 16.0))
    ssm_D = 1.0 + nrm((NB, SSM_HEADS), 0.1)
    ssm_norm_w = 1.0 + nrm((NB, SSM_D_INNER), 0.05)
    ssm_w_out = nrm((NB, SSM_D_INNER, D), beta * SSM_D_INNER ** -0.5)
    ln_mix_g = 1.0 + nrm((DEPTH, D), 0.05)
    ln_mix_b = nrm((DEPTH, D), 0.02)
    ffn_w_up = nrm((DEPTH, D, 2 * FFN_DIM), D ** -0.5)
    ffn_conv_w = nrm((DEPTH, FFN_CONV, FFN_DIM), FFN_CONV ** -0.5)
    ffn_conv_b = nrm((DEPTH, FFN_DIM), 0.02)
    ffn_w_down = nrm((DEPTH, FFN_DIM, D), beta * FFN_DIM ** -0.5)
    ln_ffn_g = 1.0 + nrm((DEPTH, D), 0.05)
    ln_ffn_b = nrm((DEPTH, D), 0.02)
    ple_w_proj = nrm((DEPTH, PLE_DIM, D), beta * PLE_DIM ** -0.5)
    ple_w_gate = nrm((DEPTH, D, D), D ** -0.5)
    ple_b_gate = nrm((DEPTH, D), 0.02)
    return {"x": x, "p": p,
            "attn_w_in": attn_w_in, "attn_b_f": attn_b_f, "attn_w_out": attn_w_out,
            "ssm_w_in": ssm_w_in, "ssm_conv_w": ssm_conv_w, "ssm_conv_b": ssm_conv_b,
            "ssm_dt_bias": ssm_dt_bias, "ssm_A_log": ssm_A_log, "ssm_D": ssm_D,
            "ssm_norm_w": ssm_norm_w, "ssm_w_out": ssm_w_out,
            "ln_mix_g": ln_mix_g, "ln_mix_b": ln_mix_b,
            "ffn_w_up": ffn_w_up, "ffn_conv_w": ffn_conv_w, "ffn_conv_b": ffn_conv_b,
            "ffn_w_down": ffn_w_down, "ln_ffn_g": ln_ffn_g, "ln_ffn_b": ln_ffn_b,
            "ple_w_proj": ple_w_proj, "ple_w_gate": ple_w_gate, "ple_b_gate": ple_b_gate}

def first_block(x, p, attn_w_in, attn_b_f, attn_w_out, ssm_w_in, ssm_conv_w, ssm_conv_b,
              ssm_dt_bias, ssm_A_log, ssm_D, ssm_norm_w, ssm_w_out, ln_mix_g, ln_mix_b,
              ffn_w_up, ffn_conv_w, ffn_conv_b, ffn_w_down, ln_ffn_g, ln_ffn_b,
              ple_w_proj, ple_w_gate, ple_b_gate):
    for i in range(DEPTH):
        j = i // N_MIXERS
        if i % N_MIXERS == 0:
            mix = fox_mixer(x, attn_w_in[j], attn_b_f[j], attn_w_out[j])
        else:
            mix = ssd_mixer(x, ssm_w_in[j], ssm_conv_w[j], ssm_conv_b[j], ssm_dt_bias[j],
                            ssm_A_log[j], ssm_D[j], ssm_norm_w[j], ssm_w_out[j])
        x = layer_norm(DEEPNORM_ALPHA * x + mix, ln_mix_g[i], ln_mix_b[i])
        ffn = conv_ffn(x, ffn_w_up[i], ffn_conv_w[i], ffn_conv_b[i], ffn_w_down[i])
        x = layer_norm(DEEPNORM_ALPHA * x + ffn, ln_ffn_g[i], ln_ffn_b[i])
        gate = jax.nn.sigmoid(x @ ple_w_gate[i] + ple_b_gate[i])
        x = x + gate * (p[i] @ ple_w_proj[i])
    return x


RET_HEADS = 4
RET_HEAD_DIM = D_MODEL // 2 // RET_HEADS
RET_WIDTH = RET_HEADS * RET_HEAD_DIM
RET_CHUNK = 128
DN_HEADS = 4
DN_HEAD_DIM = D_MODEL // 2 // DN_HEADS
DN_WIDTH = DN_HEADS * DN_HEAD_DIM
DN_CHUNK = 64
CONV_WIDTH = 4
ROPE_THETA = 10000.0
N_GROUPS = 4
EXPERTS_PER_GROUP = 8
N_EXPERTS = N_GROUPS * EXPERTS_PER_GROUP
TOP_K = 2
D_EXPERT = D_MODEL // 2
N_MOD = 6
NORM_EPS = 1e-6
IN_COLS = 4 * RET_WIDTH + 4 * DN_WIDTH + 2 * DN_HEADS


def rmsnorm(x, w=None):
    xf = x.astype(jnp.float32)
    y = xf * lax.rsqrt(jnp.mean(xf * xf, axis=-1, keepdims=True) + NORM_EPS)
    if w is not None:
        y = y * w.astype(jnp.float32)
    return y.astype(x.dtype)

def l2norm(x):
    return x * lax.rsqrt(jnp.sum(x * x, axis=-1, keepdims=True) + NORM_EPS)

def modulate(h, shift, scale):
    return h * (1.0 + scale[:, None, :]) + shift[:, None, :]

def rotary(x, positions):
    dh = x.shape[-1]
    inv_freq = ROPE_THETA ** (-jnp.arange(0, dh, 2, dtype=jnp.float32) / dh)
    ang = positions.astype(jnp.float32)[..., None] * inv_freq
    cos, sin = jnp.cos(ang)[:, :, None, :], jnp.sin(ang)[:, :, None, :]
    xf = x.astype(jnp.float32)
    x1, x2 = xf[..., : dh // 2], xf[..., dh // 2:]
    return jnp.concatenate([x1 * cos - x2 * sin, x2 * cos + x1 * sin], axis=-1)

def retention(q, k, v):
    B, T, H, Dh = q.shape
    C = RET_CHUNK
    N = T // C
    log_gamma = jnp.log1p(-jnp.power(2.0, -5.0 - jnp.arange(H, dtype=jnp.float32)))
    q = q.astype(jnp.float32).reshape(B, N, C, H, Dh)
    k = (k.astype(jnp.float32) * Dh ** -0.5).reshape(B, N, C, H, Dh)
    v = v.astype(jnp.float32).reshape(B, N, C, H, Dh)
    idx = jnp.arange(C, dtype=jnp.float32)
    rel = idx[:, None] - idx[None, :]
    causal = rel >= 0
    decay = jnp.where(causal[None], jnp.exp(log_gamma[:, None, None] * jnp.where(causal, rel, 0.0)[None]), 0.0)
    scores = jnp.einsum('bnihd,bnjhd->bnhij', q, k) * decay[None, None]
    inner = jnp.einsum('bnhij,bnjhd->bnihd', scores, v)
    k_w = k * jnp.exp(log_gamma[None, :] * (C - 1 - idx)[:, None])[:, :, None]
    incr = jnp.einsum('bnjhk,bnjhv->nbhkv', k_w, v)
    chunk_decay = jnp.exp(log_gamma * C)[None, :, None, None]

    def step(state, incr_n):
        return chunk_decay * state + incr_n, state

    _, s_prev = lax.scan(step, jnp.zeros((B, H, Dh, Dh), jnp.float32), incr)
    q_w = q * jnp.exp(log_gamma[None, :] * (idx + 1.0)[:, None])[:, :, None]
    cross = jnp.einsum('bnihk,nbhkv->bnihv', q_w, s_prev)
    return (inner + cross).reshape(B, T, H, Dh)

def causal_dwconv_2(x, w):
    k = w.shape[0]
    return lax.conv_general_dilated(x, w[:, None, :].astype(x.dtype), window_strides=(1,), padding=((k - 1, 0),),
                                    dimension_numbers=('NWC', 'WIO', 'NWC'), feature_group_count=x.shape[-1])

def gated_delta_rule(q, k, v, g, beta):
    B, T, H, Dh = q.shape
    C = DN_CHUNK
    N = T // C
    to_chunks = lambda t: t.reshape(B, N, C, H, -1).transpose(0, 3, 1, 2, 4)
    q, k, v = to_chunks(q), to_chunks(k), to_chunks(v)
    g = jnp.cumsum(g.reshape(B, N, C, H).transpose(0, 3, 1, 2), axis=-1)
    beta = beta.reshape(B, N, C, H).transpose(0, 3, 1, 2)
    k_beta = k * beta[..., None]
    v_beta = v * beta[..., None]
    tri_incl = jnp.tril(jnp.ones((C, C), bool))
    tri_strict = jnp.tril(jnp.ones((C, C), bool), -1)
    decay = jnp.exp(jnp.where(tri_incl, g[..., :, None] - g[..., None, :], -jnp.inf))
    a_mat = jnp.where(tri_strict, (k_beta @ jnp.swapaxes(k, -1, -2)) * decay, 0.0)
    eye = jnp.eye(C, dtype=jnp.float32)
    t_mat = lax.linalg.triangular_solve(eye + a_mat, jnp.broadcast_to(eye, a_mat.shape),
                                        left_side=True, lower=True, unit_diagonal=True)
    u = t_mat @ v_beta
    w = t_mat @ (k_beta * jnp.exp(g)[..., None])
    attn = (q @ jnp.swapaxes(k, -1, -2)) * decay
    q_g = q * jnp.exp(g)[..., None]
    k_tail = k * jnp.exp(g[..., -1:] - g)[..., None]
    g_last = jnp.exp(g[..., -1])
    lead = lambda t: jnp.moveaxis(t, 2, 0)

    def step(state, inp):
        u_n, w_n, qg_n, kt_n, attn_n, gl_n = inp
        v_new = u_n - w_n @ state
        o_n = qg_n @ state + attn_n @ v_new
        state = state * gl_n[..., None, None] + jnp.swapaxes(kt_n, -1, -2) @ v_new
        return state, o_n

    _, o = lax.scan(step, jnp.zeros((B, H, Dh, Dh), jnp.float32),
                    (lead(u), lead(w), lead(q_g), lead(k_tail), lead(attn), lead(g_last)))
    return o.transpose(1, 0, 3, 2, 4).reshape(B, T, H, Dh)

def hierarchical_moe(h, w_group, b_group, w_expert, b_expert, w1, w3, w2):
    B, T, D = h.shape
    xf = h.reshape(-1, D)
    n = xf.shape[0]
    group_probs = jax.nn.softmax((xf @ w_group + b_group).astype(jnp.float32), axis=-1)
    p_group, g_idx = lax.top_k(group_probs, 1)
    e_logits = (xf @ w_expert + b_expert).astype(jnp.float32).reshape(n, N_GROUPS, EXPERTS_PER_GROUP)
    e_logits = jnp.take_along_axis(e_logits, g_idx[:, :, None], axis=1)[:, 0]
    p_exp, e_local = lax.top_k(jax.nn.softmax(e_logits, axis=-1), TOP_K)
    gate = p_group * p_exp / jnp.sum(p_exp, axis=-1, keepdims=True)
    flat_e = (g_idx * EXPERTS_PER_GROUP + e_local).reshape(-1)
    order = jnp.argsort(flat_e)
    tok = order // TOP_K
    group_sizes = jnp.bincount(flat_e, length=N_EXPERTS).astype(jnp.int32)
    xs = xf[tok]
    hid = jax.nn.silu(lax.ragged_dot(xs, w1, group_sizes)) * lax.ragged_dot(xs, w3, group_sizes)
    ys = lax.ragged_dot(hid.astype(xs.dtype), w2, group_sizes) * gate.reshape(-1)[order][:, None].astype(xs.dtype)
    return jax.ops.segment_sum(ys, tok, num_segments=n).reshape(B, T, D)

def second_inputs(seed: int = 0) -> dict:
    key = jax.random.key(seed)
    ks = jax.random.split(key, 24)
    f32 = jnp.float32
    nrm = lambda k, shape, s: jax.random.normal(k, shape, f32) * s
    dt = jnp.exp(jax.random.uniform(ks[9], (DEPTH, DN_HEADS), f32, np.log(1e-3), np.log(1e-1)))
    return {
        'x': nrm(ks[0], (BATCH, SEQ, D_MODEL), 1.0),
        'c': nrm(ks[1], (BATCH, D_MODEL), 1.0),
        'positions': jnp.broadcast_to(jnp.arange(SEQ, dtype=jnp.int32)[None], (BATCH, SEQ)),
        'w_ada': nrm(ks[2], (DEPTH, D_MODEL, N_MOD * D_MODEL), D_MODEL ** -0.5),
        'b_ada': nrm(ks[3], (DEPTH, N_MOD * D_MODEL), 0.01),
        'norm1_w': 1.0 + nrm(ks[4], (DEPTH, D_MODEL), 0.01),
        'w_in': nrm(ks[5], (DEPTH, D_MODEL, IN_COLS), D_MODEL ** -0.5),
        'conv_w': nrm(ks[6], (DEPTH, CONV_WIDTH, 3 * DN_WIDTH), CONV_WIDTH ** -0.5),
        'a_log': jnp.log(jax.random.uniform(ks[7], (DEPTH, DN_HEADS), f32, 1.0, 16.0)),
        'dt_bias': dt + jnp.log(-jnp.expm1(-dt)),
        'dn_norm_w': 1.0 + nrm(ks[8], (DEPTH, DN_HEAD_DIM), 0.01),
        'w_out': nrm(ks[10], (DEPTH, D_MODEL, D_MODEL), D_MODEL ** -0.5),
        'norm2_w': 1.0 + nrm(ks[11], (DEPTH, D_MODEL), 0.01),
        'w_group': nrm(ks[12], (DEPTH, D_MODEL, N_GROUPS), D_MODEL ** -0.5),
        'b_group': nrm(ks[13], (DEPTH, N_GROUPS), 0.01),
        'w_expert': nrm(ks[14], (DEPTH, D_MODEL, N_EXPERTS), D_MODEL ** -0.5),
        'b_expert': nrm(ks[15], (DEPTH, N_EXPERTS), 0.01),
        'w1': nrm(ks[16], (DEPTH, N_EXPERTS, D_MODEL, D_EXPERT), D_MODEL ** -0.5),
        'w3': nrm(ks[17], (DEPTH, N_EXPERTS, D_MODEL, D_EXPERT), D_MODEL ** -0.5),
        'w2': nrm(ks[18], (DEPTH, N_EXPERTS, D_EXPERT, D_MODEL), D_EXPERT ** -0.5),
        'final_norm_w': 1.0 + nrm(ks[19], (D_MODEL,), 0.01),
    }

def second_block(x, c, positions, w_ada, b_ada, norm1_w, w_in, conv_w, a_log, dt_bias, dn_norm_w, w_out,
              norm2_w, w_group, b_group, w_expert, b_expert, w1, w3, w2, final_norm_w):
    B, T, D = x.shape
    cuts = [RET_WIDTH, 2 * RET_WIDTH, 3 * RET_WIDTH, 4 * RET_WIDTH,
            4 * RET_WIDTH + DN_WIDTH, 4 * RET_WIDTH + 2 * DN_WIDTH, 4 * RET_WIDTH + 3 * DN_WIDTH,
            4 * RET_WIDTH + 4 * DN_WIDTH, 4 * RET_WIDTH + 4 * DN_WIDTH + DN_HEADS]
    for l in range(DEPTH):
        mod = jax.nn.silu(c) @ w_ada[l] + b_ada[l]
        shift1, scale1, gate1, shift2, scale2, gate2 = jnp.split(mod, N_MOD, axis=-1)

        h = modulate(rmsnorm(x, norm1_w[l]), shift1, scale1)
        proj = h @ w_in[l]
        r_q, r_k, r_v, r_g, d_q, d_k, d_v, d_z, d_a, d_b = jnp.split(proj, cuts, axis=-1)

        heads = lambda t, nh: t.reshape(B, T, nh, -1)
        rq = rotary(heads(r_q, RET_HEADS), positions)
        rk = rotary(heads(r_k, RET_HEADS), positions)
        ret = retention(rq, rk, heads(r_v, RET_HEADS))
        ret = rmsnorm(ret).reshape(B, T, RET_WIDTH) * jax.nn.silu(r_g.astype(jnp.float32))

        qkv = jax.nn.silu(causal_dwconv_2(jnp.concatenate([d_q, d_k, d_v], axis=-1), conv_w[l]))
        cq, ck, cv = jnp.split(qkv.astype(jnp.float32), 3, axis=-1)
        dq = l2norm(heads(cq, DN_HEADS)) * DN_HEAD_DIM ** -0.5
        dk = l2norm(heads(ck, DN_HEADS))
        beta = jax.nn.sigmoid(d_b.astype(jnp.float32))
        g = -jnp.exp(a_log[l].astype(jnp.float32)) * jax.nn.softplus((d_a + dt_bias[l]).astype(jnp.float32))
        dn = gated_delta_rule(dq, dk, heads(cv, DN_HEADS), g, beta)
        dn = rmsnorm(dn, dn_norm_w[l]).reshape(B, T, DN_WIDTH) * jax.nn.silu(d_z.astype(jnp.float32))

        mix = jnp.concatenate([ret, dn], axis=-1).astype(x.dtype) @ w_out[l]
        x = x + gate1[:, None, :] * mix

        h2 = modulate(rmsnorm(x, norm2_w[l]), shift2, scale2)
        ffn = hierarchical_moe(h2, w_group[l], b_group[l], w_expert[l], b_expert[l], w1[l], w3[l], w2[l])
        x = x + gate2[:, None, :] * ffn.astype(x.dtype)
    return rmsnorm(x, final_norm_w)


def setup_inputs(seed=0):
    out = dict(first_inputs(seed))
    for name, value in second_inputs(seed + 1).items():
        if name != "x":
            out[name + "_2"] = value
    return out


def reference(
    x, p, attn_w_in, attn_b_f, attn_w_out, ssm_w_in, ssm_conv_w, ssm_conv_b, ssm_dt_bias,
    ssm_A_log, ssm_D, ssm_norm_w, ssm_w_out, ln_mix_g, ln_mix_b, ffn_w_up, ffn_conv_w,
    ffn_conv_b, ffn_w_down, ln_ffn_g, ln_ffn_b, ple_w_proj, ple_w_gate, ple_b_gate, c_2,
    positions_2, w_ada_2, b_ada_2, norm1_w_2, w_in_2, conv_w_2, a_log_2, dt_bias_2, dn_norm_w_2,
    w_out_2, norm2_w_2, w_group_2, b_group_2, w_expert_2, b_expert_2, w1_2, w3_2, w2_2,
    final_norm_w_2,
):
    x = first_block(
        x, p, attn_w_in, attn_b_f, attn_w_out, ssm_w_in, ssm_conv_w, ssm_conv_b, ssm_dt_bias,
        ssm_A_log, ssm_D, ssm_norm_w, ssm_w_out, ln_mix_g, ln_mix_b, ffn_w_up, ffn_conv_w,
        ffn_conv_b, ffn_w_down, ln_ffn_g, ln_ffn_b, ple_w_proj, ple_w_gate, ple_b_gate,
    )
    return second_block(
        x, c_2, positions_2, w_ada_2, b_ada_2, norm1_w_2, w_in_2, conv_w_2, a_log_2, dt_bias_2,
        dn_norm_w_2, w_out_2, norm2_w_2, w_group_2, b_group_2, w_expert_2, b_expert_2, w1_2,
        w3_2, w2_2, final_norm_w_2,
    )


_drawn_inputs = setup_inputs


def setup_inputs(seed=0):
    import zlib

    import numpy as np

    out = dict(_drawn_inputs(seed))
    spreads = {}
    factors = {'ffn_conv_b': 3.982,
     'ple_b_gate': 8.0,
     'norm1_w_2': 3.395,
     'dn_norm_w_2': 6.807,
     'norm2_w_2': 2.821,
     'b_group_2': 8.701,
     'b_expert_2': 8.0,
     'final_norm_w_2': 26.423}
    for name, (base, spread) in spreads.items():
        noise = np.random.default_rng([zlib.crc32(name.encode()), seed]).standard_normal(out[name].shape)
        drawn = base * np.exp(spread * noise) if base else spread * noise
        out[name] = __import__('jax').numpy.asarray(drawn.astype(out[name].dtype))
    for name, factor in factors.items():
        out[name] = (out[name] * factor).astype(out[name].dtype)
    return out
```

```python
from contextlib import ExitStack

import numpy as np

import concourse.bass as bass
from concourse import mybir

F32 = mybir.dt.float32
BF16 = mybir.dt.bfloat16
I32 = mybir.dt.int32
U32 = mybir.dt.uint32
ALU = mybir.AluOpType
ACT = mybir.ActivationFunctionType
AX_X = mybir.AxisListType.X
ds = bass.ds

P = 128
T = 1024
D = 1024
TT = T // P
DT = D // P
HALF = 512
NH = D // HALF

HEADS = 16
HD = 64
PAIRS = HEADS // 2
ALPHA = 2.0 ** 0.25
LN_EPS = 1e-5
FFN = 2816
FT = FFN // P
PLE = 256

EPS = 1e-6
MH = 4
MHD = 128
MW = MH * MHD
QKV = 3 * MW // P
N_MOD = 6
GROUPS = 4
PER_GROUP = 8
EXPERTS = GROUPS * PER_GROUP
TOP = 2
DE = 512
LEVELS = 7
BLOCKS = (TOP * T - EXPERTS) // P + EXPERTS
BLOCKS += BLOCKS % 2
SLOTS = BLOCKS * P
ROPE_THETA = 10000.0
TWO_PI = 2.0 * np.pi
PI2_A = 6.28125
PI2_B = float(np.float32(np.round((TWO_PI - PI2_A) * 2.0 ** 21) / 2.0 ** 21))
PI2_C = TWO_PI - PI2_A - PI2_B
ROUND = 1.5 * 2.0 ** 23
MASKED = -(2.0 ** 100)


def group(pe, out, operands):
    last = len(operands) - 1
    for n, (stationary, moving) in enumerate(operands):
        ins = pe.matmul(out, stationary, moving, start=(n == 0), stop=(n == last))
    return ins


def bcast(row, shape):
    return row.to_broadcast(shape)




def stage_values(nc, d, m):
    with ExitStack() as ctx:
        def sb(name, shape, dt=F32):
            return ctx.enter_context(nc.sbuf_tensor(name, shape, dt))

        def sem(name):
            return nc.alloc_semaphore(name)

        wv = sb("wv", [P, NH, DT, HALF])
        wf = sb("wf", [P, DT, HEADS])
        bf = sb("bf", [P, HEADS])
        fg = sb("fg", [P, TT, HEADS])
        fabs = sb("fabs", [P, TT, HEADS])
        fmin = sb("fmin", [P, TT, HEADS])
        lf = sb("lf", [P, TT, HEADS])
        within = sb("within", [P, TT, HEADS])
        carry = sb("carry", [P, TT, HEADS])
        neg = sb("neg", [HEADS, T])
        rest = sb("rest", [HEADS, 2, T])
        parts = sb("parts", [HEADS, 3, T], BF16)
        slice_loaded = [sem(f"v_loaded{k}") for k in range(DT)]
        second_loaded, f_loaded = sem("v_second_loaded"), sem("f_loaded")
        v_bank, v_out, f_bank, f_step = sem("v_bank"), sem("v_out"), sem("f_bank"), sem("f_step")
        f_exp, sums_bank, turned, negated, parted = (sem("f_exp"), sem("f_sums"), sem("f_turned"),
                                                     sem("f_negated"), sem("f_parted"))
        spread = sem("f_spread")
        ps = m.ps
        block = ctx.enter_context(nc.Block())

        @block.sync
        def _(sp):
            for k in range(DT):
                sp.dma_start(m.xT[:, k, :], d["xT"][:, k, :]).then_inc(slice_loaded[k], 16)
                sp.dma_start(wv[:, 0, k, :], d["attn_w"][4][:, k, :]).then_inc(slice_loaded[k], 16)
            sp.dma_start(wf[:], d["attn_wf"]).then_inc(f_loaded, 16)
            sp.dma_start(bf[:], d["attn_bf"].partition_broadcast(P)).then_inc(f_loaded, 16)
            sp.dma_start(wv[:, 1], d["attn_w"][5]).then_inc(second_loaded, 16)
            sp.wait_ge(parted, 5)
            for j in range(3):
                sp.dma_start(m.negc[j:j + 1, :, :], parts[:, j, :]).then_inc(spread, 16)
            sp.wait_ge(spread, 48)

        @block.gpsimd
        def _(pool):
            pool.dma_start(m.consts[:], d["consts"]).then_inc(m.consts_loaded, 16)

        @block.tensor
        def _(pe):
            for n in range(NH):
                for t in range(TT):
                    if n:
                        pe.wait_ge(v_out, TT * (n - 1) + t + 1)
                    for k in range(DT):
                        if t == 0 and n == 0:
                            pe.wait_ge(slice_loaded[k], 32)
                        if t == 0 and n == 1 and k == 0:
                            pe.wait_ge(second_loaded, 16)
                        ins = pe.matmul(ps[:, t, :], m.xT[:, k, t * P:(t + 1) * P], wv[:, n, k, :],
                                        start=(k == 0), stop=(k == DT - 1))
                    ins.then_inc(v_bank, 1)
            pe.wait_ge(f_loaded, 32)
            pe.wait_ge(v_out, TT * (NH - 1) + 1)
            for t in range(TT):
                ins = group(pe, ps[:, 0, t * HEADS:(t + 1) * HEADS],
                            [(m.xT[:, k, t * P:(t + 1) * P], wf[:, k, :]) for k in range(DT)])
            ins.then_inc(f_bank, 1)
            pe.wait_ge(f_step, 4)
            pe.wait_ge(v_out, TT * (NH - 1) + 3)
            pe.wait_ge(m.consts_loaded, 16)
            flat = lf[:].rearrange("p t h -> p (t h)")
            pe.matmul(ps[:, 1, 0:P], m.upto[:], flat, start=True, stop=True)
            pe.matmul(ps[:, 2, 0:P], m.ones[:], flat, start=True, stop=True).then_inc(sums_bank, 1)
            pe.wait_ge(f_step, 5 + TT)
            pe.wait_ge(v_out, TT * NH)
            for t in range(TT):
                ins = pe.transpose(ps[0:HEADS, 4 + t // 4, (t % 4) * P:(t % 4 + 1) * P],
                                   within[:, t, :], m.ident[:])
            ins.then_inc(turned, 1)

        @block.vector
        def _(dve):
            for n in range(NH):
                for t in range(0, TT, 1):
                    dve.wait_ge(v_bank, TT * n + t + 1)
                    dve.tensor_copy(m.v[:, t, n * HALF:(n + 1) * HALF], ps[:, t, :]).then_inc(v_out, 1)
            dve.wait_ge(f_bank, 1)
            dve.wait_ge(f_loaded, 32)
            z = ps[:, 0, 0:TT * HEADS].rearrange("p (t h) -> p t h", t=TT)
            dve.tensor_tensor(fg[:], z, bf[:].unsqueeze(1).to_broadcast([P, TT, HEADS]),
                              ALU.add).then_inc(f_step, 1)
            dve.wait_ge(f_step, 1)
            dve.tensor_scalar(fmin[:], fg[:], 0.0, None, ALU.min).then_inc(f_step, 1)
            dve.wait_ge(f_step, 2)
            dve.scalar_tensor_tensor(fabs[:], fg[:], 0.0, fmin[:], ALU.max, ALU.subtract).then_inc(f_step, 1)
            dve.wait_ge(f_exp, 2)
            dve.tensor_tensor(lf[:], fmin[:], fabs[:], ALU.subtract).then_inc(f_step, 1)
            dve.wait_ge(sums_bank, 1)
            total = ps[:, 2, 0:P].rearrange("p (t h) -> p t h", t=TT)
            dve.memset(carry[:, 0, :], 0.0).then_inc(f_step, 1)
            for t in range(1, TT):
                dve.wait_ge(f_step, 4 + t)
                dve.tensor_tensor(carry[:, t, :], carry[:, t - 1, :], total[:, t - 1, :],
                                  ALU.add).then_inc(f_step, 1)
            dve.wait_ge(f_step, 4 + TT)
            dve.tensor_tensor(within[:], ps[:, 1, 0:P].rearrange("p (t h) -> p t h", t=TT), carry[:],
                              ALU.add).then_inc(f_step, 1)
            dve.wait_ge(turned, 1)
            turned_c = ps[0:HEADS, 4:6, :].rearrange("p b n -> p (b n)")
            dve.tensor_scalar(neg[:], turned_c, -1.0, None, ALU.mult).then_inc(negated, 1)
            dve.wait_ge(negated, 1)
            dve.tensor_copy(parts[:, 0, :], neg[:]).then_inc(parted, 1)
            dve.wait_ge(parted, 1)
            dve.tensor_tensor(rest[:, 0], neg[:], parts[:, 0, :], ALU.subtract).then_inc(parted, 1)
            dve.wait_ge(parted, 2)
            dve.tensor_copy(parts[:, 1, :], rest[:, 0]).then_inc(parted, 1)
            dve.wait_ge(parted, 3)
            dve.tensor_tensor(rest[:, 1], rest[:, 0], parts[:, 1, :], ALU.subtract).then_inc(parted, 1)
            dve.wait_ge(parted, 4)
            dve.tensor_copy(parts[:, 2, :], rest[:, 1]).then_inc(parted, 1)
            dve.wait_ge(m.consts_loaded, 16)
            dve.tensor_copy(m.ident16[:], m.ident[:])
            dve.tensor_copy(m.ahead16[:], m.ahead[:])
            dve.memset(m.ones16[:], 1.0)

        @block.scalar
        def _(act):
            act.wait_ge(f_step, 3)
            act.activation(fabs[:], fabs[:], ACT.Exp, scale=-1.0).then_inc(f_exp, 1)
            act.wait_ge(f_exp, 1)
            act.activation(fabs[:], fabs[:], ACT.Ln, bias=1.0).then_inc(f_exp, 1)


def stage_attention(nc, d, m):
    with ExitStack() as ctx:
        def sb(name, shape, dt=F32):
            return ctx.enter_context(nc.sbuf_tensor(name, shape, dt))

        def sem(name):
            return nc.alloc_semaphore(name)

        wqk = sb("wqk", [P, 2, DT, 2 * P])
        qk = sb("qk", [P, 2, 2, T])
        vp = sb("vp", [P, 2, TT, P])
        probs = sb("probs", [P, 2, T])
        probsT = sb("probsT", [P, 2, TT, P])
        top = sb("top", [P, 4])
        total = sb("total", [P, 4])
        inv = sb("inv", [P, 4])
        w_loaded = [sem("qk_loaded0"), sem("qk_loaded1")]
        proj_bank, proj_out = sem("qk_bank"), sem("qk_out")
        vp_ready = [sem("vp_ready0"), sem("vp_ready1")]
        weighed = [sem("weighed0"), sem("weighed1")]
        scored, maxed, exped = sem("scored"), sem("maxed"), sem("exped")
        turned, turned_out, inverted, o_out = (sem("p_turned"), sem("p_turned_out"), sem("inverted"),
                                               sem("o_out"))
        ps = m.ps
        UNITS = 2 * TT
        block = ctx.enter_context(nc.Block())

        def scores_at(u):
            b = 2 * (u % 2)
            return ps[:, b:b + 2, :].rearrange("p b n -> p (b n)")

        @block.sync
        def _(sp):
            with sp.Fori(0, PAIRS // 2) as i:
                for s in range(2):
                    sp.wait_ge(weighed[s], UNITS * i)
                    sp.dma_start(wqk[:, s], d["attn_wqk"][2 * i + s]).then_inc(w_loaded[s], 16)

        @block.gpsimd
        def _(pool):
            with pool.Fori(0, PAIRS // 2) as i:
                for s in range(2):
                    pool.wait_ge(weighed[s], UNITS * i)
                    pool.tensor_copy(vp[:, s], m.v[:, :, ds((2 * i + s) * P, P)]).then_inc(vp_ready[s], 1)

        @block.tensor
        def _(pe):
            with pe.Fori(0, PAIRS // 2) as i:
                for s in range(2):
                    base = UNITS * (2 * i + s)
                    pe.wait_ge(w_loaded[s], 16 * (i + 1))
                    pe.wait_ge(exped, base)
                    for j in range(2):
                        for h in range(2):
                            group(pe, ps[:, 2 * j + h, :],
                                  [(wqk[:, s, k, j * P:(j + 1) * P], m.xT[:, k, h * HALF:(h + 1) * HALF])
                                   for k in range(DT)]).then_inc(proj_bank, 1)
                    pe.wait_ge(proj_out, 4 * (2 * i + s) + 4)
                    pe.wait_ge(vp_ready[s], i + 1)

                    def scores(u):
                        head, t = u // TT, u % TT
                        lo = head * HD
                        if u >= 2:
                            pe.wait_ge(exped, base + u - 1)
                        q = qk[lo:lo + HD, s, 0, t * P:(t + 1) * P]
                        width = (t + 1) * P
                        for b in range((width + HALF - 1) // HALF):
                            w = min(HALF, width - b * HALF)
                            out = scores_at(u)[:, b * HALF:b * HALF + w]
                            diagonal = b == t // 4
                            pe.matmul(out, q, qk[lo:lo + HD, s, 1, b * HALF:b * HALF + w],
                                      start=True, stop=False)
                            ins = pe.matmul(out, m.ones16[0:3, :],
                                            m.negc[0:3, 4 * i + 2 * s + head, b * HALF:b * HALF + w],
                                            start=False, stop=not diagonal)
                            if diagonal:
                                ins = pe.matmul(scores_at(u)[:, t * P:(t + 1) * P], m.ident16[:],
                                                m.ahead16[:], start=False, stop=True)
                        ins.then_inc(scored, 1)

                    def turn(u):
                        t = u % TT
                        pe.wait_ge(exped, base + u + 1)
                        pe.wait_ge(turned_out, base + u)
                        for k in range(t + 1):
                            ins = pe.transpose(ps[:, 4 + k // 4, (k % 4) * P:(k % 4 + 1) * P],
                                               probs[:, u % 2, k * P:(k + 1) * P], m.ident[:])
                        ins.then_inc(turned, 1)

                    def weigh(u):
                        head, t = u // TT, u % TT
                        pe.wait_ge(turned_out, base + u + 1)
                        pe.wait_ge(o_out, base + max(u - 1, 0))
                        group(pe, ps[:, 6 + u % 2, 0:HD],
                              [(probsT[:, u % 2, k, :], vp[:, s, k, head * HD:(head + 1) * HD])
                               for k in range(t + 1)]).then_inc(weighed[s], 1)

                    scores(0)
                    for u in range(UNITS):
                        if u + 1 < UNITS:
                            scores(u + 1)
                        if u:
                            weigh(u - 1)
                        turn(u)
                    weigh(UNITS - 1)

        @block.vector
        def _(dve):
            with dve.Fori(0, PAIRS // 2) as i:
                for s in range(2):
                    base = UNITS * (2 * i + s)

                    def row_max(u):
                        dve.wait_ge(scored, base + u + 1)
                        dve.tensor_reduce(top[:, u % 4:u % 4 + 1], scores_at(u)[:, 0:(u % TT + 1) * P],
                                          AX_X, ALU.max, negate=True).then_inc(maxed, 1)

                    def out(u):
                        dve.wait_ge(weighed[s], UNITS * i + u + 1)
                        dve.wait_ge(inverted, base + u + 1)
                        head, t = u // TT, u % TT
                        col = (4 * i + 2 * s + head) * HD
                        dve.tensor_scalar(m.o[:, t, ds(col, HD)], ps[:, 6 + u % 2, 0:HD],
                                          inv[:, u % 4:u % 4 + 1], None, ALU.mult).then_inc(o_out, 1)

                    def turned_copy(u):
                        t = u % TT
                        dve.wait_ge(turned, base + u + 1)
                        dve.reciprocal(inv[:, u % 4:u % 4 + 1], total[:, u % 4:u % 4 + 1]).then_inc(inverted, 1)
                        dve.wait_ge(weighed[s], UNITS * i + max(u - 1, 0))
                        both = ps[:, 4:6, :].rearrange("p b n -> p (b n)")
                        dve.tensor_copy(probsT[:, u % 2, 0:t + 1, :].rearrange("p k n -> p (k n)"),
                                        both[:, 0:(t + 1) * P]).then_inc(turned_out, 1)

                    row_max(0)
                    for u in range(UNITS):
                        if u + 1 < UNITS:
                            row_max(u + 1)
                        if u:
                            out(u - 1)
                        turned_copy(u)
                    out(UNITS - 1)

        @block.scalar
        def _(act):
            with act.Fori(0, PAIRS // 2) as i:
                for s in range(2):
                    base = UNITS * (2 * i + s)
                    for n in range(4):
                        act.wait_ge(proj_bank, 4 * (2 * i + s) + n + 1)
                        j, h = n // 2, n % 2
                        act.activation(qk[:, s, j, h * HALF:(h + 1) * HALF], ps[:, n, :], ACT.Copy,
                                       scale=(HD ** -0.5 if j == 0 else 1.0)).then_inc(proj_out, 1)
                    for u in range(UNITS):
                        act.wait_ge(maxed, base + u + 1)
                        act.wait_ge(turned, base + max(u - 1, 0))
                        act.activation(probs[:, u % 2, 0:(u % TT + 1) * P],
                                       scores_at(u)[:, 0:(u % TT + 1) * P], ACT.Exp,
                                       bias=top[:, u % 4:u % 4 + 1],
                                       accum_out=total[:, u % 4:u % 4 + 1]).then_inc(exped, 1)




def turn_tile(pe, ps, bank, rows, ident):
    for k in range(DT):
        ins = pe.transpose(ps[:, bank + k // 4, (k % 4) * P:(k % 4 + 1) * P], rows[:, k * P:(k + 1) * P],
                           ident)
    return ins


def two_banks(ps, bank):
    return ps[:, bank:bank + 2, :].rearrange("p b (k n) -> p (b k) n", n=P)


class Norm:

    def __init__(self, sb, sem, name):
        self.stats = sb(name + "_stats", [P, TT, 2, 6])
        self.mean = sb(name + "_mean", [P, TT, 2])
        self.std = sb(name + "_std", [P, TT, 2])
        self.g = sb(name + "_g", [P, D])
        self.b = sb(name + "_b", [P, D])
        self.stats_done, self.mean_done = sem(name + "_stats_done"), sem(name + "_mean_done")
        self.var_done, self.rooted = sem(name + "_var_done"), sem(name + "_rooted")
        self.inverted, self.normed = sem(name + "_inverted"), sem(name + "_normed")
        self.scaled, self.shifted = sem(name + "_scaled"), sem(name + "_shifted")

    def on_vector(self, dve, row, t):
        for n in range(NH):
            dve.bn_stats(self.stats[:, t, n, :], row[:, n * HALF:(n + 1) * HALF]).then_inc(self.stats_done, 1)
        dve.wait_ge(self.stats_done, 2 * t + 2)
        dve.bn_aggr(self.mean[:, t, :], self.stats[:, t].rearrange("p n s -> p (n s)")
                    ).then_inc(self.mean_done, 1)
        dve.wait_ge(self.mean_done, t + 1)
        dve.tensor_scalar(self.std[:, t, 0:1], self.mean[:, t, 1:2], LN_EPS, None, ALU.add
                          ).then_inc(self.var_done, 1)
        dve.wait_ge(self.rooted, t + 1)
        dve.reciprocal(self.std[:, t, 1:2], self.std[:, t, 0:1]).then_inc(self.inverted, 1)
        dve.wait_ge(self.inverted, t + 1)
        dve.tensor_scalar(row, row, self.mean[:, t, 0:1], self.std[:, t, 1:2], ALU.subtract, ALU.mult
                          ).then_inc(self.normed, 1)

    def on_scalar(self, act, t):
        act.wait_ge(self.var_done, t + 1)
        act.activation(self.std[:, t, 0:1], self.std[:, t, 0:1], ACT.Sqrt).then_inc(self.rooted, 1)

    def on_pool(self, pool, row, t):
        pool.wait_ge(self.normed, t + 1)
        pool.tensor_tensor(row, row, self.g[:], ALU.mult).then_inc(self.scaled, 1)
        pool.wait_ge(self.scaled, t + 1)
        pool.tensor_tensor(row, row, self.b[:], ALU.add).then_inc(self.shifted, 1)


def stage_attention_out(nc, d, m):
    with ExitStack() as ctx:
        def sb(name, shape, dt=F32):
            return ctx.enter_context(nc.sbuf_tensor(name, shape, dt))

        def sem(name):
            return nc.alloc_semaphore(name)

        oT = sb("oT", [P, DT, T])
        w = sb("w_attn_out", [P, NH, DT, HALF])
        norm = Norm(sb, sem, "ln1")
        loaded, x_loaded = sem("ao_loaded"), sem("ao_x_loaded")
        turned, turned_out = sem("o_turned"), sem("oT_out")
        mixed, added = sem("ao_mixed"), sem("ao_added")
        x_turned, x_turned_out = sem("ao_x_turned"), sem("ao_x_turned_out")
        ps = m.ps
        block = ctx.enter_context(nc.Block())

        @block.sync
        def _(sp):
            for n in range(NH):
                sp.dma_start(w[:, n], d["attn_w_out"][n]).then_inc(loaded, 16)
            sp.dma_start(m.res[:], d["x"]).then_inc(x_loaded, 16)
            sp.dma_start(norm.g[:], d["ln_mix_g"].partition_broadcast(P)).then_inc(x_loaded, 16)
            sp.dma_start(norm.b[:], d["ln_mix_b"].partition_broadcast(P)).then_inc(x_loaded, 16)

        @block.tensor
        def _(pe):
            for t in range(TT):
                if t >= 2:
                    pe.wait_ge(turned_out, t - 1)
                turn_tile(pe, ps, 2 * (t % 2), m.o[:, t, :], m.ident[:]).then_inc(turned, 1)
            pe.wait_ge(loaded, 16 * NH)
            pe.wait_ge(turned_out, TT)
            for t in range(TT + 2):
                if t < TT:
                    if t >= 2:
                        pe.wait_ge(added, 2 * (t - 1))
                    for n in range(NH):
                        group(pe, ps[:, 2 * (t % 2) + n, :],
                              [(oT[:, k, t * P:(t + 1) * P], w[:, n, k, :]) for k in range(DT)]
                              ).then_inc(mixed, 1)
                if t >= 2:
                    pe.wait_ge(norm.shifted, t - 1)
                    if t >= 4:
                        pe.wait_ge(x_turned_out, t - 3)
                    turn_tile(pe, ps, 4 + 2 * (t % 2), m.res[:, t - 2, :], m.ident[:]).then_inc(x_turned, 1)

        @block.vector
        def _(dve):
            for t in range(TT):
                dve.wait_ge(turned, t + 1)
                dve.tensor_copy(oT[:, :, t * P:(t + 1) * P], two_banks(ps, 2 * (t % 2))).then_inc(turned_out, 1)
            dve.wait_ge(x_loaded, 48)
            for t in range(TT):
                for n in range(NH):
                    half = m.res[:, t, n * HALF:(n + 1) * HALF]
                    dve.wait_ge(mixed, 2 * t + n + 1)
                    dve.scalar_tensor_tensor(half, half, ALPHA, ps[:, 2 * (t % 2) + n, :], ALU.mult,
                                             ALU.add).then_inc(added, 1)
                dve.wait_ge(added, 2 * t + 2)
                norm.on_vector(dve, m.res[:, t, :], t)

        @block.scalar
        def _(act):
            for t in range(TT + 2):
                if t < TT:
                    norm.on_scalar(act, t)
                if t >= 2:
                    act.wait_ge(x_turned, t - 1)
                    act.activation(m.xT[:, :, (t - 2) * P:(t - 1) * P], two_banks(ps, 4 + 2 * (t % 2)),
                                   ACT.Copy).then_inc(x_turned_out, 1)

        @block.gpsimd
        def _(pool):
            pool.wait_ge(x_loaded, 48)
            for t in range(TT):
                norm.on_pool(pool, m.res[:, t, :], t)




def stage_ffn_up(nc, d, m):
    with ExitStack() as ctx:
        def sb(name, shape, dt=F32):
            return ctx.enter_context(nc.sbuf_tensor(name, shape, dt))

        def sem(name):
            return nc.alloc_semaphore(name)

        TAPS = 3
        w = sb("w_up", [P, 2, DT, 2 * P])
        taps = sb("ffn_taps", [P, FT, TAPS])
        bias = sb("ffn_bias", [P, FT])
        conv = sb("ffn_conv", [P, 2, T])
        gate = sb("ffn_gate", [P, 2, T])
        taps_loaded = sem("taps_loaded")
        loaded = [sem("up_loaded0"), sem("up_loaded1")]
        summed = [sem("up_summed0"), sem("up_summed1")]
        tap2, tap1, tap0, gelued = sem("up_tap2"), sem("up_tap1"), sem("up_tap0"), sem("up_gelued")
        gated = [sem("up_gated0"), sem("up_gated1")]
        ps = m.ps
        block = ctx.enter_context(nc.Block())

        def u_of(s):
            return ps[:, 4 * s:4 * s + 2, :].rearrange("p b n -> p (b n)")

        def g_of(s):
            return ps[:, 4 * s + 2:4 * s + 4, :].rearrange("p b n -> p (b n)")

        @block.sync
        def _(sp):
            sp.dma_start(taps[:], d["ffn_taps"]).then_inc(taps_loaded, 16)
            sp.dma_start(bias[:], d["ffn_bias"]).then_inc(taps_loaded, 16)
            with sp.Fori(0, FT // 2) as i:
                for s in range(2):
                    sp.wait_ge(summed[s], 2 * i)
                    sp.dma_start(w[:, s], d["ffn_w_up"][2 * i + s]).then_inc(loaded[s], 16)

        @block.tensor
        def _(pe):
            with pe.Fori(0, FT // 2) as i:
                for s in range(2):
                    pe.wait_ge(loaded[s], 16 * (i + 1))
                    pe.wait_ge(gated[s], i)
                    for j in range(2):
                        for h in range(2):
                            ins = group(pe, ps[:, 4 * s + 2 * (1 - j) + h, :],
                                        [(w[:, s, k, (1 - j) * P:(2 - j) * P],
                                          m.xT[:, k, h * HALF:(h + 1) * HALF]) for k in range(DT)])
                        ins.then_inc(summed[s], 1)

        @block.scalar
        def _(act):
            act.wait_ge(taps_loaded, 32)
            with act.Fori(0, FT // 2) as i:
                for s in range(2):
                    c = 2 * i + s
                    act.wait_ge(summed[s], 2 * i + 1)
                    act.wait_ge(gelued, c)
                    act.activation(conv[:, s, :], g_of(s), ACT.Identity, bias=bias[:, ds(c, 1)],
                                   scale=taps[:, ds(c, 1), TAPS - 1]).then_inc(tap2, 1)
                    act.wait_ge(tap0, c + 1)
                    act.wait_ge(gated[s], i)
                    act.activation(gate[:, s, :], conv[:, s, :], ACT.Gelu).then_inc(gelued, 1)

        @block.vector
        def _(dve):
            dve.wait_ge(taps_loaded, 32)
            with dve.Fori(0, FT // 2) as i:
                for s in range(2):
                    c = 2 * i + s
                    dve.wait_ge(tap2, c + 1)
                    dve.scalar_tensor_tensor(conv[:, s, 1:T], g_of(s)[:, 0:T - 1], taps[:, ds(c, 1), 1],
                                             conv[:, s, 1:T], ALU.mult, ALU.add).then_inc(tap1, 1)
                    dve.wait_ge(tap1, c + 1)
                    dve.scalar_tensor_tensor(conv[:, s, 2:T], g_of(s)[:, 0:T - 2], taps[:, ds(c, 1), 0],
                                             conv[:, s, 2:T], ALU.mult, ALU.add).then_inc(tap0, 1)
                    dve.wait_ge(gelued, c + 1)
                    dve.wait_ge(summed[s], 2 * i + 2)
                    dve.tensor_tensor(m.hT[:, ds(c, 1), :].rearrange("p c t -> p (c t)"), gate[:, s, :], u_of(s),
                                      ALU.mult).then_inc(gated[s], 1)


def stage_ffn_down(nc, d, m):
    with ExitStack() as ctx:
        def sb(name, shape, dt=F32):
            return ctx.enter_context(nc.sbuf_tensor(name, shape, dt))

        def sem(name):
            return nc.alloc_semaphore(name)

        w = sb("w_down", [P, 2, FT, P])
        y = sb("down_y", [P, 2, T])
        norm = Norm(sb, sem, "ln2")
        loaded = [sem("down_loaded0"), sem("down_loaded1")]
        summed = [sem("down_summed0"), sem("down_summed1")]
        g_loaded = sem("ln2_loaded")
        y_out, turned, added = sem("down_y_out"), sem("down_turned"), sem("down_added")
        x_turned, x_turned_out = sem("x2_turned"), sem("x2_turned_out")
        ps = m.ps
        block = ctx.enter_context(nc.Block())

        @block.sync
        def _(sp):
            sp.dma_start(norm.g[:], d["ln_ffn_g"].partition_broadcast(P)).then_inc(g_loaded, 16)
            sp.dma_start(norm.b[:], d["ln_ffn_b"].partition_broadcast(P)).then_inc(g_loaded, 16)
            with sp.Fori(0, DT // 2) as i:
                for s in range(2):
                    sp.wait_ge(summed[s], 2 * i)
                    sp.dma_start(w[:, s], d["ffn_w_down"][2 * i + s]).then_inc(loaded[s], 16)

        @block.tensor
        def _(pe):
            with pe.Fori(0, DT // 2) as i:
                for s in range(2):
                    c = 2 * i + s
                    pe.wait_ge(loaded[s], 16 * (i + 1))
                    pe.wait_ge(y_out, 2 * c)
                    for h in range(2):
                        ins = group(pe, ps[:, 2 * s + h, :],
                                    [(w[:, s, k, :], m.hT[:, k, h * HALF:(h + 1) * HALF]) for k in range(FT)])
                        ins.then_inc(summed[s], 1)
                    pe.wait_ge(added, 2 * c)
                    for h in range(2):
                        pe.wait_ge(y_out, 2 * c + h + 1)
                        for t in range(4 * h, 4 * h + 4):
                            ins = pe.transpose(ps[:, 4 + h, (t % 4) * P:(t % 4 + 1) * P],
                                               y[:, s, t * P:(t + 1) * P], m.ident[:])
                        ins.then_inc(turned, 1)
            for t in range(TT):
                pe.wait_ge(norm.shifted, t + 1)
                if t >= 2:
                    pe.wait_ge(x_turned_out, t - 1)
                turn_tile(pe, ps, 2 * (t % 2), m.res[:, t, :], m.ident[:]).then_inc(x_turned, 1)

        @block.scalar
        def _(act):
            with act.Fori(0, DT // 2) as i:
                for s in range(2):
                    for h in range(2):
                        c = 2 * i + s
                        act.wait_ge(summed[s], 2 * i + h + 1)
                        act.wait_ge(turned, 2 * c)
                        act.activation(y[:, s, h * HALF:(h + 1) * HALF], ps[:, 2 * s + h, :], ACT.Copy
                                       ).then_inc(y_out, 1)
            for t in range(TT):
                norm.on_scalar(act, t)
            for t in range(TT):
                act.wait_ge(x_turned, t + 1)
                act.activation(m.xT[:, :, t * P:(t + 1) * P], two_banks(ps, 2 * (t % 2)),
                               ACT.Copy).then_inc(x_turned_out, 1)

        @block.vector
        def _(dve):
            with dve.Fori(0, DT // 2) as i:
                for s in range(2):
                    for h in range(2):
                        c = 2 * i + s
                        dve.wait_ge(turned, 2 * c + h + 1)
                        part = m.res[:, 4 * h:4 * h + 4, ds(c * P, P)]
                        dve.scalar_tensor_tensor(part, part, ALPHA,
                                                 ps[:, 4 + h, :].rearrange("p (t n) -> p t n", n=P),
                                                 ALU.mult, ALU.add).then_inc(added, 1)
            dve.wait_ge(added, 2 * DT)
            for t in range(TT):
                norm.on_vector(dve, m.res[:, t, :], t)

        @block.gpsimd
        def _(pool):
            pool.wait_ge(g_loaded, 32)
            for t in range(TT):
                norm.on_pool(pool, m.res[:, t, :], t)


def stage_per_layer_input(nc, d, m):
    with ExitStack() as ctx:
        def sb(name, shape, dt=F32):
            return ctx.enter_context(nc.sbuf_tensor(name, shape, dt))

        def sem(name):
            return nc.alloc_semaphore(name)

        w = sb("w_ple_gate", [P, NH, DT, HALF])
        wp = sb("w_ple", [P, PLE // P, D])
        pT = sb("pT", [P, PLE // P, T])
        bg = sb("ple_b", [P, D])
        z = sb("ple_z", [P, 2, HALF])
        c = sb("c", [P, DT])
        wa = sb("w_ada", [P, N_MOD, D])
        loaded, p_loaded, c_loaded = sem("ple_loaded"), sem("ple_p_loaded"), sem("c_loaded")
        a_loaded = [sem(f"ada_loaded{n}") for n in range(N_MOD)]
        ada = [sem(f"ada_step{n}") for n in range(N_MOD)]
        summed, biased, gated, scaled, added = (sem("ple_summed"), sem("ple_biased"), sem("ple_gated"),
                                                sem("ple_scaled"), sem("ple_added"))
        c_silu = sem("c_silu")
        ps = m.ps
        STEPS = DT * N_MOD
        PER_HALF = STEPS // (2 * TT)
        block = ctx.enter_context(nc.Block())

        @block.sync
        def _(sp):
            sp.dma_start(wp[:], d["ple_w_proj"]).then_inc(p_loaded, 16)
            sp.dma_start(pT[:], d["pT"]).then_inc(p_loaded, 16)
            sp.dma_start(c[:], d["c"]).then_inc(c_loaded, 16)
            sp.dma_start(bg[:], d["ple_b_gate"].partition_broadcast(P)).then_inc(p_loaded, 16)
            for n in range(NH):
                sp.dma_start(w[:, n], d["ple_w_gate"][n]).then_inc(loaded, 16)
            with sp.Fori(0, DT) as k:
                for n in range(N_MOD):
                    sp.wait_ge(ada[n], k)
                    sp.dma_start(wa[:, n, :], d["w_ada"][k, n]).then_inc(a_loaded[n], 16)

        @block.tensor
        def _(pe):
            pe.wait_ge(p_loaded, 48)
            pe.wait_ge(loaded, 16 * NH)
            for t in range(TT):
                rows = slice(t * P, (t + 1) * P)
                for n in range(NH):
                    i = NH * t + n
                    b = 2 * (i % 4)
                    cols = slice(n * HALF, (n + 1) * HALF)
                    if i >= 4:
                        pe.wait_ge(scaled, i - 3)
                    group(pe, ps[:, b, :], [(m.xT[:, k, rows], w[:, n, k, :]) for k in range(DT)])
                    group(pe, ps[:, b + 1, :], [(pT[:, k, rows], wp[:, k, cols]) for k in range(PLE // P)]
                          ).then_inc(summed, 1)

        @block.scalar
        def _(act):
            act.wait_ge(c_loaded, 16)
            act.activation(c[:], c[:], ACT.Silu).then_inc(c_silu, 1)
            for i in range(NH * TT):
                act.wait_ge(biased, i + 1)
                act.activation(z[:, i % 2], z[:, i % 2], ACT.Sigmoid).then_inc(gated, 1)

        @block.vector
        def _(dve):
            dve.wait_ge(p_loaded, 48)
            dve.wait_ge(c_silu, 1)

            def ada_product(j):
                k, n = j // N_MOD, j % N_MOD
                acc = m.mod[:, n * D:(n + 1) * D]
                dve.wait_ge(a_loaded[n], 16 * (k + 1))
                if k == 0:
                    dve.tensor_scalar(acc, wa[:, n, :], c[:, 0:1], None, ALU.mult).then_inc(ada[n], 1)
                else:
                    dve.wait_ge(ada[n], k)
                    dve.scalar_tensor_tensor(acc, wa[:, n, :], c[:, k:k + 1], acc, ALU.mult, ALU.add
                                             ).then_inc(ada[n], 1)

            for i in range(NH * TT):
                t, n = i // NH, i % NH
                b = 2 * (i % 4)
                cols = slice(n * HALF, (n + 1) * HALF)
                dve.wait_ge(summed, i + 1)
                if i >= 2:
                    dve.wait_ge(added, i - 1)
                dve.tensor_tensor(z[:, i % 2], ps[:, b, :], bg[:, cols], ALU.add).then_inc(biased, 1)
                for j in range(PER_HALF * i, PER_HALF * (i + 1)):
                    ada_product(j)
                dve.wait_ge(gated, i + 1)
                dve.tensor_tensor(z[:, i % 2], z[:, i % 2], ps[:, b + 1, :], ALU.mult).then_inc(scaled, 1)
                dve.wait_ge(scaled, i + 1)
                dve.tensor_tensor(m.res[:, t, cols], m.res[:, t, cols], z[:, i % 2], ALU.add
                                  ).then_inc(added, 1)




def stage_modulation(nc, d, m):
    with ExitStack() as ctx:
        b = ctx.enter_context(nc.sbuf_tensor("b_ada", [P, N_MOD * D], F32))
        nw = ctx.enter_context(nc.sbuf_tensor("norm_w", [P, 2, D], F32))
        loaded, summed, added = (nc.alloc_semaphore(n)
                                 for n in ("mod_loaded", "mod_summed", "mod_added"))
        CH = N_MOD * D // HALF
        block = ctx.enter_context(nc.Block())

        @block.sync
        def _(sp):
            sp.dma_start(b[:], d["b_ada"].partition_broadcast(P)).then_inc(loaded, 16)
            sp.dma_start(nw[:, 0, :], d["norm1_w"].partition_broadcast(P)).then_inc(loaded, 16)
            sp.dma_start(nw[:, 1, :], d["norm2_w"].partition_broadcast(P)).then_inc(loaded, 16)

        @block.tensor
        def _(pe):
            for j in range(CH):
                if j >= 8:
                    pe.wait_ge(added, j - 7)
                pe.matmul(m.ps[:, j % 8, :], m.ones[:], m.mod[:, j * HALF:(j + 1) * HALF],
                          start=True, stop=True).then_inc(summed, 1)

        @block.vector
        def _(dve):
            dve.wait_ge(loaded, 48)
            for j in range(CH):
                cols = slice(j * HALF, (j + 1) * HALF)
                dve.wait_ge(summed, j + 1)
                dve.tensor_tensor(m.mod[:, cols], m.ps[:, j % 8, :], b[:, cols], ALU.add).then_inc(added, 1)
            dve.wait_ge(added, CH)
            for j in range(2):
                scale = m.mod[:, (3 * j + 1) * D:(3 * j + 2) * D]
                dve.scalar_tensor_tensor(scale, scale, 1.0, nw[:, j, :], ALU.add, ALU.mult)


def stage_modulated_norm(nc, d, m, name, second):
    with ExitStack() as ctx:
        def sb(name, shape, dt=F32):
            return ctx.enter_context(nc.sbuf_tensor(name, shape, dt))

        def sem(name):
            return nc.alloc_semaphore(name)

        square = sb(name + "_square", [P, D])
        ss = sb(name + "_ss", [P, TT])
        inv = sb(name + "_inv", [P, TT])
        h = sb(name + "_h", [P, 2, D])
        squared, meaned, rooted, inverted, scaled, shifted = (
            sem(name + "_" + n) for n in ("squared", "meaned", "rooted", "inverted", "scaled", "shifted"))
        turned, turned_out = sem(name + "_turned"), sem(name + "_turned_out")
        stored = [sem(name + "_stored0"), sem(name + "_stored1")]
        j = 3 if second else 0
        shift, scale = m.mod[:, j * D:(j + 1) * D], m.mod[:, (j + 1) * D:(j + 2) * D]
        block = ctx.enter_context(nc.Block())

        @block.scalar
        def _(act):
            for t in range(TT):
                if t:
                    act.wait_ge(squared, t)
                act.activation(square[:], m.res[:, t, :], ACT.Square, accum_out=ss[:, t:t + 1]
                               ).then_inc(squared, 1)
            act.wait_ge(meaned, 1)
            act.activation(ss[:], ss[:], ACT.Sqrt).then_inc(rooted, 1)
            for t in range(TT):
                act.wait_ge(turned, t + 1)
                act.activation(m.xT[:, :, t * P:(t + 1) * P], two_banks(m.ps, 2 * (t % 2)), ACT.Copy
                               ).then_inc(turned_out, 1)

        @block.vector
        def _(dve):
            dve.wait_ge(squared, TT)
            dve.tensor_scalar(ss[:], ss[:], 1.0 / D, EPS, ALU.mult, ALU.add).then_inc(meaned, 1)
            dve.wait_ge(rooted, 1)
            dve.reciprocal(inv[:], ss[:]).then_inc(inverted, 1)
            dve.wait_ge(inverted, 1)
            for t in range(TT):
                s = t % 2
                if t >= 2:
                    dve.wait_ge(turned, t - 1)
                    if second:
                        dve.wait_ge(stored[s], 16 * (t // 2))
                dve.scalar_tensor_tensor(h[:, s], m.res[:, t, :], inv[:, t:t + 1], scale, ALU.mult, ALU.mult
                                         ).then_inc(scaled, 1)
                dve.wait_ge(scaled, t + 1)
                dve.tensor_tensor(h[:, s], h[:, s], shift, ALU.add).then_inc(shifted, 1)

        @block.tensor
        def _(pe):
            for t in range(TT):
                pe.wait_ge(shifted, t + 1)
                if t >= 2:
                    pe.wait_ge(turned_out, t - 1)
                turn_tile(pe, m.ps, 2 * (t % 2), h[:, t % 2], m.ident[:]).then_inc(turned, 1)

        @block.sync
        def _(sp):
            if second:
                for t in range(TT):
                    sp.wait_ge(shifted, t + 1)
                    sp.dma_start(d["h2_rows"][t * P:(t + 1) * P, :], h[:, t % 2]).then_inc(stored[t % 2], 16)
                for s in range(2):
                    sp.wait_ge(stored[s], 16 * (TT // 2))




ROW_CHUNKS = 5


def stage_project_rows(nc, d, m):
    with ExitStack() as ctx:
        def sb(name, shape, dt=F32):
            return ctx.enter_context(nc.sbuf_tensor(name, shape, dt))

        def sem(name):
            return nc.alloc_semaphore(name)

        w = sb("w_rows", [P, 2, DT, HALF])
        wab = sb("w_ab", [P, DT, 2 * MH])
        loaded = [sem("rows_loaded0"), sem("rows_loaded1")]
        ab_loaded, summed, out, ab_summed = sem("ab_loaded"), sem("rows_summed"), sem("rows_out"), sem("ab_summed")
        ps = m.ps
        block = ctx.enter_context(nc.Block())

        @block.sync
        def _(sp):
            for n in range(ROW_CHUNKS):
                if n >= 2:
                    sp.wait_ge(summed, TT * (n - 1))
                sp.dma_start(w[:, n % 2], d["w_rows"][n]).then_inc(loaded[n % 2], 16)
            sp.dma_start(wab[:], d["w_ab"]).then_inc(ab_loaded, 16)

        @block.tensor
        def _(pe):
            for n in range(ROW_CHUNKS):
                pe.wait_ge(loaded[n % 2], 16 * (n // 2 + 1))
                for t in range(TT):
                    if n:
                        pe.wait_ge(out, TT * (n - 1) + t + 1)
                    group(pe, ps[:, t, :], [(m.xT[:, k, t * P:(t + 1) * P], w[:, n % 2, k, :])
                                            for k in range(DT)]).then_inc(summed, 1)
            pe.wait_ge(ab_loaded, 16)
            pe.wait_ge(out, TT * (ROW_CHUNKS - 1) + 1)
            for t in range(TT):
                ins = group(pe, ps[:, 0, t * 2 * MH:(t + 1) * 2 * MH],
                            [(m.xT[:, k, t * P:(t + 1) * P], wab[:, k, :]) for k in range(DT)])
            ins.then_inc(ab_summed, 1)

        @block.scalar
        def _(act):
            for n in range(ROW_CHUNKS):
                for t in range(TT):
                    act.wait_ge(summed, TT * n + t + 1)
                    if n < 2:
                        act.activation(m.mixed[:, t, n * HALF:(n + 1) * HALF], ps[:, t, :], ACT.Silu
                                       ).then_inc(out, 1)
                    else:
                        act.activation(m.r_qkv[:, n - 2, t, :], ps[:, t, :], ACT.Copy).then_inc(out, 1)
            act.wait_ge(ab_summed, 1)
            act.activation(m.ab[:].rearrange("p t c -> p (t c)"), ps[:, 0, 0:TT * 2 * MH], ACT.Copy)


def stage_project_cols(nc, d, m):
    with ExitStack() as ctx:
        def sb(name, shape, dt=F32):
            return ctx.enter_context(nc.sbuf_tensor(name, shape, dt))

        def sem(name):
            return nc.alloc_semaphore(name)

        TAPS = 4
        w = sb("w_cols", [P, 2, DT, P])
        taps = sb("dn_taps", [P, QKV, TAPS])
        conv = sb("dn_conv", [P, 2, T])
        taps_loaded = sem("dn_taps_loaded")
        loaded = [sem("cols_loaded0"), sem("cols_loaded1")]
        summed = [sem("cols_summed0"), sem("cols_summed1")]
        tap3, silued = [sem("tap3_0"), sem("tap3_1")], [sem("silued0"), sem("silued1")]
        tapped = [sem("tapped0"), sem("tapped1")]
        ps = m.ps
        block = ctx.enter_context(nc.Block())

        def sums(s):
            return ps[:, 2 * s:2 * s + 2, :].rearrange("p b n -> p (b n)")

        @block.sync
        def _(sp):
            sp.dma_start(taps[:], d["dn_taps"]).then_inc(taps_loaded, 16)
            with sp.Fori(0, QKV // 2) as i:
                for s in range(2):
                    sp.wait_ge(summed[s], i)
                    sp.dma_start(w[:, s], d["w_cols"][2 * i + s]).then_inc(loaded[s], 16)

        @block.tensor
        def _(pe):
            with pe.Fori(0, QKV // 2) as i:
                for s in range(2):
                    pe.wait_ge(loaded[s], 16 * (i + 1))
                    pe.wait_ge(tapped[s], 3 * i)
                    for h in range(2):
                        ins = group(pe, ps[:, 2 * s + h, :],
                                    [(w[:, s, k, :], m.xT[:, k, h * HALF:(h + 1) * HALF]) for k in range(DT)])
                    ins.then_inc(summed[s], 1)

        @block.scalar
        def _(act):
            act.wait_ge(taps_loaded, 16)
            with act.Fori(0, QKV // 2) as i:
                for s in range(2):
                    act.wait_ge(summed[s], i + 1)
                    act.wait_ge(silued[s], i)
                    act.activation(conv[:, s, :], sums(s), ACT.Identity,
                                   scale=taps[:, ds(2 * i + s, 1), TAPS - 1]).then_inc(tap3[s], 1)
                    act.wait_ge(tap3[s], i + 1)
                    act.wait_ge(tapped[s], 3 * i + 3)
                    act.activation(m.qkv[:, ds(2 * i + s, 1), :].rearrange("p c t -> p (c t)"), conv[:, s, :],
                                   ACT.Silu).then_inc(silued[s], 1)

        @block.vector
        def _(dve):
            dve.wait_ge(taps_loaded, 16)
            with dve.Fori(0, QKV // 2) as i:
                for s in range(2):
                    dve.wait_ge(tap3[s], i + 1)
                    for back in range(1, TAPS):
                        if back > 1:
                            dve.wait_ge(tapped[s], 3 * i + back - 1)
                        dve.scalar_tensor_tensor(conv[:, s, back:T], sums(s)[:, 0:T - back],
                                                 taps[:, ds(2 * i + s, 1), TAPS - 1 - back],
                                                 conv[:, s, back:T], ALU.mult, ALU.add).then_inc(tapped[s], 1)




def heads_of(ap):
    return ap.rearrange("p (h n) -> p h n", n=MHD)


def stage_rotary_tables(nc, d, m):
    with ExitStack() as ctx:
        def sb(name, shape, dt=F32):
            return ctx.enter_context(nc.sbuf_tensor(name, shape, dt))

        def sem(name):
            return nc.alloc_semaphore(name)

        F = MHD // 2
        pos = sb("pos", [P, TT], I32)
        posf = sb("posf", [P, TT])
        freq = sb("freq", [P, F])
        angle = sb("angle", [P, TT, F])
        turns = sb("turns", [P, 2, TT, F])
        loaded, step, folded = sem("pos_loaded"), sem("angle_step"), sem("angle_folded")
        block = ctx.enter_context(nc.Block())

        @block.sync
        def _(sp):
            sp.dma_start(pos[:], d["positions"]).then_inc(loaded, 16)
            sp.dma_start(freq[:], d["freq"].partition_broadcast(P)).then_inc(loaded, 16)

        @block.vector
        def _(dve):
            dve.wait_ge(loaded, 32)
            dve.tensor_copy(posf[:], pos[:]).then_inc(step, 1)
            dve.wait_ge(step, 1)
            dve.tensor_tensor(angle[:], posf[:].unsqueeze(2).to_broadcast([P, TT, F]),
                              freq[:].unsqueeze(1).to_broadcast([P, TT, F]), ALU.mult).then_inc(step, 1)
            n = 2
            for j, (tab, lead) in enumerate(((m.sin, 0.0), (m.cos, 0.25))):
                k = turns[:, j]
                dve.wait_ge(step, n)
                dve.tensor_scalar(k, angle[:], 1.0 / TWO_PI, lead, ALU.mult, ALU.add).then_inc(step, 1)
                dve.wait_ge(step, n + 1)
                dve.tensor_scalar(k, k, ROUND, ROUND, ALU.add, ALU.subtract).then_inc(step, 1)
                n += 2
                before = angle
                for part in (PI2_A, PI2_B, PI2_C):
                    dve.wait_ge(step, n)
                    dve.scalar_tensor_tensor(tab[:], k, -part, before[:], ALU.mult, ALU.add).then_inc(step, 1)
                    before = tab
                    n += 1
                dve.wait_ge(step, n)
                dve.tensor_scalar(tab[:], tab[:], lead * TWO_PI, float(np.float32(3.1415925)), ALU.add, ALU.min
                                  ).then_inc(step, 1)
                n += 1
                dve.wait_ge(step, n)
                dve.tensor_scalar(tab[:], tab[:], -float(np.float32(3.1415925)), None, ALU.max
                                  ).then_inc(folded, 1)

        @block.scalar
        def _(act):
            act.wait_ge(folded, 1)
            act.activation(m.sin[:], m.sin[:], ACT.Sin)
            act.wait_ge(folded, 2)
            act.activation(m.cos[:], m.cos[:], ACT.Sin)


def stage_retention(nc, d, m):
    with ExitStack() as ctx:
        def sb(name, shape, dt=F32):
            return ctx.enter_context(nc.sbuf_tensor(name, shape, dt))

        def sem(name):
            return nc.alloc_semaphore(name)

        F = MHD // 2
        tables = sb("ret_tables", [P, 3, MW])
        kdecay = sb("ret_kdecay", [P, MH])
        decay, qdecay, sdecay = tables[:, 0], tables[:, 1], tables[:, 2]
        product = sb("rot_product", [P, 2, 2, MW])
        rot = sb("rot", [P, 2, MW])
        kw = sb("ret_kw", [P, MW])
        qT = sb("ret_qT", [P, MW])
        kT = sb("ret_kT", [P, MW])
        qwT = sb("ret_qwT", [P, MW])
        sT = sb("ret_sT", [P, MW])
        state = sb("ret_state", [P, MW])
        loaded = sem("ret_loaded")
        product_done = [sem("rotq_product"), sem("rotk_product")]
        rotated = [sem("q_rotated"), sem("k_rotated")]
        turned, q_out, k_out, qw_out = sem("ret_turned"), sem("ret_q_out"), sem("ret_k_out"), sem("ret_qw_out")
        kw_done, scored, decayed, grown, summed, o_out, shrunk, state_done = (
            sem("ret_" + n) for n in ("kw_done", "scored", "decayed", "grown", "summed", "o_out", "shrunk",
                                      "state_done"))
        ps = m.ps
        block = ctx.enter_context(nc.Block())

        def rotate(eng, j, n):
            x = m.r_qkv[:, j, ds(n, 1), :].rearrange("p a (h c f) -> p (a h) c f", c=2, f=F)
            xc = product[:, j, 0].rearrange("p (h c f) -> p h c f", c=2, f=F)
            xs = product[:, j, 1].rearrange("p (h c f) -> p h c f", c=2, f=F)
            out = rot[:, j].rearrange("p (h c f) -> p h c f", c=2, f=F)
            for tab, to in ((m.cos, xc), (m.sin, xs)):
                row = tab[:, ds(n, 1), :].unsqueeze(1).to_broadcast([P, MH, 2, F])
                eng.tensor_tensor(to, x, row, ALU.mult).then_inc(product_done[j], 1)
            eng.wait_ge(product_done[j], 2 * n + 2)
            eng.wait_ge(turned, n)
            eng.tensor_tensor(out[:, :, 0, :], xc[:, :, 0, :], xs[:, :, 1, :], ALU.subtract
                              ).then_inc(rotated[j], 1)
            eng.tensor_tensor(out[:, :, 1, :], xs[:, :, 0, :], xc[:, :, 1, :], ALU.add
                              ).then_inc(rotated[j], 1)

        @block.sync
        def _(sp):
            sp.dma_start(tables[:], d["ret_tables"]).then_inc(loaded, 16)
            sp.dma_start(kdecay[:], d["ret_kdecay"]).then_inc(loaded, 16)

        @block.gpsimd
        def _(pool):
            pool.wait_ge(loaded, 32)
            with pool.Fori(0, TT) as n:
                pool.wait_ge(rotated[1], 2 * n)
                rotate(pool, 1, n)
                pool.wait_ge(rotated[1], 2 * n + 2)
                pool.wait_ge(grown, n)
                pool.tensor_tensor(heads_of(kw[:]), heads_of(rot[:, 1]),
                                   kdecay[:].unsqueeze(2).to_broadcast([P, MH, MHD]), ALU.mult
                                   ).then_inc(kw_done, 1)

        @block.vector
        def _(dve):
            dve.memset(state[:], 0.0).then_inc(state_done, 1)
            dve.wait_ge(loaded, 32)
            with dve.Fori(0, TT) as n:
                dve.wait_ge(rotated[0], 2 * n)
                rotate(dve, 0, n)
                dve.wait_ge(q_out, n + 1)
                dve.wait_ge(summed, n)
                dve.tensor_tensor(qwT[:], qT[:], qdecay, ALU.mult).then_inc(qw_out, 1)
                dve.wait_ge(scored, n + 1)
                dve.tensor_tensor(sT[:], ps[:, 2, :], decay, ALU.mult).then_inc(decayed, 1)
                dve.wait_ge(summed, n + 1)
                dve.tensor_tensor(state[:], state[:], sdecay, ALU.mult).then_inc(shrunk, 1)
                dve.wait_ge(shrunk, n + 1)
                dve.wait_ge(grown, n + 1)
                dve.tensor_tensor(state[:], state[:], ps[:, 4, :], ALU.add).then_inc(state_done, 1)

        @block.tensor
        def _(pe):
            with pe.Fori(0, TT) as n:
                for j in range(2):
                    pe.wait_ge(rotated[j], 2 * n + 2)
                pe.wait_ge(q_out, n)
                pe.wait_ge(k_out, n)
                pe.wait_ge(kw_done, n + 1)
                for j in range(2):
                    for h in range(MH):
                        ins = pe.transpose(ps[:, j, h * MHD:(h + 1) * MHD], rot[:, j, h * MHD:(h + 1) * MHD],
                                           m.ident[:])
                ins.then_inc(turned, 1)
                pe.wait_ge(state_done, n + 1)
                for h in range(MH):
                    cols = slice(h * MHD, (h + 1) * MHD)
                    ins = pe.matmul(ps[:, 4, cols], kw[:, cols],
                                    m.r_qkv[:, 2, ds(n, 1), cols].rearrange("p a c -> p (a c)"),
                                    start=True, stop=True)
                ins.then_inc(grown, 1)
                pe.wait_ge(q_out, n + 1)
                pe.wait_ge(k_out, n + 1)
                pe.wait_ge(decayed, n)
                for h in range(MH):
                    cols = slice(h * MHD, (h + 1) * MHD)
                    ins = pe.matmul(ps[:, 2, cols], kT[:, cols], qT[:, cols], start=True, stop=True)
                ins.then_inc(scored, 1)
                pe.wait_ge(decayed, n + 1)
                pe.wait_ge(qw_out, n + 1)
                pe.wait_ge(o_out, n)
                for h in range(MH):
                    cols = slice(h * MHD, (h + 1) * MHD)
                    ins = group(pe, ps[:, 3, cols],
                                [(qwT[:, cols], state[:, cols]),
                                 (sT[:, cols], m.r_qkv[:, 2, ds(n, 1), cols].rearrange("p a c -> p (a c)"))])
                ins.then_inc(summed, 1)

        @block.scalar
        def _(act):
            with act.Fori(0, TT) as n:
                act.wait_ge(turned, n + 1)
                act.wait_ge(scored, n)
                act.wait_ge(qw_out, n)
                act.activation(qT[:], ps[:, 0, :], ACT.Copy).then_inc(q_out, 1)
                act.activation(kT[:], ps[:, 1, :], ACT.Copy).then_inc(k_out, 1)
                act.wait_ge(summed, n + 1)
                act.activation(m.r_qkv[:, 0, ds(n, 1), :].rearrange("p a c -> p (a c)"), ps[:, 3, :], ACT.Copy
                               ).then_inc(o_out, 1)


def stage_head_norm(nc, d, m, name, raw, scratch, gate, weight):
    with ExitStack() as ctx:
        G = sum(r.shape[1] for r in raw)
        ss = ctx.enter_context(nc.sbuf_tensor(name + "_ss", [P, G], F32))
        inv = ctx.enter_context(nc.sbuf_tensor(name + "_inv", [P, G], F32))
        w = ctx.enter_context(nc.sbuf_tensor(name + "_w", [P, MHD], F32))
        squared, summed, meaned, rooted, inverted, loaded, scaled, weighed = (
            nc.alloc_semaphore(name + "_" + n)
            for n in ("squared", "summed", "meaned", "rooted", "inverted", "loaded", "scaled", "weighed"))
        at = [sum(r.shape[1] for r in raw[:n]) for n in range(len(raw) + 1)]
        block = ctx.enter_context(nc.Block())

        @block.sync
        def _(sp):
            if weight is not None:
                sp.dma_start(w[:], weight.partition_broadcast(P)).then_inc(loaded, 16)

        @block.scalar
        def _(act):
            for n, r in enumerate(raw):
                act.activation(scratch[n], r, ACT.Square).then_inc(squared, 1)
            act.wait_ge(meaned, 1)
            act.activation(ss[:], ss[:], ACT.Sqrt).then_inc(rooted, 1)

        @block.vector
        def _(dve):
            for n, r in enumerate(raw):
                dve.wait_ge(squared, n + 1)
                dve.tensor_reduce(ss[:, at[n]:at[n + 1]], scratch[n], AX_X, ALU.add).then_inc(summed, 1)
            dve.wait_ge(summed, len(raw))
            dve.tensor_scalar(ss[:], ss[:], 1.0 / MHD, EPS, ALU.mult, ALU.add).then_inc(meaned, 1)
            dve.wait_ge(rooted, 1)
            dve.reciprocal(inv[:], ss[:]).then_inc(inverted, 1)
            dve.wait_ge(inverted, 1)
            for n, r in enumerate(raw):
                by = inv[:, at[n]:at[n + 1]].unsqueeze(2).to_broadcast([P, r.shape[1], MHD])
                dve.tensor_tensor(r, r, by, ALU.mult).then_inc(scaled, 1)
            if weight is not None:
                dve.wait_ge(loaded, 16)
                for n, r in enumerate(raw):
                    dve.wait_ge(scaled, n + 1)
                    dve.tensor_tensor(r, r, w[:].unsqueeze(1).to_broadcast([P, r.shape[1], MHD]), ALU.mult
                                      ).then_inc(weighed, 1)
            for n, r in enumerate(raw):
                dve.wait_ge(scaled if weight is None else weighed, n + 1)
                dve.tensor_tensor(gate[n], gate[n], r, ALU.mult)




def per_head(ap):
    return ap.unsqueeze(2).to_broadcast([P, MH, MHD])


def over_heads(ap):
    return ap.unsqueeze(1).to_broadcast([P, MH, MHD])


def stage_delta_gates(nc, d, m):
    with ExitStack() as ctx:
        def sb(name, shape, dt=F32):
            return ctx.enter_context(nc.sbuf_tensor(name, shape, dt))

        def sem(name):
            return nc.alloc_semaphore(name)

        rows = sb("dn_rows", [P, 2, MH])
        z = sb("dn_z", [P, TT, MH])
        zmin = sb("dn_zmin", [P, TT, MH])
        soft = sb("dn_soft", [P, TT, MH])
        square = sb("dn_square", [P, 2, T])
        loaded, step, exped, summed, sums_read, coef = (sem("dg_" + n) for n in (
            "loaded", "step", "exped", "summed", "sums_read", "coef"))
        squared, square_summed, rooting, rooted, inverted, normed = (sem("l2_" + n) for n in (
            "squared", "summed", "rooting", "rooted", "inverted", "normed"))
        root = square
        ps = m.ps
        shape = [P, TT, MH]
        N = TT * MH
        block = ctx.enter_context(nc.Block())

        def flat(t):
            return t[:].rearrange("p t h -> p (t h)")

        @block.sync
        def _(sp):
            sp.dma_start(rows[:, 0, :], d["dt_bias"].partition_broadcast(P)).then_inc(loaded, 16)
            sp.dma_start(rows[:, 1, :], d["a_log"].partition_broadcast(P)).then_inc(loaded, 16)

        @block.vector
        def _(dve):
            a = m.ab[:, :, 0:MH]
            dve.wait_ge(loaded, 32)
            dve.tensor_tensor(z[:], a, rows[:, 0, :].unsqueeze(1).to_broadcast(shape), ALU.add
                              ).then_inc(step, 1)
            dve.wait_ge(step, 1)
            dve.tensor_scalar(zmin[:], z[:], 0.0, None, ALU.min).then_inc(step, 1)
            dve.wait_ge(step, 2)
            dve.scalar_tensor_tensor(soft[:], z[:], 0.0, zmin[:], ALU.max, ALU.subtract).then_inc(step, 1)
            dve.wait_ge(exped, 3)
            dve.scalar_tensor_tensor(soft[:], z[:], 0.0, soft[:], ALU.max, ALU.add).then_inc(step, 1)
            dve.wait_ge(step, 4)
            dve.scalar_tensor_tensor(m.dn_g[:], soft[:], -1.0, rows[:, 1, :].unsqueeze(1).to_broadcast(shape),
                                     ALU.mult, ALU.mult).then_inc(step, 1)
            dve.wait_ge(summed, 1)
            dve.tensor_copy(flat(m.dn_cum), ps[:, 7, 0:N]).then_inc(sums_read, 1)
            dve.tensor_copy(flat(m.dn_last), ps[:, 7, N:2 * N]).then_inc(sums_read, 1)
            dve.wait_ge(sums_read, 2)
            dve.tensor_tensor(m.dn_tail[:], m.dn_last[:], m.dn_cum[:], ALU.subtract).then_inc(sums_read, 1)
            dve.wait_ge(exped, 7)
            dve.tensor_tensor(m.dn_bexp[:], m.dn_bexp[:], m.dn_beta[:], ALU.mult).then_inc(coef, 1)

            def norms(first, scale):
                with dve.Fori(0, MH // 2) as i:
                    for s in range(2):
                        n = first + 2 * i + s
                        dve.wait_ge(square_summed, n + 1)
                        sums = ps[:, 2 * s:2 * s + 2, :].rearrange("p b n -> p (b n)")
                        dve.tensor_scalar(root[:, s, :], sums, EPS, None, ALU.add).then_inc(rooting, 1)
                        dve.wait_ge(rooted, n + 1)
                        dve.reciprocal(root[:, s, :], root[:, s, :]).then_inc(inverted, 1)
                        dve.wait_ge(inverted, n + 1)
                        x = m.qkv[:, ds(n, 1), :].rearrange("p c t -> p (c t)")
                        dve.scalar_tensor_tensor(x, x, scale, root[:, s, :], ALU.mult, ALU.mult
                                                 ).then_inc(normed, 1)

            norms(0, MHD ** -0.5)
            norms(MH, 1.0)

        @block.scalar
        def _(act):
            act.wait_ge(step, 3)
            act.activation(soft[:], soft[:], ACT.Exp, scale=-1.0).then_inc(exped, 1)
            act.activation(rows[:, 1, :], rows[:, 1, :], ACT.Exp).then_inc(exped, 1)
            act.wait_ge(exped, 1)
            act.activation(soft[:], soft[:], ACT.Ln, bias=1.0).then_inc(exped, 1)
            act.wait_ge(sums_read, 3)
            act.activation(m.dn_bexp[:], m.dn_cum[:], ACT.Exp).then_inc(exped, 1)
            act.activation(m.dn_tail[:], m.dn_tail[:], ACT.Exp).then_inc(exped, 1)
            act.activation(m.dn_last[:], m.dn_last[:], ACT.Exp).then_inc(exped, 1)
            act.activation(m.dn_beta[:], m.ab[:, :, MH:2 * MH], ACT.Sigmoid).then_inc(exped, 1)
            with act.Fori(0, MH) as i:
                for s in range(2):
                    n = 2 * i + s
                    act.wait_ge(normed, 2 * i)
                    act.activation(square[:, s, :], m.qkv[:, ds(n, 1), :].rearrange("p c t -> p (c t)"),
                                   ACT.Square).then_inc(squared, 1)
                for s in range(2):
                    act.wait_ge(rooting, 2 * i + s + 1)
                    act.activation(root[:, s, :], root[:, s, :], ACT.Sqrt).then_inc(rooted, 1)

        @block.tensor
        def _(pe):
            pe.wait_ge(step, 5)
            pe.matmul(ps[:, 7, 0:N], m.upto[:], flat(m.dn_g), start=True, stop=True)
            pe.matmul(ps[:, 7, N:2 * N], m.ones[:], flat(m.dn_g), start=True, stop=True).then_inc(summed, 1)
            with pe.Fori(0, MH) as i:
                for s in range(2):
                    pe.wait_ge(squared, 2 * i + s + 1)
                    pe.wait_ge(rooting, 2 * i)
                    for h in range(2):
                        ins = pe.matmul(ps[:, 2 * s + h, :], m.ones[:], square[:, s, h * HALF:(h + 1) * HALF],
                                        start=True, stop=True)
                    ins.then_inc(square_summed, 1)


def stage_delta(nc, d, m):
    with ExitStack() as ctx:
        def sb(name, shape, dt=F32):
            return ctx.enter_context(nc.sbuf_tensor(name, shape, dt))

        def sem(name):
            return nc.alloc_semaphore(name)

        def two(name):
            return [sem(name + "0"), sem(name + "1")]

        masks = sb("dn_masks", [P, 2 + LEVELS, P])
        cur = sb("dn_cur", [P, 2, QKV, P])
        state = sb("dn_state", [P, MW])
        more = sb("dn_more", [P, 4, MW])
        tiles = [m.xT[:, k, h * HALF:(h + 1) * HALF] for k in range(DT) for h in range(2)]
        tiles += [more[:, k, :] for k in range(4)]
        names = ["y", "A", "scores", "qg", "kbg", "ktail", "vb", "M", "W", "X"]
        t = [{n: tiles[len(names) * s + k] for k, n in enumerate(names)} for s in range(2)]
        loaded, shrunk, state_done = sem("dn_loaded"), sem("dn_shrunk"), sem("dn_state_done")
        copied, stepped, spread, shifted, grown_exp = (two("dn_" + n) for n in (
            "copied", "stepped", "spread", "shifted", "grown_exp"))
        scores_exp, a_exp, kk, kq, k_turned, v_turned = (two("dn_" + n) for n in (
            "scores_exp", "a_exp", "kk", "kq", "k_turned", "v_turned"))
        a_done, scores_done, k_rows, v_rows, qg_done = (two("dn_" + n) for n in (
            "a_done", "scores_done", "k_rows", "v_rows", "qg_done"))
        masked, y_sum, y_out, w_sum, x_sum, w_done, x_done = (two("dn_" + n) for n in (
            "masked", "y_sum", "y_out", "w_sum", "x_sum", "w_done", "x_done"))
        wT_sum, wT_out, v_sum, v_out, o_sum, o_out, growth = (two("dn_" + n) for n in (
            "wT_sum", "wT_out", "v_sum", "v_out", "o_sum", "o_out", "growth"))
        ps = m.ps
        PAIRS_OF_CHUNKS = TT // 2
        block = ctx.enter_context(nc.Block())

        def bank(s, b):
            return ps[:, 4 * s + b, :]

        def head(h):
            return slice(h * MHD, (h + 1) * MHD)

        def coef(tile, n):
            return per_head(tile[:, ds(n, 1), :].rearrange("p a h -> p (a h)"))

        @block.sync
        def _(sp):
            sp.dma_start(masks[:], d["dn_masks"]).then_inc(loaded, 16)

        @block.gpsimd
        def _(pool):
            pool.wait_ge(loaded, 16)
            with pool.Fori(0, PAIRS_OF_CHUNKS) as i:
                for s in range(2):
                    pool.wait_ge(v_turned[s], i)
                    pool.tensor_copy(cur[:, s], m.qkv[:, :, ds((2 * i + s) * P, P)]).then_inc(copied[s], 1)
                for s in range(2):
                    pool.wait_ge(grown_exp[s], i + 1)
                    pool.wait_ge(copied[s], i + 1)
                    pool.tensor_tensor(t[s]["qg"], cur[:, s, 0:MH, :].rearrange("p h n -> p (h n)"), t[s]["qg"],
                                       ALU.mult).then_inc(qg_done[s], 1)
                for level in range(LEVELS):
                    for s in range(2):
                        if level == 0:
                            pool.wait_ge(a_done[s], 2 * i + 2)
                        else:
                            pool.wait_ge(y_sum[s], LEVELS * i + level)
                            pool.wait_ge(x_done[s], (LEVELS - 1) * i + 1)
                        pool.tensor_tensor(heads_of(t[s]["M"]), heads_of(t[s]["A"]),
                                           over_heads(masks[:, 2 + level, :]), ALU.mult).then_inc(masked[s], 1)

        @block.vector
        def _(dve):
            dve.memset(state[:], 0.0).then_inc(state_done, 1)
            dve.wait_ge(loaded, 16)
            with dve.Fori(0, PAIRS_OF_CHUNKS) as i:
                for s in range(2):
                    dve.tensor_tensor(heads_of(t[s]["y"]), over_heads(m.upto), coef(m.dn_g, 2 * i + s),
                                      ALU.mult).then_inc(stepped[s], 1)
                for s in range(2):
                    dve.wait_ge(spread[s], i + 1)
                    dve.tensor_tensor(heads_of(t[s]["A"]), heads_of(bank(s, 0)), coef(m.dn_cum, 2 * i + s),
                                      ALU.subtract).then_inc(shifted[s], 1)
                for s in range(2):
                    dve.wait_ge(shifted[s], 3 * i + 1)
                    dve.tensor_tensor(heads_of(t[s]["scores"]), heads_of(t[s]["A"]), over_heads(masks[:, 0, :]),
                                      ALU.add).then_inc(shifted[s], 1)
                    dve.scalar_tensor_tensor(heads_of(t[s]["A"]), heads_of(t[s]["A"]), -1.0,
                                             over_heads(masks[:, 1, :]), ALU.mult, ALU.add
                                             ).then_inc(shifted[s], 1)
                for s in range(2):
                    dve.wait_ge(kk[s], i + 1)
                    dve.wait_ge(a_exp[s], i + 1)
                    dve.tensor_tensor(t[s]["A"], bank(s, 1), t[s]["A"], ALU.mult).then_inc(a_done[s], 1)
                for s in range(2):
                    dve.wait_ge(a_done[s], 2 * i + 1)
                    dve.tensor_tensor(heads_of(t[s]["A"]), heads_of(t[s]["A"]), coef(m.dn_beta, 2 * i + s),
                                      ALU.mult).then_inc(a_done[s], 1)
                for s in range(2):
                    dve.wait_ge(kq[s], i + 1)
                    dve.wait_ge(scores_exp[s], i + 1)
                    dve.tensor_tensor(t[s]["scores"], bank(s, 2), t[s]["scores"], ALU.mult
                                      ).then_inc(scores_done[s], 1)
                for s in range(2):
                    dve.wait_ge(k_turned[s], i + 1)
                    dve.tensor_tensor(heads_of(t[s]["kbg"]), heads_of(bank(s, 3)), coef(m.dn_bexp, 2 * i + s),
                                      ALU.mult).then_inc(k_rows[s], 1)
                    dve.tensor_tensor(heads_of(t[s]["ktail"]), heads_of(bank(s, 3)),
                                      coef(m.dn_tail, 2 * i + s), ALU.mult).then_inc(k_rows[s], 1)
                for s in range(2):
                    dve.wait_ge(v_turned[s], i + 1)
                    dve.tensor_tensor(heads_of(t[s]["vb"]), heads_of(bank(s, 3)), coef(m.dn_beta, 2 * i + s),
                                      ALU.mult).then_inc(v_rows[s], 1)
                for level in range(LEVELS):
                    for s in range(2):
                        if level == 0:
                            dve.wait_ge(y_sum[s], LEVELS * i + 1)
                            dve.tensor_tensor(heads_of(t[s]["W"]), over_heads(m.ident), heads_of(bank(s, 0)),
                                              ALU.subtract).then_inc(w_done[s], 1)
                            dve.tensor_tensor(heads_of(t[s]["X"]), over_heads(m.ident), heads_of(t[s]["M"]),
                                              ALU.subtract).then_inc(x_done[s], 1)
                            continue
                        dve.wait_ge(w_sum[s], (LEVELS - 1) * i + level)
                        dve.tensor_tensor(t[s]["W"], t[s]["W"], bank(s, 1), ALU.subtract).then_inc(w_done[s], 1)
                        if level < LEVELS - 1:
                            dve.wait_ge(x_sum[s], (LEVELS - 2) * i + level)
                            dve.tensor_tensor(t[s]["X"], t[s]["X"], bank(s, 2), ALU.subtract
                                              ).then_inc(x_done[s], 1)
                for s in range(2):
                    dve.wait_ge(o_sum[s], i + 1)
                    dve.tensor_tensor(heads_of(state[:]), heads_of(state[:]), coef(m.dn_last, 2 * i + s),
                                      ALU.mult).then_inc(shrunk, 1)
                    dve.wait_ge(shrunk, 2 * i + s + 1)
                    dve.wait_ge(growth[s], i + 1)
                    dve.tensor_tensor(state[:], state[:], bank(s, 3), ALU.add).then_inc(state_done, 1)

        @block.scalar
        def _(act):
            with act.Fori(0, PAIRS_OF_CHUNKS) as i:
                for s in range(2):
                    act.wait_ge(shifted[s], 3 * i + 1)
                    act.activation(t[s]["qg"], bank(s, 0), ACT.Exp).then_inc(grown_exp[s], 1)
                for s in range(2):
                    act.wait_ge(shifted[s], 3 * i + 3)
                    act.activation(t[s]["A"], t[s]["A"], ACT.Exp).then_inc(a_exp[s], 1)
                for s in range(2):
                    act.activation(t[s]["scores"], t[s]["scores"], ACT.Exp).then_inc(scores_exp[s], 1)
                for level in range(1, LEVELS):
                    for s in range(2):
                        act.wait_ge(y_sum[s], LEVELS * i + level + 1)
                        act.activation(t[s]["y"], bank(s, 0), ACT.Copy).then_inc(y_out[s], 1)
                for s in range(2):
                    act.wait_ge(wT_sum[s], i + 1)
                    act.activation(t[s]["y"], bank(s, 0), ACT.Copy, scale=-1.0).then_inc(wT_out[s], 1)
                for s in range(2):
                    act.wait_ge(v_sum[s], i + 1)
                    act.activation(t[s]["X"], bank(s, 1), ACT.Copy).then_inc(v_out[s], 1)
                    act.wait_ge(o_sum[s], i + 1)
                    act.activation(m.qkv[:, 0:MH, ds((2 * i + s) * P, P)], heads_of(bank(s, 2)), ACT.Copy
                                   ).then_inc(o_out[s], 1)

        @block.tensor
        def _(pe):
            with pe.Fori(0, PAIRS_OF_CHUNKS) as i:
                for s in range(2):
                    pe.wait_ge(stepped[s], i + 1)
                    pe.wait_ge(wT_out[s], i)
                    pe.matmul(bank(s, 0), m.ones[:], t[s]["y"], start=True, stop=True).then_inc(spread[s], 1)
                for s in range(2):
                    pe.wait_ge(copied[s], i + 1)
                    pe.wait_ge(v_out[s], i)
                    for h in range(MH):
                        ins = pe.matmul(bank(s, 1)[:, head(h)], cur[:, s, MH + h, :], cur[:, s, MH + h, :],
                                        start=True, stop=True)
                    ins.then_inc(kk[s], 1)
                    pe.wait_ge(o_out[s], i)
                    for h in range(MH):
                        ins = pe.matmul(bank(s, 2)[:, head(h)], cur[:, s, MH + h, :], cur[:, s, h, :],
                                        start=True, stop=True)
                    ins.then_inc(kq[s], 1)
                    pe.wait_ge(state_done, 2 * i + 1)
                    for h in range(MH):
                        ins = pe.transpose(bank(s, 3)[:, head(h)], cur[:, s, MH + h, :], m.ident[:])
                    ins.then_inc(k_turned[s], 1)
                for s in range(2):
                    pe.wait_ge(k_rows[s], 2 * i + 2)
                    for h in range(MH):
                        ins = pe.transpose(bank(s, 3)[:, head(h)], cur[:, s, 2 * MH + h, :], m.ident[:])
                    ins.then_inc(v_turned[s], 1)
                for level in range(LEVELS):
                    for s in range(2):
                        pe.wait_ge(masked[s], LEVELS * i + level + 1)
                        if level == 0:
                            pe.wait_ge(grown_exp[s], i + 1)
                        else:
                            pe.wait_ge(w_done[s], LEVELS * i + level)
                        for h in range(MH):
                            moving = m.ident[:] if level == 0 else t[s]["W"][:, head(h)]
                            ins = pe.matmul(bank(s, 0)[:, head(h)], t[s]["M"][:, head(h)], moving,
                                            start=True, stop=True)
                        ins.then_inc(y_sum[s], 1)
                    if level == 0:
                        continue
                    for s in range(2):
                        pe.wait_ge(y_out[s], (LEVELS - 1) * i + level)
                        pe.wait_ge(x_done[s], (LEVELS - 1) * i + level)
                        for h in range(MH):
                            ins = pe.matmul(bank(s, 1)[:, head(h)], t[s]["X"][:, head(h)],
                                            t[s]["y"][:, head(h)], start=True, stop=True)
                        ins.then_inc(w_sum[s], 1)
                        if level == LEVELS - 1:
                            continue
                        pe.wait_ge(scores_done[s], i + 1)
                        for h in range(MH):
                            ins = pe.matmul(bank(s, 2)[:, head(h)], t[s]["y"][:, head(h)],
                                            t[s]["X"][:, head(h)], start=True, stop=True)
                        ins.then_inc(x_sum[s], 1)
                for s in range(2):
                    pe.wait_ge(w_done[s], LEVELS * i + LEVELS)
                    for h in range(MH):
                        ins = pe.matmul(bank(s, 0)[:, head(h)], t[s]["kbg"][:, head(h)], t[s]["W"][:, head(h)],
                                        start=True, stop=True)
                    ins.then_inc(wT_sum[s], 1)
                for s in range(2):
                    pe.wait_ge(wT_out[s], i + 1)
                    pe.wait_ge(v_rows[s], i + 1)
                    pe.wait_ge(state_done, 2 * i + s + 1)
                    for h in range(MH):
                        ins = group(pe, bank(s, 1)[:, head(h)],
                                    [(t[s]["W"][:, head(h)], t[s]["vb"][:, head(h)]),
                                     (t[s]["y"][:, head(h)], state[:, head(h)])])
                    ins.then_inc(v_sum[s], 1)
                    pe.wait_ge(v_out[s], i + 1)
                    pe.wait_ge(qg_done[s], i + 1)
                    for h in range(MH):
                        ins = group(pe, bank(s, 2)[:, head(h)],
                                    [(t[s]["qg"][:, head(h)], state[:, head(h)]),
                                     (t[s]["scores"][:, head(h)], t[s]["X"][:, head(h)])])
                    ins.then_inc(o_sum[s], 1)
                    for h in range(MH):
                        ins = pe.matmul(bank(s, 3)[:, head(h)], t[s]["ktail"][:, head(h)],
                                        t[s]["X"][:, head(h)], start=True, stop=True)
                    ins.then_inc(growth[s], 1)


def stage_mix_out(nc, d, m):
    with ExitStack() as ctx:
        def sb(name, shape, dt=F32):
            return ctx.enter_context(nc.sbuf_tensor(name, shape, dt))

        def sem(name):
            return nc.alloc_semaphore(name)

        w = sb("w_mix_out", [P, NH, DT, HALF])
        part = sb("mix_part", [P, 2, HALF])
        loaded, turned, turned_out, summed, gated, added = (sem("mix_" + n) for n in (
            "loaded", "turned", "turned_out", "summed", "gated", "added"))
        gate1 = m.mod[:, 2 * D:3 * D]
        ps = m.ps
        block = ctx.enter_context(nc.Block())

        @block.sync
        def _(sp):
            for n in range(NH):
                sp.dma_start(w[:, n], d["w_mix_out"][n]).then_inc(loaded, 16)

        @block.tensor
        def _(pe):
            for t in range(TT):
                if t >= 2:
                    pe.wait_ge(turned_out, t - 1)
                turn_tile(pe, ps, 2 * (t % 2), m.mixed[:, t, :], m.ident[:]).then_inc(turned, 1)
            pe.wait_ge(loaded, 16 * NH)
            pe.wait_ge(turned_out, TT)
            for i in range(NH * TT):
                t, n = i // NH, i % NH
                if i >= 4:
                    pe.wait_ge(gated, i - 3)
                group(pe, ps[:, 4 + i % 4, :], [(m.xT[:, k, t * P:(t + 1) * P], w[:, n, k, :])
                                                for k in range(DT)]).then_inc(summed, 1)

        @block.scalar
        def _(act):
            for t in range(TT):
                act.wait_ge(turned, t + 1)
                act.activation(m.xT[:, :, t * P:(t + 1) * P], two_banks(ps, 2 * (t % 2)), ACT.Copy
                               ).then_inc(turned_out, 1)

        @block.vector
        def _(dve):
            for i in range(NH * TT):
                t, n = i // NH, i % NH
                cols = slice(n * HALF, (n + 1) * HALF)
                dve.wait_ge(summed, i + 1)
                if i >= 2:
                    dve.wait_ge(added, i - 1)
                dve.tensor_tensor(part[:, i % 2], ps[:, 4 + i % 4, :], gate1[:, cols], ALU.mult
                                  ).then_inc(gated, 1)
                dve.wait_ge(gated, i + 1)
                dve.tensor_tensor(m.res[:, t, cols], m.res[:, t, cols], part[:, i % 2], ALU.add
                                  ).then_inc(added, 1)




def stage_route(nc, d, m):
    with ExitStack() as ctx:
        def sb(name, shape, dt=F32):
            return ctx.enter_context(nc.sbuf_tensor(name, shape, dt))

        def sem(name):
            return nc.alloc_semaphore(name)

        C = GROUPS + EXPERTS
        FAR = 64.0
        w = sb("w_route", [P, DT, C])
        bias = sb("route_bias", [P, C])
        ids = sb("token_ids", [P, TT])
        iota = sb("iota", [P, 64])
        zeros = sb("zero_slots", [BLOCKS, P])
        logits = sb("logits", [P, TT, C])
        g_top, g_sum, g_prob = sb("g_top", [P, TT]), sb("g_sum", [P, TT]), sb("g_prob", [P, TT])
        g_exp = sb("g_exp", [P, TT, GROUPS])
        g_hot = sb("g_hot", [P, TT, GROUPS])
        chosen = sb("chosen", [P, TT, EXPERTS])
        e_log = sb("e_log", [P, TT, PER_GROUP])
        e_top = sb("e_top", [P, TOP, TT])
        e_hot = sb("e_hot", [P, TOP, TT, PER_GROUP])
        key = sb("route_key", [P, TT, PER_GROUP])
        key_min = sb("route_key_min", [P, TT])
        second = sb("second", [P, TT])
        hot = sb("hot", [P, TOP, TT, EXPERTS])
        both = sb("both_hot", [P, TT, EXPERTS])
        place = sb("place", [P, TT, EXPERTS])
        carry = sb("route_carry", [P, TT + 1, EXPERTS])
        blocks = sb("expert_blocks", [P, EXPERTS])
        ends = sb("expert_ends", [P, 2, EXPERTS])
        slot_f = sb("slot_f", [P, TOP, TT])
        before_end = sb("before_end", [P, BLOCKS, EXPERTS])
        owner = sb("owner_f", [P, BLOCKS])
        table = sb("slot_rows", [BLOCKS, P])
        loaded, summed, exped, ranked, slots_ready = (sem("route_" + n) for n in (
            "loaded", "summed", "exped", "ranked", "slots_ready"))
        zeroed, cleared, scattered, read_back, turned = (sem("route_" + n) for n in (
            "zeroed", "cleared", "scattered", "read_back", "turned"))
        step = sem("route_step")
        both_ready, shifted = sem("route_both_ready"), sem("route_shifted")
        ps = m.ps
        block = ctx.enter_context(nc.Block())
        SCAN = 5

        @block.sync
        def _(sp):
            sp.dma_start(w[:], d["w_route"]).then_inc(loaded, 16)
            sp.dma_start(bias[:, 0:GROUPS], d["b_group"].partition_broadcast(P)).then_inc(loaded, 16)
            sp.dma_start(bias[:, GROUPS:C], d["b_expert"].partition_broadcast(P)).then_inc(loaded, 16)
            sp.dma_start(ids[:], d["token_ids"]).then_inc(loaded, 16)
            sp.dma_start(iota[:], d["iota"].partition_broadcast(P)).then_inc(loaded, 16)
            sp.wait_ge(zeroed, 1)
            sp.dma_start(d["slot_token"].rearrange("(b p) a -> b (p a)", p=P), zeros[:]).then_inc(cleared, 16)
            sp.wait_ge(scattered, 16 * TOP * TT)
            sp.dma_start(table[:], d["slot_token"].rearrange("(b p) a -> b (p a)", p=P)).then_inc(read_back, 16)

        @block.gpsimd
        def _(pool):
            pool.wait_ge(loaded, 80)
            pool.wait_ge(cleared, 16)
            pool.wait_ge(slots_ready, 1)
            for j in range(TOP):
                for t in range(TT):
                    pool.indirect_dma_start(
                        d["slot_token"], bass.IndirectOffsetOnAxis(ap=m.slot[:, j, t:t + 1], axis=0),
                        ids[:, t:t + 1], None).then_inc(scattered, 16)

        @block.tensor
        def _(pe):
            pe.wait_ge(loaded, 80)
            for t in range(TT):
                ins = group(pe, ps[:, 0, t * C:(t + 1) * C],
                            [(m.xT[:, k, t * P:(t + 1) * P], w[:, k, :]) for k in range(DT)])
            ins.then_inc(summed, 1)
            pe.wait_ge(both_ready, 1)
            flat = both[:].rearrange("p t e -> p (t e)")
            pe.matmul(ps[:, 1, 0:TT * EXPERTS], m.before[:], flat, start=True, stop=True)
            pe.matmul(ps[:, 2, 0:TT * EXPERTS], m.ones[:], flat, start=True, stop=True).then_inc(ranked, 1)
            pe.wait_ge(read_back, 16)
            pe.transpose(ps[:, 3, 0:BLOCKS], table[:], m.ident[0:BLOCKS, 0:BLOCKS]).then_inc(turned, 1)

        @block.scalar
        def _(act):
            act.wait_ge(shifted, 1)
            act.activation(g_exp[:], g_exp[:], ACT.Exp).then_inc(exped, 1)
            act.wait_ge(shifted, 2)
            act.activation(second[:], second[:], ACT.Exp).then_inc(exped, 1)

        @block.vector
        def _(dve):
            done = 0

            def then(ins):
                nonlocal done
                done += 1
                ins.then_inc(step, 1)
                dve.wait_ge(step, done)

            def along(ap, n):
                return ap.unsqueeze(2).to_broadcast([P, TT, n])

            def row(ap, n):
                return ap.unsqueeze(1).to_broadcast([P, TT, n])

            def first_top(values, top, out, n):
                k = key[:, :, 0:n]
                then(dve.tensor_tensor(k, values, along(top, n), ALU.is_equal))
                then(dve.scalar_tensor_tensor(k, k, -FAR, row(iota[:, 0:n], n), ALU.mult, ALU.add))
                then(dve.tensor_reduce(key_min[:], k, AX_X, ALU.min))
                then(dve.tensor_tensor(out, k, along(key_min[:], n), ALU.is_equal))

            dve.memset(zeros[:], 0.0).then_inc(zeroed, 1)
            dve.wait_ge(loaded, 80)
            dve.wait_ge(summed, 1)
            then(dve.tensor_tensor(logits[:], ps[:, 0, 0:TT * C].rearrange("p (t c) -> p t c", c=C),
                                   row(bias[:], C), ALU.add))
            lg = logits[:, :, 0:GROUPS]
            then(dve.tensor_reduce(g_top[:], lg, AX_X, ALU.max))
            dve.tensor_tensor(g_exp[:], lg, along(g_top[:], GROUPS), ALU.subtract).then_inc(shifted, 1)
            first_top(lg, g_top[:], g_hot[:], GROUPS)
            le = logits[:, :, GROUPS:C].rearrange("p t (g e) -> p t g e", g=GROUPS)
            ch = chosen[:].rearrange("p t (g e) -> p t g e", g=GROUPS)
            hot_g = g_hot[:].unsqueeze(3).to_broadcast([P, TT, GROUPS, PER_GROUP])
            then(dve.tensor_tensor(ch, le, hot_g, ALU.mult))
            then(dve.tensor_reduce(e_log[:], chosen[:].rearrange("p t (g e) -> p t e g", g=GROUPS), AX_X,
                                   ALU.add))
            then(dve.tensor_reduce(e_top[:, 0, :], e_log[:], AX_X, ALU.max))
            first_top(e_log[:], e_top[:, 0, :], e_hot[:, 0], PER_GROUP)
            then(dve.scalar_tensor_tensor(e_log[:], e_hot[:, 0], MASKED, e_log[:], ALU.mult, ALU.add))
            then(dve.tensor_reduce(e_top[:, 1, :], e_log[:], AX_X, ALU.max))
            first_top(e_log[:], e_top[:, 1, :], e_hot[:, 1], PER_GROUP)
            dve.tensor_tensor(second[:], e_top[:, 1, :], e_top[:, 0, :], ALU.subtract).then_inc(shifted, 1)
            for j in range(TOP):
                h = hot[:, j].rearrange("p t (g e) -> p t g e", g=GROUPS)
                then(dve.tensor_copy(h, e_hot[:, j].unsqueeze(2).to_broadcast([P, TT, GROUPS, PER_GROUP])))
                then(dve.tensor_tensor(h, h, hot_g, ALU.mult))
            dve.tensor_tensor(both[:], hot[:, 0], hot[:, 1], ALU.add).then_inc(both_ready, 1)
            dve.wait_ge(exped, 2)
            then(dve.tensor_reduce(g_sum[:], g_exp[:], AX_X, ALU.add))
            then(dve.reciprocal(g_prob[:], g_sum[:]))
            then(dve.tensor_scalar(g_sum[:], second[:], 1.0, None, ALU.add))
            then(dve.reciprocal(g_sum[:], g_sum[:]))
            then(dve.tensor_tensor(m.gate[:, 0, :], g_prob[:], g_sum[:], ALU.mult))
            then(dve.tensor_tensor(m.gate[:, 1, :], m.gate[:, 0, :], second[:], ALU.mult))
            dve.wait_ge(ranked, 1)
            total = ps[:, 2, 0:TT * EXPERTS].rearrange("p (t e) -> p t e", e=EXPERTS)
            then(dve.memset(carry[:, 0, :], 0.0))
            for t in range(TT):
                then(dve.tensor_tensor(carry[:, t + 1, :], carry[:, t, :], total[:, t, :], ALU.add))
            then(dve.tensor_scalar(blocks[:], carry[:, TT, :], 1.0 / P, (P - 1.0) / P - 0.5 + 0.5 / P,
                                   ALU.mult, ALU.add))
            then(dve.tensor_scalar(blocks[:], blocks[:], ROUND, ROUND, ALU.add, ALU.subtract))
            then(dve.tensor_copy(ends[:, 0, :], blocks[:]))
            for n in range(SCAN):
                by, a, b = 2 ** n, ends[:, n % 2, :], ends[:, (n + 1) % 2, :]
                then(dve.tensor_copy(b[:, 0:by], a[:, 0:by]))
                then(dve.tensor_tensor(b[:, by:], a[:, by:], a[:, 0:EXPERTS - by], ALU.add))
            end, start = ends[:, SCAN % 2, :], ends[:, (SCAN + 1) % 2, :]
            then(dve.tensor_tensor(start, end, blocks[:], ALU.subtract))
            then(dve.tensor_tensor(place[:], ps[:, 1, 0:TT * EXPERTS].rearrange("p (t e) -> p t e", e=EXPERTS),
                                   carry[:, 0:TT, :], ALU.add))
            then(dve.scalar_tensor_tensor(place[:], row(start, EXPERTS), float(P), place[:], ALU.mult, ALU.add))
            for j in range(TOP):
                then(dve.tensor_tensor(hot[:, j], hot[:, j], place[:], ALU.mult))
                then(dve.tensor_reduce(slot_f[:, j, :], hot[:, j], AX_X, ALU.add))
            dve.tensor_copy(m.slot[:], slot_f[:]).then_inc(slots_ready, 1)
            then(dve.tensor_tensor(before_end[:], end.unsqueeze(1).to_broadcast([P, BLOCKS, EXPERTS]),
                                   iota[:, 0:BLOCKS].unsqueeze(2).to_broadcast([P, BLOCKS, EXPERTS]),
                                   ALU.is_le))
            then(dve.tensor_reduce(owner[:], before_end[:], AX_X, ALU.add))
            then(dve.tensor_scalar(owner[:], owner[:], float(EXPERTS - 1), None, ALU.min))
            dve.tensor_copy(m.owner[:], owner[:])
            dve.tensor_copy(m.used[:], end[:, EXPERTS - 1:EXPERTS])
            dve.wait_ge(turned, 1)
            dve.tensor_copy(m.slot_token[:], ps[:, 3, 0:BLOCKS])


def stage_experts(nc, d, m):
    with ExitStack() as ctx:
        def sb(name, shape, dt=F32):
            return ctx.enter_context(nc.sbuf_tensor(name, shape, dt))

        def sem(name):
            return nc.alloc_semaphore(name)

        def two(name):
            return [sem(name + "0"), sem(name + "1")]

        HT = DE // P
        w13 = sb("w13", [P, 2, 2, DT, DE])
        w2 = sb("w2", [P, 2, HT, D])
        spare = sb("moe_spare", [P, 1])
        index = [sb("slot_index0", [P, 1], U32), sb("slot_index1", [P, 1], U32)]
        tiles = [m.xT[:, k, :] for k in range(DT)]
        x = tiles[0:2]
        xT = [tiles[2].rearrange("p (k n) -> p k n", n=P), tiles[3].rearrange("p (k n) -> p k n", n=P)]
        y = tiles[4:6]
        hid = [tiles[6][:, 0:DE], tiles[6][:, DE:2 * DE]]
        hidT = [tiles[7][:, 0:DE], tiles[7][:, DE:2 * DE]]
        w13_loaded, w2_loaded, indexed, gathered, x_turned, x_out = (two("moe_" + n) for n in (
            "w13_loaded", "w2_loaded", "indexed", "gathered", "x_turned", "x_out"))
        up, silued, hid_done, hid_turned, hidT_out, down, y_out, stored = (two("moe_" + n) for n in (
            "up", "silued", "hid_done", "hid_turned", "hidT_out", "down", "y_out", "stored"))
        ps = m.ps
        PAIRS_OF_BLOCKS = BLOCKS // 2
        block = ctx.enter_context(nc.Block())

        @block.sync
        def _(sp):
            with sp.Fori(0, PAIRS_OF_BLOCKS) as i:
                for s in range(2):
                    expert = sp.value_load(m.owner[0:1, ds(2 * i + s, 1)], min_val=0, max_val=EXPERTS - 1)
                    sp.wait_ge(up[s], 2 * i)
                    sp.dma_start(w13[:, s], d["w13"][ds(expert, 1)].rearrange("a p j k n -> p (a j) k n")
                                 ).then_inc(w13_loaded[s], 16)
                    sp.wait_ge(down[s], 2 * i)
                    sp.dma_start(w2[:, s], d["w2"][ds(expert, 1)].rearrange("a p k n -> p (a k) n")
                                 ).then_inc(w2_loaded[s], 16)

        @block.gpsimd
        def _(pool):
            with pool.Fori(0, PAIRS_OF_BLOCKS) as i:
                for s in range(2):
                    pool.wait_ge(x_turned[s], i)
                    pool.tensor_copy(index[s][:], m.slot_token[:, ds(2 * i + s, 1)]).then_inc(indexed[s], 1)
                    pool.wait_ge(indexed[s], i + 1)
                    pool.tensor_tensor(spare[:], m.ident[:, 0:1], m.ident[:, 1:2], ALU.add)
                    pool.indirect_dma_start(x[s], None, d["h2_rows"],
                                            bass.IndirectOffsetOnAxis(ap=index[s][:], axis=0)
                                            ).then_inc(gathered[s], 16)

        @block.tensor
        def _(pe):
            with pe.Fori(0, PAIRS_OF_BLOCKS) as i:
                for s in range(2):
                    o = 1 - s
                    pe.wait_ge(gathered[s], 16 * (i + 1))
                    pe.wait_ge(x_out[o], i + s)
                    turn_tile(pe, ps, 0, x[s], m.ident[:]).then_inc(x_turned[s], 1)
                    pe.wait_ge(w13_loaded[s], 16 * (i + 1))
                    pe.wait_ge(x_out[s], i + 1)
                    pe.wait_ge(hid_done[o], i + s)
                    for j in range(2):
                        group(pe, ps[:, 2 + j, :], [(xT[s][:, k, :], w13[:, s, j, k, :]) for k in range(DT)]
                              ).then_inc(up[s], 1)
                    pe.wait_ge(hid_done[s], i + 1)
                    pe.wait_ge(hidT_out[o], i + s)
                    for k in range(HT):
                        ins = pe.transpose(ps[:, 4, k * P:(k + 1) * P], hid[s][:, k * P:(k + 1) * P], m.ident[:])
                    ins.then_inc(hid_turned[s], 1)
                    pe.wait_ge(hidT_out[s], i + 1)
                    pe.wait_ge(w2_loaded[s], 16 * (i + 1))
                    for n in range(NH):
                        pe.wait_ge(y_out[o], NH * (i + s))
                        group(pe, ps[:, 5 + n, :], [(hidT[s][:, k * P:(k + 1) * P],
                                                     w2[:, s, k, n * HALF:(n + 1) * HALF]) for k in range(HT)]
                              ).then_inc(down[s], 1)

        @block.scalar
        def _(act):
            with act.Fori(0, PAIRS_OF_BLOCKS) as i:
                for s in range(2):
                    act.wait_ge(x_turned[s], i + 1)
                    act.wait_ge(up[s], 2 * i)
                    act.activation(xT[s], two_banks(ps, 0), ACT.Copy).then_inc(x_out[s], 1)
                    act.wait_ge(up[s], 2 * i + 1)
                    act.wait_ge(hid_turned[s], i)
                    act.activation(hid[s], ps[:, 2, :], ACT.Silu).then_inc(silued[s], 1)
                    act.wait_ge(hid_turned[s], i + 1)
                    act.wait_ge(down[s], 2 * i)
                    act.activation(hidT[s], ps[:, 4, :], ACT.Copy).then_inc(hidT_out[s], 1)
                    act.wait_ge(y_out[s], NH * (i + 1))
                    act.dma_start(d["y_rows"][ds((2 * i + s) * P, P), :], y[s]).then_inc(stored[s], 16)
            for s in range(2):
                act.wait_ge(stored[s], 16 * PAIRS_OF_BLOCKS)

        @block.vector
        def _(dve):
            with dve.Fori(0, PAIRS_OF_BLOCKS) as i:
                for s in range(2):
                    dve.wait_ge(silued[s], i + 1)
                    dve.wait_ge(up[s], 2 * i + 2)
                    dve.tensor_tensor(hid[s], hid[s], ps[:, 3, :], ALU.mult).then_inc(hid_done[s], 1)
                    dve.wait_ge(stored[s], 16 * i)
                    for n in range(NH):
                        dve.wait_ge(down[s], 2 * i + n + 1)
                        dve.tensor_copy(y[s][:, n * HALF:(n + 1) * HALF], ps[:, 5 + n, :]).then_inc(y_out[s], 1)


def stage_final(nc, d, m, out):
    with ExitStack() as ctx:
        def sb(name, shape, dt=F32):
            return ctx.enter_context(nc.sbuf_tensor(name, shape, dt))

        def sem(name):
            return nc.alloc_semaphore(name)

        y = [[sb(f"y{j}{s}", [P, D]) for s in range(2)] for j in range(TOP)]
        square = sb("fin_square", [P, D])
        ss = sb("fin_ss", [P, TT])
        inv = sb("fin_inv", [P, TT])
        w = sb("fin_w", [P, D])
        gathered = [sem("fin_gathered0"), sem("fin_gathered1")]
        loaded, first, gated, added, squared, meaned, rooted, inverted, normed, stored = (
            sem("fin_" + n) for n in ("loaded", "first", "gated", "added", "squared", "meaned",
                                      "rooted", "inverted", "normed", "stored"))
        gate2 = m.mod[:, 5 * D:6 * D]
        block = ctx.enter_context(nc.Block())

        @block.gpsimd
        def _(pool):
            for t in range(TT):
                s = t % 2
                if t >= 2:
                    pool.wait_ge(added, t - 1)
                for j in range(TOP):
                    pool.indirect_dma_start(y[j][s][:], None, d["y_rows"],
                                            bass.IndirectOffsetOnAxis(ap=m.slot[:, j, t:t + 1], axis=0)
                                            ).then_inc(gathered[s], 16)

        @block.vector
        def _(dve):
            for t in range(TT):
                s = t % 2
                dve.wait_ge(gathered[s], 16 * TOP * (t // 2 + 1))
                dve.tensor_scalar(y[0][s][:], y[0][s][:], m.gate[:, 0, t:t + 1], None, ALU.mult
                                  ).then_inc(first, 1)
                dve.wait_ge(first, t + 1)
                dve.scalar_tensor_tensor(y[0][s][:], y[1][s][:], m.gate[:, 1, t:t + 1], y[0][s][:], ALU.mult,
                                         ALU.add).then_inc(gated, 1)
                dve.wait_ge(gated, 2 * t + 1)
                dve.tensor_tensor(y[0][s][:], y[0][s][:], gate2, ALU.mult).then_inc(gated, 1)
                dve.wait_ge(gated, 2 * t + 2)
                dve.tensor_tensor(m.res[:, t, :], m.res[:, t, :], y[0][s][:], ALU.add).then_inc(added, 1)
            dve.wait_ge(squared, TT)
            dve.tensor_scalar(ss[:], ss[:], 1.0 / D, EPS, ALU.mult, ALU.add).then_inc(meaned, 1)
            dve.wait_ge(rooted, 1)
            dve.reciprocal(inv[:], ss[:]).then_inc(inverted, 1)
            dve.wait_ge(inverted, 1)
            dve.wait_ge(loaded, 16)
            for t in range(TT):
                dve.scalar_tensor_tensor(m.res[:, t, :], m.res[:, t, :], inv[:, t:t + 1], w[:], ALU.mult,
                                         ALU.mult).then_inc(normed, 1)

        @block.scalar
        def _(act):
            for t in range(TT):
                act.wait_ge(added, t + 1)
                if t:
                    act.wait_ge(squared, t)
                act.activation(square[:], m.res[:, t, :], ACT.Square, accum_out=ss[:, t:t + 1]
                               ).then_inc(squared, 1)
            act.wait_ge(meaned, 1)
            act.activation(ss[:], ss[:], ACT.Sqrt).then_inc(rooted, 1)

        @block.sync
        def _(sp):
            sp.dma_start(w[:], d["final_norm_w"].partition_broadcast(P)).then_inc(loaded, 16)
            for t in range(TT):
                sp.wait_ge(normed, t + 1)
                sp.dma_start(out[:, t, :], m.res[:, t, :]).then_inc(stored, 16)
            sp.wait_ge(stored, 16 * TT)




class Memory:
    pass


CONSTS = ["ident", "ones", "upto", "before", "ahead"]


def retention_tables():
    log_gamma = np.log1p(-(2.0 ** (-5.0 - np.arange(MH))))
    j, i = np.meshgrid(np.arange(P), np.arange(P), indexing="ij")
    scale = MHD ** -0.5
    rel = np.maximum(i - j, 0)
    decay = np.where(i >= j, np.exp(log_gamma[:, None, None] * rel), 0.0) * scale
    qdecay = np.broadcast_to(np.exp(log_gamma[:, None, None] * (i[None] + 1.0)), (MH, P, P))
    sdecay = np.broadcast_to(np.exp(log_gamma * P)[:, None, None], (MH, P, P))
    tables = np.stack([decay, qdecay, sdecay]).transpose(2, 0, 1, 3).reshape(P, 3, MW)
    kdecay = np.exp(log_gamma[None, :] * (P - 1 - np.arange(P))[:, None]) * scale
    return np.ascontiguousarray(tables, np.float32), np.ascontiguousarray(kdecay, np.float32)


def constants():
    i, j = np.meshgrid(np.arange(P), np.arange(P), indexing="ij")
    blocks = {
        "ident": i == j,
        "ones": i >= 0,
        "upto": i <= j,
        "before": i < j,
        "ahead": (j > i) * MASKED,
    }
    return np.concatenate([np.asarray(blocks[n], np.float32) for n in CONSTS], 1)


def build_program(nc, d, out):
    with ExitStack() as ctx:
        m = Memory()
        m.ps = ctx.enter_context(nc.psum_tensor("ps", [P, 8, HALF], F32))
        m.consts = ctx.enter_context(nc.sbuf_tensor("consts", [P, P * len(CONSTS)], F32))
        m.consts_loaded = ctx.enter_context(nc.semaphore("consts_loaded"))
        m.ident, m.ones, m.upto, m.before, m.ahead = (
            m.consts[:, n * P:(n + 1) * P] for n in range(len(CONSTS)))

        def sb(stack, name, shape, dt=F32):
            return stack.enter_context(nc.sbuf_tensor(name, shape, dt))

        m.ident16 = sb(ctx, "ident16", [P, P], BF16)
        m.ahead16 = sb(ctx, "ahead16", [P, P], BF16)
        m.ones16 = sb(ctx, "ones16", [P, P], BF16)
        m.res = sb(ctx, "res", [P, TT, D])
        m.v = m.res
        m.xT = sb(ctx, "xT", [P, DT, T])
        with nc.cleanup_on_exit():
            first_block(nc, d, m, sb)
        m.mod = sb(ctx, "mod", [P, N_MOD * D])
        stage_per_layer_input(nc, d, m)
        second_block(nc, d, m, sb, out)


def first_block(nc, d, m, sb):
    with ExitStack() as s1:
        m.o = sb(s1, "o", [P, TT, D])
        with ExitStack() as s2:
            m.negc = sb(s2, "negc", [3, HEADS, T], BF16)
            stage_values(nc, d, m)
            stage_attention(nc, d, m)
        stage_attention_out(nc, d, m)
    with ExitStack() as s1:
        m.hT = sb(s1, "hT", [P, FT, T])
        stage_ffn_up(nc, d, m)
        stage_ffn_down(nc, d, m)


def second_block(nc, d, m, sb, out):
    with ExitStack() as s1:
        m.mixed = sb(s1, "mixed", [P, TT, D])
        m.ab = sb(s1, "ab", [P, TT, 2 * MH])
        stage_modulation(nc, d, m)
        stage_modulated_norm(nc, d, m, "norm1", False)
        with ExitStack() as s2:
            m.r_qkv = sb(s2, "r_qkv", [P, 3, TT, MW])
            stage_project_rows(nc, d, m)
            m.cos = sb(s2, "cos", [P, TT, MHD // 2])
            m.sin = sb(s2, "sin", [P, TT, MHD // 2])
            stage_rotary_tables(nc, d, m)
            stage_retention(nc, d, m)
            stage_head_norm(nc, d, m, "ret_norm", [heads_of(m.r_qkv[:, 0, t, :]) for t in range(TT)],
                            [heads_of(m.r_qkv[:, 1, t, :]) for t in range(TT)],
                            [heads_of(m.mixed[:, t, 0:MW]) for t in range(TT)], None)
        with ExitStack() as s2:
            m.qkv = sb(s2, "qkv", [P, QKV, T])
            stage_project_cols(nc, d, m)
            m.dn_g, m.dn_cum, m.dn_last, m.dn_tail, m.dn_bexp, m.dn_beta = (
                sb(s2, "dn_" + name, [P, TT, MH]) for name in ("g", "cum", "last", "tail", "bexp", "beta"))
            with nc.cleanup_on_exit():
                stage_delta_gates(nc, d, m)
                stage_delta(nc, d, m)
            stage_head_norm(nc, d, m, "dn_norm", [m.qkv[:, 0:MH, t * P:(t + 1) * P] for t in range(TT)],
                            [m.qkv[:, MH:2 * MH, t * P:(t + 1) * P] for t in range(TT)],
                            [heads_of(m.mixed[:, t, MW:2 * MW]) for t in range(TT)], d["dn_norm_w"])
        stage_mix_out(nc, d, m)
    stage_modulated_norm(nc, d, m, "norm2", True)
    with ExitStack() as s1:
        m.gate = sb(s1, "gate", [P, TOP, TT])
        m.slot = sb(s1, "slot", [P, TOP, TT], U32)
        m.owner = sb(s1, "owner", [P, BLOCKS], I32)
        m.used = sb(s1, "used", [P, 1], I32)
        m.slot_token = sb(s1, "slot_token", [P, BLOCKS], U32)
        stage_route(nc, d, m)
        stage_experts(nc, d, m)
        stage_final(nc, d, m, out)


def delta_masks():
    i, j = np.meshgrid(np.arange(P), np.arange(P), indexing="ij")
    levels = [(i >> (n + 1) == j >> (n + 1)) & (i >> n & 1 == 1) & (j >> n & 1 == 0) for n in range(LEVELS)]
    masks = [np.where(j >= i, 0.0, MASKED), np.where(j < i, 0.0, MASKED)] + levels
    return np.ascontiguousarray(np.stack(masks, 1), np.float32)


def cols_of(a):
    return np.ascontiguousarray(a.T.reshape(-1, P, a.shape[0]).transpose(1, 0, 2))


def rows_of(a):
    return np.ascontiguousarray(a.reshape(-1, P, a.shape[1]).transpose(1, 0, 2))


def chunks_of(w, width):
    k, n = w.shape
    return np.ascontiguousarray(w.reshape(k // P, P, n // width, width).transpose(2, 1, 0, 3))


def kernel(**inputs):
    import concourse.bacc as bacc
    import concourse.bass_utils as bass_utils

    a = {k: np.asarray(v) for k, v in inputs.items()}
    w_in, w_in2 = a["attn_w_in"][0], a["w_in_2"][0]
    tables, kdecay = retention_tables()
    arrays = {
        "x": rows_of(a["x"][0]),
        "xT": cols_of(a["x"][0]),
        "attn_w": chunks_of(w_in[:, :3 * D], HALF),
        "attn_wqk": np.ascontiguousarray(
            np.concatenate([chunks_of(w_in[:, :D], P), chunks_of(w_in[:, D:2 * D], P)], 3)),
        "attn_wf": rows_of(w_in[:, 3 * D:]),
        "attn_bf": a["attn_b_f"][0],
        "attn_w_out": chunks_of(a["attn_w_out"][0], HALF),
        "ln_mix_g": a["ln_mix_g"][0], "ln_mix_b": a["ln_mix_b"][0],
        "ln_ffn_g": a["ln_ffn_g"][0], "ln_ffn_b": a["ln_ffn_b"][0],
        "ffn_w_up": np.ascontiguousarray(np.concatenate(
            [chunks_of(a["ffn_w_up"][0][:, :FFN], P), chunks_of(a["ffn_w_up"][0][:, FFN:], P)], 3)),
        "ffn_taps": np.ascontiguousarray(a["ffn_conv_w"][0].T.reshape(FT, P, 3).transpose(1, 0, 2)),
        "ffn_bias": np.ascontiguousarray(a["ffn_conv_b"][0].reshape(FT, P).T),
        "ffn_w_down": chunks_of(a["ffn_w_down"][0], P),
        "ple_w_proj": rows_of(a["ple_w_proj"][0]),
        "ple_w_gate": chunks_of(a["ple_w_gate"][0], HALF),
        "ple_b_gate": a["ple_b_gate"][0],
        "pT": cols_of(a["p"][0, 0]),
        "c": np.ascontiguousarray(a["c_2"].reshape(DT, P).T),
        "w_ada": np.ascontiguousarray(a["w_ada_2"][0].reshape(DT, P, N_MOD, D).transpose(0, 2, 1, 3)),
        "consts": constants(),
        "b_ada": a["b_ada_2"][0],
        "norm1_w": a["norm1_w_2"][0], "norm2_w": a["norm2_w_2"][0],
        "w_rows": chunks_of(np.concatenate([w_in2[:, 3 * MW:4 * MW], w_in2[:, 7 * MW:8 * MW],
                                            w_in2[:, :3 * MW]], 1), HALF),
        "w_ab": rows_of(w_in2[:, 8 * MW:]),
        "w_cols": chunks_of(w_in2[:, 4 * MW:7 * MW], P),
        "dn_taps": np.ascontiguousarray(a["conv_w_2"][0].T.reshape(QKV, P, 4).transpose(1, 0, 2)),
        "positions": np.ascontiguousarray(a["positions_2"][0].reshape(TT, P).T),
        "freq": (ROPE_THETA ** (-np.arange(0, MHD, 2, dtype=np.float32) / MHD)).astype(np.float32),
        "dt_bias": a["dt_bias_2"][0], "a_log": a["a_log_2"][0],
        "dn_masks": delta_masks(), "dn_norm_w": a["dn_norm_w_2"][0],
        "w_mix_out": chunks_of(a["w_out_2"][0], HALF),
        "w_route": rows_of(np.concatenate([a["w_group_2"][0], a["w_expert_2"][0]], 1)),
        "b_group": a["b_group_2"][0], "b_expert": a["b_expert_2"][0],
        "token_ids": np.arange(T, dtype=np.float32).reshape(TT, P).T.copy(),
        "iota": np.arange(64, dtype=np.float32),
        "w13": np.ascontiguousarray(np.stack([a["w1_2"][0], a["w3_2"][0]], 1)
                                    .reshape(EXPERTS, 2, DT, P, DE).transpose(0, 3, 1, 2, 4)),
        "w2": np.ascontiguousarray(a["w2_2"][0].reshape(EXPERTS, DE // P, P, D).transpose(0, 2, 1, 3)),
        "final_norm_w": a["final_norm_w_2"],
        "ret_tables": tables, "ret_kdecay": kdecay,
    }
    nc = bacc.Bacc("TRN2", target_bir_lowering=False, num_devices=1)
    d = {k: nc.dram_tensor("in_" + k, v.shape, mybir.dt.from_np(v.dtype), kind="ExternalInput").ap()
         for k, v in arrays.items()}
    out = nc.dram_tensor("out", (P, TT, D), F32, kind="ExternalOutput").ap()
    d["slot_token"] = nc.dram_tensor("slot_rows_dram", (SLOTS, 1), F32, kind="Internal").ap()
    d["y_rows"] = nc.dram_tensor("y_rows", (SLOTS, D), F32, kind="Internal").ap()
    d["h2_rows"] = nc.dram_tensor("h2_rows", (T, D), F32, kind="Internal").ap()
    build_program(nc, d, out)
    r = bass_utils.run_bass_kernel_spmd(nc, [{"in_" + k: v for k, v in arrays.items()}], core_ids=[0])
    got = r.results[0]["out"]
    return np.ascontiguousarray(got.transpose(1, 0, 2)).reshape(1, T, D)
```

```python
from contextlib import ExitStack

import numpy as np

import concourse.bass as bass
from concourse import mybir

F32 = mybir.dt.float32
F32R = mybir.dt.float32r
BF16 = mybir.dt.bfloat16
I32 = mybir.dt.int32
U32 = mybir.dt.uint32
ALU = mybir.AluOpType
ACT = mybir.ActivationFunctionType
AX_X = mybir.AxisListType.X
ds = bass.ds

P = 128
T = 1024
D = 1024
TT = T // P
DT = D // P
HALF = 512
NH = D // HALF

HEADS = 16
HD = 64
PAIRS = HEADS // 2
ALPHA = 2.0 ** 0.25
LN_EPS = 1e-5
FFN = 2816
FT = FFN // P
PLE = 256

EPS = 1e-6
MH = 4
MHD = 128
MW = MH * MHD
QKV = 3 * MW // P
N_MOD = 6
GROUPS = 4
PER_GROUP = 8
EXPERTS = GROUPS * PER_GROUP
TOP = 2
DE = 512
LEVELS = 7
BLOCKS = (TOP * T - EXPERTS) // P + EXPERTS
BLOCKS += BLOCKS % 2
SLOTS = BLOCKS * P
SLOTS_MIN = TOP * T
ROPE_THETA = 10000.0
TWO_PI = 2.0 * np.pi
PI2_A = 6.28125
PI2_B = float(np.float32(np.round((TWO_PI - PI2_A) * 2.0 ** 21) / 2.0 ** 21))
PI2_C = TWO_PI - PI2_A - PI2_B
ROUND = 1.5 * 2.0 ** 23
MASKED = -(2.0 ** 100)


def group(pe, out, operands):
    last = len(operands) - 1
    for n, (stationary, moving) in enumerate(operands):
        ins = pe.matmul(out, stationary, moving, start=(n == 0), stop=(n == last))
    return ins


def split_group(pe, out, operands, start=True, stop=True):
    last = 3 * len(operands) - 1
    n = 0
    for (s_high, s_low), (m_high, m_low) in operands:
        for stationary, moving in ((s_high, m_high), (s_high, m_low), (s_low, m_high)):
            ins = pe.matmul(out, stationary, moving, start=start and n == 0, stop=stop and n == last)
            n += 1
    return ins


def bcast(row, shape):
    return row.to_broadcast(shape)




def stage_values(nc, d, m):
    with ExitStack() as ctx:
        def sb(name, shape, dt=F32):
            return ctx.enter_context(nc.sbuf_tensor(name, shape, dt))

        def sem(name):
            return nc.alloc_semaphore(name)

        wv = sb("wv", [P, NH, DT, HALF])
        wf = sb("wf", [P, DT, HEADS])
        bf = sb("bf", [P, HEADS])
        fg = sb("fg", [P, TT, HEADS])
        fabs = sb("fabs", [P, TT, HEADS])
        fmin = sb("fmin", [P, TT, HEADS])
        lf = sb("lf", [P, TT, HEADS])
        within = sb("within", [P, TT, HEADS])
        carry = sb("carry", [P, TT, HEADS])
        neg = sb("neg", [HEADS, T])
        rest = sb("rest", [HEADS, 2, T])
        parts = sb("parts", [HEADS, 3, T], BF16)
        slice_loaded = [sem(f"v_loaded{k}") for k in range(DT)]
        second_loaded, f_loaded = sem("v_second_loaded"), sem("f_loaded")
        v_bank, v_out, f_bank, f_step = sem("v_bank"), sem("v_out"), sem("f_bank"), sem("f_step")
        f_exp, sums_bank, turned, negated, parted = (sem("f_exp"), sem("f_sums"), sem("f_turned"),
                                                     sem("f_negated"), sem("f_parted"))
        spread = sem("f_spread")
        ps = m.ps
        block = ctx.enter_context(nc.Block())

        @block.sync
        def _(sp):
            for k in range(DT):
                sp.dma_start(m.xT[:, k, :], d["xT"][:, k, :]).then_inc(slice_loaded[k], 16)
                sp.dma_start(wv[:, 0, k, :], d["attn_w"][4][:, k, :]).then_inc(slice_loaded[k], 16)
            sp.dma_start(wf[:], d["attn_wf"]).then_inc(f_loaded, 16)
            sp.dma_start(bf[:], d["attn_bf"].partition_broadcast(P)).then_inc(f_loaded, 16)
            sp.dma_start(wv[:, 1], d["attn_w"][5]).then_inc(second_loaded, 16)
            sp.wait_ge(parted, 5)
            for j in range(3):
                sp.dma_start(m.negc[j:j + 1, :, :], parts[:, j, :]).then_inc(spread, 16)
            sp.wait_ge(spread, 48)

        @block.gpsimd
        def _(pool):
            pool.dma_start(m.consts[:], d["consts"]).then_inc(m.consts_loaded, 16)

        @block.tensor
        def _(pe):
            for n in range(NH):
                for t in range(TT):
                    if n:
                        pe.wait_ge(v_out, TT * (n - 1) + t + 1)
                    for k in range(DT):
                        if t == 0 and n == 0:
                            pe.wait_ge(slice_loaded[k], 32)
                        if t == 0 and n == 1 and k == 0:
                            pe.wait_ge(second_loaded, 16)
                        ins = pe.matmul(ps[:, t, :], m.xT[:, k, t * P:(t + 1) * P], wv[:, n, k, :],
                                        start=(k == 0), stop=(k == DT - 1))
                    ins.then_inc(v_bank, 1)
            pe.wait_ge(f_loaded, 32)
            pe.wait_ge(v_out, TT * (NH - 1) + 1)
            for t in range(TT):
                ins = group(pe, ps[:, 0, t * HEADS:(t + 1) * HEADS],
                            [(m.xT[:, k, t * P:(t + 1) * P], wf[:, k, :]) for k in range(DT)])
            ins.then_inc(f_bank, 1)
            pe.wait_ge(f_step, 4)
            pe.wait_ge(v_out, TT * (NH - 1) + 3)
            pe.wait_ge(m.consts_loaded, 16)
            flat = lf[:].rearrange("p t h -> p (t h)")
            pe.matmul(ps[:, 1, 0:P], m.upto[:], flat, start=True, stop=True)
            pe.matmul(ps[:, 2, 0:P], m.ones[:], flat, start=True, stop=True).then_inc(sums_bank, 1)
            pe.wait_ge(f_step, 5 + TT)
            pe.wait_ge(v_out, TT * NH)
            for t in range(TT):
                ins = pe.transpose(ps[0:HEADS, 4 + t // 4, (t % 4) * P:(t % 4 + 1) * P],
                                   within[:, t, :], m.ident[:])
            ins.then_inc(turned, 1)

        @block.vector
        def _(dve):
            for n in range(NH):
                for t in range(0, TT, 1):
                    dve.wait_ge(v_bank, TT * n + t + 1)
                    dve.tensor_copy(m.v[:, t, n * HALF:(n + 1) * HALF], ps[:, t, :]).then_inc(v_out, 1)
            dve.wait_ge(f_bank, 1)
            dve.wait_ge(f_loaded, 32)
            z = ps[:, 0, 0:TT * HEADS].rearrange("p (t h) -> p t h", t=TT)
            dve.tensor_tensor(fg[:], z, bf[:].unsqueeze(1).to_broadcast([P, TT, HEADS]),
                              ALU.add).then_inc(f_step, 1)
            dve.wait_ge(f_step, 1)
            dve.tensor_scalar(fmin[:], fg[:], 0.0, None, ALU.min).then_inc(f_step, 1)
            dve.wait_ge(f_step, 2)
            dve.scalar_tensor_tensor(fabs[:], fg[:], 0.0, fmin[:], ALU.max, ALU.subtract).then_inc(f_step, 1)
            dve.wait_ge(f_exp, 2)
            dve.tensor_tensor(lf[:], fmin[:], fabs[:], ALU.subtract).then_inc(f_step, 1)
            dve.wait_ge(sums_bank, 1)
            total = ps[:, 2, 0:P].rearrange("p (t h) -> p t h", t=TT)
            dve.memset(carry[:, 0, :], 0.0).then_inc(f_step, 1)
            for t in range(1, TT):
                dve.wait_ge(f_step, 4 + t)
                dve.tensor_tensor(carry[:, t, :], carry[:, t - 1, :], total[:, t - 1, :],
                                  ALU.add).then_inc(f_step, 1)
            dve.wait_ge(f_step, 4 + TT)
            dve.tensor_tensor(within[:], ps[:, 1, 0:P].rearrange("p (t h) -> p t h", t=TT), carry[:],
                              ALU.add).then_inc(f_step, 1)
            dve.wait_ge(turned, 1)
            turned_c = ps[0:HEADS, 4:6, :].rearrange("p b n -> p (b n)")
            dve.tensor_scalar(neg[:], turned_c, -1.0, None, ALU.mult).then_inc(negated, 1)
            dve.wait_ge(negated, 1)
            dve.tensor_copy(parts[:, 0, :], neg[:]).then_inc(parted, 1)
            dve.wait_ge(parted, 1)
            dve.tensor_tensor(rest[:, 0], neg[:], parts[:, 0, :], ALU.subtract).then_inc(parted, 1)
            dve.wait_ge(parted, 2)
            dve.tensor_copy(parts[:, 1, :], rest[:, 0]).then_inc(parted, 1)
            dve.wait_ge(parted, 3)
            dve.tensor_tensor(rest[:, 1], rest[:, 0], parts[:, 1, :], ALU.subtract).then_inc(parted, 1)
            dve.wait_ge(parted, 4)
            dve.tensor_copy(parts[:, 2, :], rest[:, 1]).then_inc(parted, 1)
            dve.wait_ge(m.consts_loaded, 16)
            dve.tensor_copy(m.ident16[:], m.ident[:])
            dve.tensor_copy(m.ahead16[:], m.ahead[:])
            dve.memset(m.ones16[:], 1.0)

        @block.scalar
        def _(act):
            act.wait_ge(f_step, 3)
            act.activation(fabs[:], fabs[:], ACT.Exp, scale=-1.0).then_inc(f_exp, 1)
            act.wait_ge(f_exp, 1)
            act.activation(fabs[:], fabs[:], ACT.Ln, bias=1.0).then_inc(f_exp, 1)


def stage_attention(nc, d, m):
    with ExitStack() as ctx:
        def sb(name, shape, dt=F32):
            return ctx.enter_context(nc.sbuf_tensor(name, shape, dt))

        def sem(name):
            return nc.alloc_semaphore(name)

        wqk = sb("wqk", [P, 2, DT, 2 * P])
        qk = sb("qk", [P, 2, 2, T])
        vp = sb("vp", [P, 2, TT, P])
        probs = sb("probs", [P, 2, T])
        probsT = sb("probsT", [P, 2, TT, P])
        top = sb("top", [P, 4])
        total = sb("total", [P, 4])
        inv = sb("inv", [P, 4])
        w_loaded = [sem("qk_loaded0"), sem("qk_loaded1")]
        proj_bank, proj_out = sem("qk_bank"), sem("qk_out")
        vp_ready = [sem("vp_ready0"), sem("vp_ready1")]
        weighed = [sem("weighed0"), sem("weighed1")]
        scored, maxed, exped = sem("scored"), sem("maxed"), sem("exped")
        turned, turned_out, inverted, o_out = (sem("p_turned"), sem("p_turned_out"), sem("inverted"),
                                               sem("o_out"))
        ps = m.ps
        UNITS = 2 * TT
        block = ctx.enter_context(nc.Block())

        def scores_at(u):
            b = 2 * (u % 2)
            return ps[:, b:b + 2, :].rearrange("p b n -> p (b n)")

        @block.sync
        def _(sp):
            with sp.Fori(0, PAIRS // 2) as i:
                for s in range(2):
                    sp.wait_ge(weighed[s], UNITS * i)
                    sp.dma_start(wqk[:, s], d["attn_wqk"][2 * i + s]).then_inc(w_loaded[s], 16)

        @block.gpsimd
        def _(pool):
            with pool.Fori(0, PAIRS // 2) as i:
                for s in range(2):
                    pool.wait_ge(weighed[s], UNITS * i)
                    pool.tensor_copy(vp[:, s], m.v[:, :, ds((2 * i + s) * P, P)]).then_inc(vp_ready[s], 1)

        @block.tensor
        def _(pe):
            with pe.Fori(0, PAIRS // 2) as i:
                for s in range(2):
                    base = UNITS * (2 * i + s)
                    pe.wait_ge(w_loaded[s], 16 * (i + 1))
                    pe.wait_ge(exped, base)
                    for j in range(2):
                        for h in range(2):
                            group(pe, ps[:, 2 * j + h, :],
                                  [(wqk[:, s, k, j * P:(j + 1) * P], m.xT[:, k, h * HALF:(h + 1) * HALF])
                                   for k in range(DT)]).then_inc(proj_bank, 1)
                    pe.wait_ge(proj_out, 4 * (2 * i + s) + 4)
                    pe.wait_ge(vp_ready[s], i + 1)

                    def scores(u):
                        head, t = u // TT, u % TT
                        lo = head * HD
                        if u >= 2:
                            pe.wait_ge(exped, base + u - 1)
                        q = qk[lo:lo + HD, s, 0, t * P:(t + 1) * P]
                        width = (t + 1) * P
                        for b in range((width + HALF - 1) // HALF):
                            w = min(HALF, width - b * HALF)
                            out = scores_at(u)[:, b * HALF:b * HALF + w]
                            diagonal = b == t // 4
                            pe.matmul(out, q, qk[lo:lo + HD, s, 1, b * HALF:b * HALF + w],
                                      start=True, stop=False)
                            ins = pe.matmul(out, m.ones16[0:3, :],
                                            m.negc[0:3, 4 * i + 2 * s + head, b * HALF:b * HALF + w],
                                            start=False, stop=not diagonal)
                            if diagonal:
                                ins = pe.matmul(scores_at(u)[:, t * P:(t + 1) * P], m.ident16[:],
                                                m.ahead16[:], start=False, stop=True)
                        ins.then_inc(scored, 1)

                    def turn(u):
                        t = u % TT
                        pe.wait_ge(exped, base + u + 1)
                        pe.wait_ge(turned_out, base + u)
                        for k in range(t + 1):
                            ins = pe.transpose(ps[:, 4 + k // 4, (k % 4) * P:(k % 4 + 1) * P],
                                               probs[:, u % 2, k * P:(k + 1) * P], m.ident[:])
                        ins.then_inc(turned, 1)

                    def weigh(u):
                        head, t = u // TT, u % TT
                        pe.wait_ge(turned_out, base + u + 1)
                        pe.wait_ge(o_out, base + max(u - 1, 0))
                        group(pe, ps[:, 6 + u % 2, 0:HD],
                              [(probsT[:, u % 2, k, :], vp[:, s, k, head * HD:(head + 1) * HD])
                               for k in range(t + 1)]).then_inc(weighed[s], 1)

                    scores(0)
                    for u in range(UNITS):
                        if u + 1 < UNITS:
                            scores(u + 1)
                        if u:
                            weigh(u - 1)
                        turn(u)
                    weigh(UNITS - 1)

        @block.vector
        def _(dve):
            with dve.Fori(0, PAIRS // 2) as i:
                for s in range(2):
                    base = UNITS * (2 * i + s)

                    def row_max(u):
                        dve.wait_ge(scored, base + u + 1)
                        dve.tensor_reduce(top[:, u % 4:u % 4 + 1], scores_at(u)[:, 0:(u % TT + 1) * P],
                                          AX_X, ALU.max, negate=True).then_inc(maxed, 1)

                    def out(u):
                        dve.wait_ge(weighed[s], UNITS * i + u + 1)
                        dve.wait_ge(inverted, base + u + 1)
                        head, t = u // TT, u % TT
                        col = (4 * i + 2 * s + head) * HD
                        dve.tensor_scalar(m.o[:, t, ds(col, HD)], ps[:, 6 + u % 2, 0:HD],
                                          inv[:, u % 4:u % 4 + 1], None, ALU.mult).then_inc(o_out, 1)

                    def turned_copy(u):
                        t = u % TT
                        dve.wait_ge(turned, base + u + 1)
                        dve.reciprocal(inv[:, u % 4:u % 4 + 1], total[:, u % 4:u % 4 + 1]).then_inc(inverted, 1)
                        dve.wait_ge(weighed[s], UNITS * i + max(u - 1, 0))
                        both = ps[:, 4:6, :].rearrange("p b n -> p (b n)")
                        dve.tensor_copy(probsT[:, u % 2, 0:t + 1, :].rearrange("p k n -> p (k n)"),
                                        both[:, 0:(t + 1) * P]).then_inc(turned_out, 1)

                    row_max(0)
                    for u in range(UNITS):
                        if u + 1 < UNITS:
                            row_max(u + 1)
                        if u:
                            out(u - 1)
                        turned_copy(u)
                    out(UNITS - 1)

        @block.scalar
        def _(act):
            with act.Fori(0, PAIRS // 2) as i:
                for s in range(2):
                    base = UNITS * (2 * i + s)
                    for n in range(4):
                        act.wait_ge(proj_bank, 4 * (2 * i + s) + n + 1)
                        j, h = n // 2, n % 2
                        act.activation(qk[:, s, j, h * HALF:(h + 1) * HALF], ps[:, n, :], ACT.Copy,
                                       scale=(HD ** -0.5 if j == 0 else 1.0)).then_inc(proj_out, 1)
                    for u in range(UNITS):
                        act.wait_ge(maxed, base + u + 1)
                        act.wait_ge(turned, base + max(u - 1, 0))
                        act.activation(probs[:, u % 2, 0:(u % TT + 1) * P],
                                       scores_at(u)[:, 0:(u % TT + 1) * P], ACT.Exp,
                                       bias=top[:, u % 4:u % 4 + 1],
                                       accum_out=total[:, u % 4:u % 4 + 1]).then_inc(exped, 1)




def turn_tile(pe, ps, bank, rows, ident):
    for k in range(DT):
        ins = pe.transpose(ps[:, bank + k // 4, (k % 4) * P:(k % 4 + 1) * P], rows[:, k * P:(k + 1) * P],
                           ident)
    return ins


def two_banks(ps, bank):
    return ps[:, bank:bank + 2, :].rearrange("p b (k n) -> p (b k) n", n=P)


class Norm:

    def __init__(self, sb, sem, name):
        self.stats = sb(name + "_stats", [P, TT, 2, 6])
        self.mean = sb(name + "_mean", [P, TT, 2])
        self.std = sb(name + "_std", [P, TT, 2])
        self.g = sb(name + "_g", [P, D])
        self.b = sb(name + "_b", [P, D])
        self.stats_done, self.mean_done = sem(name + "_stats_done"), sem(name + "_mean_done")
        self.var_done, self.rooted = sem(name + "_var_done"), sem(name + "_rooted")
        self.inverted, self.normed = sem(name + "_inverted"), sem(name + "_normed")
        self.scaled, self.shifted = sem(name + "_scaled"), sem(name + "_shifted")

    def on_vector(self, dve, row, t):
        for n in range(NH):
            dve.bn_stats(self.stats[:, t, n, :], row[:, n * HALF:(n + 1) * HALF]).then_inc(self.stats_done, 1)
        dve.wait_ge(self.stats_done, 2 * t + 2)
        dve.bn_aggr(self.mean[:, t, :], self.stats[:, t].rearrange("p n s -> p (n s)")
                    ).then_inc(self.mean_done, 1)
        dve.wait_ge(self.mean_done, t + 1)
        dve.tensor_scalar(self.std[:, t, 0:1], self.mean[:, t, 1:2], LN_EPS, None, ALU.add
                          ).then_inc(self.var_done, 1)
        dve.wait_ge(self.rooted, t + 1)
        dve.reciprocal(self.std[:, t, 1:2], self.std[:, t, 0:1]).then_inc(self.inverted, 1)
        dve.wait_ge(self.inverted, t + 1)
        dve.tensor_scalar(row, row, self.mean[:, t, 0:1], self.std[:, t, 1:2], ALU.subtract, ALU.mult
                          ).then_inc(self.normed, 1)
        dve.wait_ge(self.normed, t + 1)
        dve.tensor_tensor(row, row, self.g[:], ALU.mult).then_inc(self.scaled, 1)

    def on_scalar(self, act, t):
        act.wait_ge(self.var_done, t + 1)
        act.activation(self.std[:, t, 0:1], self.std[:, t, 0:1], ACT.Sqrt).then_inc(self.rooted, 1)

    def on_pool(self, pool, row, t):
        pool.wait_ge(self.scaled, t + 1)
        pool.tensor_tensor(row, row, self.b[:], ALU.add).then_inc(self.shifted, 1)


def stage_attention_out(nc, d, m):
    with ExitStack() as ctx:
        def sb(name, shape, dt=F32):
            return ctx.enter_context(nc.sbuf_tensor(name, shape, dt))

        def sem(name):
            return nc.alloc_semaphore(name)

        oT = sb("oT", [P, DT, T])
        w = sb("w_attn_out", [P, NH, DT, HALF])
        norm = Norm(sb, sem, "ln1")
        loaded, x_loaded = sem("ao_loaded"), sem("ao_x_loaded")
        turned, turned_out = sem("o_turned"), sem("oT_out")
        mixed, added = sem("ao_mixed"), sem("ao_added")
        x_turned, high_done, low_done = sem("ao_x_turned"), sem("x1_high_done"), sem("x1_low_done")
        spilled = sem("ao_x1_spilled")
        ps = m.ps
        block = ctx.enter_context(nc.Block())

        @block.sync
        def _(sp):
            for n in range(NH):
                sp.dma_start(w[:, n], d["attn_w_out"][n]).then_inc(loaded, 16)
            sp.dma_start(m.res[:], d["x"]).then_inc(x_loaded, 16)
            sp.dma_start(norm.g[:], d["ln_mix_g"].partition_broadcast(P)).then_inc(x_loaded, 16)
            sp.dma_start(norm.b[:], d["ln_mix_b"].partition_broadcast(P)).then_inc(x_loaded, 16)
            for t in range(TT):
                sp.wait_ge(norm.shifted, t + 1)
                sp.dma_start(d["x1_rows"][:, t, :], m.res[:, t, :]).then_inc(spilled, 16)
            sp.wait_ge(spilled, 16 * TT)

        @block.tensor
        def _(pe):
            for t in range(TT):
                if t >= 2:
                    pe.wait_ge(turned_out, t - 1)
                turn_tile(pe, ps, 2 * (t % 2), m.o[:, t, :], m.ident[:]).then_inc(turned, 1)
            pe.wait_ge(loaded, 16 * NH)
            pe.wait_ge(turned_out, TT)
            for t in range(TT + 2):
                if t < TT:
                    if t >= 2:
                        pe.wait_ge(added, 2 * (t - 1))
                    for n in range(NH):
                        group(pe, ps[:, 2 * (t % 2) + n, :],
                              [(oT[:, k, t * P:(t + 1) * P], w[:, n, k, :]) for k in range(DT)]
                              ).then_inc(mixed, 1)
                if t >= 2:
                    pe.wait_ge(norm.shifted, t - 1)
                    if t >= 4:
                        pe.wait_ge(low_done, t - 3)
                    turn_tile(pe, ps, 4 + 2 * (t % 2), m.res[:, t - 2, :], m.ident[:]).then_inc(x_turned, 1)

        @block.vector
        def _(dve):
            def low(t):
                c = slice(t * P, (t + 1) * P)
                dve.wait_ge(high_done, t + 1)
                dve.tensor_tensor(m.x_low[:, :, c], two_banks(ps, 4 + 2 * (t % 2)),
                                  m.x_high[:, :, c].bitcast(F32), ALU.subtract).then_inc(low_done, 1)

            for t in range(TT):
                dve.wait_ge(turned, t + 1)
                dve.tensor_copy(oT[:, :, t * P:(t + 1) * P], two_banks(ps, 2 * (t % 2))).then_inc(turned_out, 1)
            dve.wait_ge(x_loaded, 48)
            for t in range(TT):
                for n in range(NH):
                    half = m.res[:, t, n * HALF:(n + 1) * HALF]
                    dve.wait_ge(mixed, 2 * t + n + 1)
                    dve.scalar_tensor_tensor(half, half, ALPHA, ps[:, 2 * (t % 2) + n, :], ALU.mult,
                                             ALU.add).then_inc(added, 1)
                dve.wait_ge(added, 2 * t + 2)
                norm.on_vector(dve, m.res[:, t, :], t)
                if t >= 2:
                    low(t - 2)
            for t in range(TT - 2, TT):
                low(t)

        @block.scalar
        def _(act):
            for t in range(TT + 2):
                if t < TT:
                    norm.on_scalar(act, t)
                if t >= 2:
                    act.wait_ge(x_turned, t - 1)
                    act.activation(m.x_high[:, :, (t - 2) * P:(t - 1) * P], two_banks(ps, 4 + 2 * (t % 2)),
                                   ACT.Copy).then_inc(high_done, 1)

        @block.gpsimd
        def _(pool):
            pool.wait_ge(x_loaded, 48)
            for t in range(TT):
                norm.on_pool(pool, m.res[:, t, :], t)




def stage_ffn_up(nc, d, m):
    with ExitStack() as ctx:
        def sb(name, shape, dt=F32):
            return ctx.enter_context(nc.sbuf_tensor(name, shape, dt))

        def sem(name):
            return nc.alloc_semaphore(name)

        TAPS = 3
        w = sb("w_up", [P, DT, 2 * P])
        w_high, w_low = sb("w_up_high", [P, 2, DT, P], F32R), sb("w_up_low", [P, 2, DT, P], F32R)
        taps = sb("ffn_taps", [P, FT, TAPS])
        bias = sb("ffn_bias", [P, FT])
        conv = sb("ffn_conv", [P, 2, T])
        gate = sb("ffn_gate", [P, 2, T])
        taps_loaded = sem("taps_loaded")
        loaded = sem("up_loaded")
        w_high_done, w_split, multiplied = ([sem("up_" + n + "0"), sem("up_" + n + "1")] for n in (
            "w_high_done", "w_split", "multiplied"))
        tap2, tap1, tap0, gelued = sem("up_tap2"), sem("up_tap1"), sem("up_tap0"), sem("up_gelued")
        gated = [sem("up_gated0"), sem("up_gated1")]
        ps = m.ps
        block = ctx.enter_context(nc.Block())

        def u_of(s):
            return ps[:, 4 * s:4 * s + 2, :].rearrange("p b n -> p (b n)")

        def g_of(s):
            return ps[:, 4 * s + 2:4 * s + 4, :].rearrange("p b n -> p (b n)")

        @block.sync
        def _(sp):
            sp.dma_start(taps[:], d["ffn_taps"]).then_inc(taps_loaded, 16)
            sp.dma_start(bias[:], d["ffn_bias"]).then_inc(taps_loaded, 16)
            with sp.Fori(0, FT // 2) as i:
                for s in range(2):
                    sp.wait_ge(w_split[1], 2 * i + s)
                    sp.dma_start(w[:], d["ffn_w_up"][2 * i + s]).then_inc(loaded, 16)

        @block.gpsimd
        def _(pool):
            one = m.ones[:, 0:1].unsqueeze(2).to_broadcast([P, DT, P])
            with pool.Fori(0, FT // 2) as i:
                for s in range(2):
                    for j in range(2):
                        w_j = w[:, :, (1 - j) * P:(2 - j) * P]
                        pool.wait_ge(loaded, 16 * (2 * i + s + 1))
                        pool.wait_ge(multiplied[j], 2 * i + s)
                        pool.tensor_tensor(w_high[:, j], w_j, one, ALU.mult).then_inc(w_high_done[j], 1)
                        pool.wait_ge(w_high_done[j], 2 * i + s + 1)
                        pool.tensor_tensor(w_low[:, j], w_j, w_high[:, j].bitcast(F32), ALU.subtract
                                           ).then_inc(w_split[j], 1)

        @block.tensor
        def _(pe):
            with pe.Fori(0, FT // 2) as i:
                for s in range(2):
                    pe.wait_ge(gated[s], i)
                    for j in range(2):
                        pe.wait_ge(w_split[j], 2 * i + s + 1)
                        for h in range(2):
                            t = slice(h * HALF, (h + 1) * HALF)
                            ins = split_group(pe, ps[:, 4 * s + 2 * (1 - j) + h, :],
                                              [((w_high[:, j, k, :], w_low[:, j, k, :]),
                                                (m.x_high[:, k, t], m.x_low[:, k, t])) for k in range(DT)])
                        ins.then_inc(multiplied[j], 1)

        @block.scalar
        def _(act):
            act.wait_ge(taps_loaded, 32)
            with act.Fori(0, FT // 2) as i:
                for s in range(2):
                    c = 2 * i + s
                    act.wait_ge(multiplied[0], c + 1)
                    act.wait_ge(gelued, c)
                    act.activation(conv[:, s, :], g_of(s), ACT.Identity, bias=bias[:, ds(c, 1)],
                                   scale=taps[:, ds(c, 1), TAPS - 1]).then_inc(tap2, 1)
                    act.wait_ge(tap0, c + 1)
                    act.wait_ge(gated[s], i)
                    act.activation(gate[:, s, :], conv[:, s, :], ACT.Gelu).then_inc(gelued, 1)

        @block.vector
        def _(dve):
            dve.wait_ge(taps_loaded, 32)
            with dve.Fori(0, FT // 2) as i:
                for s in range(2):
                    c = 2 * i + s
                    dve.wait_ge(tap2, c + 1)
                    dve.scalar_tensor_tensor(conv[:, s, 1:T], g_of(s)[:, 0:T - 1], taps[:, ds(c, 1), 1],
                                             conv[:, s, 1:T], ALU.mult, ALU.add).then_inc(tap1, 1)
                    dve.wait_ge(tap1, c + 1)
                    dve.scalar_tensor_tensor(conv[:, s, 2:T], g_of(s)[:, 0:T - 2], taps[:, ds(c, 1), 0],
                                             conv[:, s, 2:T], ALU.mult, ALU.add).then_inc(tap0, 1)
                    dve.wait_ge(gelued, c + 1)
                    dve.wait_ge(multiplied[1], c + 1)
                    dve.tensor_tensor(m.hT[:, ds(c, 1), :].rearrange("p c t -> p (c t)"), gate[:, s, :], u_of(s),
                                      ALU.mult).then_inc(gated[s], 1)


def stage_ffn_down(nc, d, m):
    with ExitStack() as ctx:
        def sb(name, shape, dt=F32):
            return ctx.enter_context(nc.sbuf_tensor(name, shape, dt))

        def sem(name):
            return nc.alloc_semaphore(name)

        def two(name):
            return [sem(name + "0"), sem(name + "1")]

        w = sb("w_down", [P, 2, D])
        w_high, w_low = sb("w_down_high", [P, 2, D], F32R), sb("w_down_low", [P, 2, D], F32R)
        h_high, h_low = sb("h_high", [P, 2, HALF], F32R), sb("h_low", [P, 2, HALF], F32R)
        norm = Norm(sb, sem, "ln2")
        loaded, w_high_done, w_split, h_high_done, h_split, multiplied = (two("down_" + n) for n in (
            "loaded", "w_high_done", "w_split", "h_high_done", "h_split", "multiplied"))
        g_loaded, summed, added = sem("ln2_loaded"), sem("down_summed"), sem("down_added")
        x_turned, x_turned_out = sem("x2_turned"), sem("x2_turned_out")
        x1_loaded = sem("down_x1_loaded")
        ps = m.ps
        BACK = 4
        block = ctx.enter_context(nc.Block())

        def over_features(eng, body):
            pairs = FT // 2
            for half in range(2):
                before = half * pairs
                for s in range(2):
                    body(half, s, s, before, s == 0, False)
                with eng.Fori(1, pairs - 1) as i:
                    for s in range(2):
                        body(half, s, 2 * i + s, before + i, False, False)
                for s in range(2):
                    body(half, s, FT - 2 + s, before + pairs - 1, False, s == 1)
                yield half

        def at(k):
            return ds(k, 1)

        @block.sync
        def _(sp):
            def load(half, s, k, before, first, last):
                if not (isinstance(before, int) and before == 0):
                    sp.wait_ge(w_split[s], before)
                sp.dma_start(w[:, s], d["ffn_w_down"][at(k)].rearrange("a p n -> p (a n)")
                             ).then_inc(loaded[s], 16)

            sp.dma_start(m.res[:], d["x1_rows"]).then_inc(x1_loaded, 16)
            sp.dma_start(norm.g[:], d["ln_ffn_g"].partition_broadcast(P)).then_inc(g_loaded, 16)
            sp.dma_start(norm.b[:], d["ln_ffn_b"].partition_broadcast(P)).then_inc(g_loaded, 16)
            for _ in over_features(sp, load):
                pass

        @block.scalar
        def _(act):
            def high(half, s, k, before, first, last):
                if not (isinstance(before, int) and before == 0):
                    act.wait_ge(multiplied[s], before)
                act.activation(h_high[:, s], m.hT[:, at(k), half * HALF:(half + 1) * HALF]
                               .rearrange("p a t -> p (a t)"), ACT.Copy).then_inc(h_high_done[s], 1)
                act.wait_ge(loaded[s], 16 * before + 16)
                act.activation(w_high[:, s], w[:, s], ACT.Copy).then_inc(w_high_done[s], 1)

            for _ in over_features(act, high):
                pass
            for t in range(TT):
                norm.on_scalar(act, t)
            for t in range(TT):
                act.wait_ge(x_turned, t + 1)
                act.activation(m.xT[:, :, t * P:(t + 1) * P], two_banks(ps, 2 * (t % 2)),
                               ACT.Copy).then_inc(x_turned_out, 1)

        @block.gpsimd
        def _(pool):
            def low(half, s, k, before, first, last):
                pool.wait_ge(w_high_done[s], before + 1)
                pool.tensor_tensor(w_low[:, s], w[:, s], w_high[:, s].bitcast(F32), ALU.subtract
                                   ).then_inc(w_split[s], 1)

            for _ in over_features(pool, low):
                pass
            pool.wait_ge(g_loaded, 32)
            for t in range(TT):
                norm.on_pool(pool, m.res[:, t, :], t)

        @block.tensor
        def _(pe):
            def multiply(half, s, k, before, first, last):
                pe.wait_ge(h_split[s], before + 1)
                pe.wait_ge(w_split[s], before + 1)
                for t in range(BACK):
                    for n in range(NH):
                        if first and half:
                            pe.wait_ge(added, NH * t + n + 1)
                        c, cols = slice(t * P, (t + 1) * P), slice(n * HALF, (n + 1) * HALF)
                        ins = split_group(pe, ps[:, NH * t + n, :],
                                          [((h_high[:, s, c], h_low[:, s, c]),
                                            (w_high[:, s, cols], w_low[:, s, cols]))], first, last)
                        if last and not (t == BACK - 1 and n == NH - 1):
                            ins.then_inc(summed, 1)
                ins.then_inc(multiplied[s], 1)

            for _ in over_features(pe, multiply):
                pass
            for t in range(TT):
                pe.wait_ge(norm.shifted, t + 1)
                if t >= 2:
                    pe.wait_ge(x_turned_out, t - 1)
                turn_tile(pe, ps, 2 * (t % 2), m.res[:, t, :], m.ident[:]).then_inc(x_turned, 1)

        @block.vector
        def _(dve):
            def low(half, s, k, before, first, last):
                dve.wait_ge(h_high_done[s], before + 1)
                dve.tensor_tensor(h_low[:, s], m.hT[:, at(k), half * HALF:(half + 1) * HALF]
                                  .rearrange("p a t -> p (a t)"), h_high[:, s].bitcast(F32), ALU.subtract
                                  ).then_inc(h_split[s], 1)

            for half in over_features(dve, low):
                if half == 0:
                    dve.wait_ge(x1_loaded, 16)
                for t in range(BACK):
                    for n in range(NH):
                        row = m.res[:, half * BACK + t, n * HALF:(n + 1) * HALF]
                        if t == BACK - 1 and n == NH - 1:
                            dve.wait_ge(multiplied[1], (half + 1) * FT // 2)
                        else:
                            dve.wait_ge(summed, half * (NH * BACK - 1) + NH * t + n + 1)
                        dve.scalar_tensor_tensor(row, row, ALPHA, ps[:, NH * t + n, :], ALU.mult, ALU.add
                                                 ).then_inc(added, 1)
            dve.wait_ge(added, NH * TT)
            dve.wait_ge(g_loaded, 32)
            for t in range(TT):
                norm.on_vector(dve, m.res[:, t, :], t)


def stage_per_layer_input(nc, d, m):
    with ExitStack() as ctx:
        def sb(name, shape, dt=F32):
            return ctx.enter_context(nc.sbuf_tensor(name, shape, dt))

        def sem(name):
            return nc.alloc_semaphore(name)

        w = sb("w_ple_gate", [P, NH, DT, HALF])
        wp = sb("w_ple", [P, PLE // P, D])
        pT = sb("pT", [P, PLE // P, T])
        bg = sb("ple_b", [P, D])
        z = sb("ple_z", [P, 2, HALF])
        c = sb("c", [P, DT])
        wa = sb("w_ada", [P, N_MOD, D])
        loaded, p_loaded, c_loaded = sem("ple_loaded"), sem("ple_p_loaded"), sem("c_loaded")
        a_loaded = [sem(f"ada_loaded{n}") for n in range(N_MOD)]
        ada = [sem(f"ada_step{n}") for n in range(N_MOD)]
        summed, biased, gated, scaled, added = (sem("ple_summed"), sem("ple_biased"), sem("ple_gated"),
                                                sem("ple_scaled"), sem("ple_added"))
        c_silu = sem("c_silu")
        ps = m.ps
        STEPS = DT * N_MOD
        PER_HALF = STEPS // (2 * TT)
        block = ctx.enter_context(nc.Block())

        @block.sync
        def _(sp):
            sp.dma_start(wp[:], d["ple_w_proj"]).then_inc(p_loaded, 16)
            sp.dma_start(pT[:], d["pT"]).then_inc(p_loaded, 16)
            sp.dma_start(c[:], d["c"]).then_inc(c_loaded, 16)
            sp.dma_start(bg[:], d["ple_b_gate"].partition_broadcast(P)).then_inc(p_loaded, 16)
            for n in range(NH):
                sp.dma_start(w[:, n], d["ple_w_gate"][n]).then_inc(loaded, 16)
            with sp.Fori(0, DT) as k:
                for n in range(N_MOD):
                    sp.wait_ge(ada[n], k)
                    sp.dma_start(wa[:, n, :], d["w_ada"][k, n]).then_inc(a_loaded[n], 16)

        @block.tensor
        def _(pe):
            pe.wait_ge(p_loaded, 48)
            pe.wait_ge(loaded, 16 * NH)
            for t in range(TT):
                rows = slice(t * P, (t + 1) * P)
                for n in range(NH):
                    i = NH * t + n
                    b = 2 * (i % 4)
                    cols = slice(n * HALF, (n + 1) * HALF)
                    if i >= 4:
                        pe.wait_ge(scaled, i - 3)
                    group(pe, ps[:, b, :], [(m.xT[:, k, rows], w[:, n, k, :]) for k in range(DT)])
                    group(pe, ps[:, b + 1, :], [(pT[:, k, rows], wp[:, k, cols]) for k in range(PLE // P)]
                          ).then_inc(summed, 1)

        @block.scalar
        def _(act):
            act.wait_ge(c_loaded, 16)
            act.activation(c[:], c[:], ACT.Silu).then_inc(c_silu, 1)
            for i in range(NH * TT):
                act.wait_ge(biased, i + 1)
                act.activation(z[:, i % 2], z[:, i % 2], ACT.Sigmoid).then_inc(gated, 1)

        @block.vector
        def _(dve):
            dve.wait_ge(p_loaded, 48)
            dve.wait_ge(c_silu, 1)

            def ada_product(j):
                k, n = j // N_MOD, j % N_MOD
                acc = m.mod[:, n * D:(n + 1) * D]
                dve.wait_ge(a_loaded[n], 16 * (k + 1))
                if k == 0:
                    dve.tensor_scalar(acc, wa[:, n, :], c[:, 0:1], None, ALU.mult).then_inc(ada[n], 1)
                else:
                    dve.wait_ge(ada[n], k)
                    dve.scalar_tensor_tensor(acc, wa[:, n, :], c[:, k:k + 1], acc, ALU.mult, ALU.add
                                             ).then_inc(ada[n], 1)

            for i in range(NH * TT):
                t, n = i // NH, i % NH
                b = 2 * (i % 4)
                cols = slice(n * HALF, (n + 1) * HALF)
                dve.wait_ge(summed, i + 1)
                if i >= 2:
                    dve.wait_ge(added, i - 1)
                dve.tensor_tensor(z[:, i % 2], ps[:, b, :], bg[:, cols], ALU.add).then_inc(biased, 1)
                for j in range(PER_HALF * i, PER_HALF * (i + 1)):
                    ada_product(j)
                dve.wait_ge(gated, i + 1)
                dve.tensor_tensor(z[:, i % 2], z[:, i % 2], ps[:, b + 1, :], ALU.mult).then_inc(scaled, 1)
                dve.wait_ge(scaled, i + 1)
                dve.tensor_tensor(m.res[:, t, cols], m.res[:, t, cols], z[:, i % 2], ALU.add
                                  ).then_inc(added, 1)




def stage_modulation(nc, d, m):
    with ExitStack() as ctx:
        b = ctx.enter_context(nc.sbuf_tensor("b_ada", [P, N_MOD * D], F32))
        nw = ctx.enter_context(nc.sbuf_tensor("norm_w", [P, 2, D], F32))
        loaded, summed, added = (nc.alloc_semaphore(n)
                                 for n in ("mod_loaded", "mod_summed", "mod_added"))
        CH = N_MOD * D // HALF
        block = ctx.enter_context(nc.Block())

        @block.sync
        def _(sp):
            sp.dma_start(b[:], d["b_ada"].partition_broadcast(P)).then_inc(loaded, 16)
            sp.dma_start(nw[:, 0, :], d["norm1_w"].partition_broadcast(P)).then_inc(loaded, 16)
            sp.dma_start(nw[:, 1, :], d["norm2_w"].partition_broadcast(P)).then_inc(loaded, 16)

        @block.tensor
        def _(pe):
            for j in range(CH):
                if j >= 8:
                    pe.wait_ge(added, j - 7)
                pe.matmul(m.ps[:, j % 8, :], m.ones[:], m.mod[:, j * HALF:(j + 1) * HALF],
                          start=True, stop=True).then_inc(summed, 1)

        @block.vector
        def _(dve):
            dve.wait_ge(loaded, 48)
            for j in range(CH):
                cols = slice(j * HALF, (j + 1) * HALF)
                dve.wait_ge(summed, j + 1)
                dve.tensor_tensor(m.mod[:, cols], m.ps[:, j % 8, :], b[:, cols], ALU.add).then_inc(added, 1)
            dve.wait_ge(added, CH)
            for j in range(2):
                scale = m.mod[:, (3 * j + 1) * D:(3 * j + 2) * D]
                dve.scalar_tensor_tensor(scale, scale, 1.0, nw[:, j, :], ALU.add, ALU.mult)


def stage_modulated_norm(nc, d, m, name, second):
    with ExitStack() as ctx:
        def sb(name, shape, dt=F32):
            return ctx.enter_context(nc.sbuf_tensor(name, shape, dt))

        def sem(name):
            return nc.alloc_semaphore(name)

        square = sb(name + "_square", [P, D])
        ss = sb(name + "_ss", [P, TT])
        inv = sb(name + "_inv", [P, TT])
        h = sb(name + "_h", [P, 2, D])
        squared, meaned, rooted, inverted, scaled, shifted = (
            sem(name + "_" + n) for n in ("squared", "meaned", "rooted", "inverted", "scaled", "shifted"))
        turned, turned_out = sem(name + "_turned"), sem(name + "_turned_out")
        stored = [sem(name + "_stored0"), sem(name + "_stored1")]
        j = 3 if second else 0
        shift, scale = m.mod[:, j * D:(j + 1) * D], m.mod[:, (j + 1) * D:(j + 2) * D]
        block = ctx.enter_context(nc.Block())

        @block.scalar
        def _(act):
            for t in range(TT):
                if t:
                    act.wait_ge(squared, t)
                act.activation(square[:], m.res[:, t, :], ACT.Square, accum_out=ss[:, t:t + 1]
                               ).then_inc(squared, 1)
            act.wait_ge(meaned, 1)
            act.activation(ss[:], ss[:], ACT.Sqrt).then_inc(rooted, 1)
            for t in range(TT):
                act.wait_ge(turned, t + 1)
                act.activation(m.xT[:, :, t * P:(t + 1) * P], two_banks(m.ps, 2 * (t % 2)), ACT.Copy
                               ).then_inc(turned_out, 1)

        @block.vector
        def _(dve):
            dve.wait_ge(squared, TT)
            dve.tensor_scalar(ss[:], ss[:], 1.0 / D, EPS, ALU.mult, ALU.add).then_inc(meaned, 1)
            dve.wait_ge(rooted, 1)
            dve.reciprocal(inv[:], ss[:]).then_inc(inverted, 1)
            dve.wait_ge(inverted, 1)
            for t in range(TT):
                s = t % 2
                if t >= 2:
                    dve.wait_ge(turned, t - 1)
                    if second:
                        dve.wait_ge(stored[s], 16 * (t // 2))
                dve.scalar_tensor_tensor(h[:, s], m.res[:, t, :], inv[:, t:t + 1], scale, ALU.mult, ALU.mult
                                         ).then_inc(scaled, 1)
                dve.wait_ge(scaled, t + 1)
                dve.tensor_tensor(h[:, s], h[:, s], shift, ALU.add).then_inc(shifted, 1)

        @block.tensor
        def _(pe):
            for t in range(TT):
                pe.wait_ge(shifted, t + 1)
                if t >= 2:
                    pe.wait_ge(turned_out, t - 1)
                turn_tile(pe, m.ps, 2 * (t % 2), h[:, t % 2], m.ident[:]).then_inc(turned, 1)

        @block.sync
        def _(sp):
            if second:
                for t in range(TT):
                    sp.wait_ge(shifted, t + 1)
                    sp.dma_start(d["h2_rows"][t * P:(t + 1) * P, :], h[:, t % 2]).then_inc(stored[t % 2], 16)
                for s in range(2):
                    sp.wait_ge(stored[s], 16 * (TT // 2))




ROW_CHUNKS = 5


def stage_project_rows(nc, d, m):
    with ExitStack() as ctx:
        def sb(name, shape, dt=F32):
            return ctx.enter_context(nc.sbuf_tensor(name, shape, dt))

        def sem(name):
            return nc.alloc_semaphore(name)

        w = sb("w_rows", [P, 2, DT, HALF])
        wab = sb("w_ab", [P, DT, 2 * MH])
        loaded = [sem("rows_loaded0"), sem("rows_loaded1")]
        ab_loaded, summed, out, ab_summed = sem("ab_loaded"), sem("rows_summed"), sem("rows_out"), sem("ab_summed")
        ps = m.ps
        block = ctx.enter_context(nc.Block())

        @block.sync
        def _(sp):
            for n in range(ROW_CHUNKS):
                if n >= 2:
                    sp.wait_ge(summed, TT * (n - 1))
                sp.dma_start(w[:, n % 2], d["w_rows"][n]).then_inc(loaded[n % 2], 16)
            sp.dma_start(wab[:], d["w_ab"]).then_inc(ab_loaded, 16)

        @block.tensor
        def _(pe):
            for n in range(ROW_CHUNKS):
                pe.wait_ge(loaded[n % 2], 16 * (n // 2 + 1))
                for t in range(TT):
                    if n:
                        pe.wait_ge(out, TT * (n - 1) + t + 1)
                    group(pe, ps[:, t, :], [(m.xT[:, k, t * P:(t + 1) * P], w[:, n % 2, k, :])
                                            for k in range(DT)]).then_inc(summed, 1)
            pe.wait_ge(ab_loaded, 16)
            pe.wait_ge(out, TT * (ROW_CHUNKS - 1) + 1)
            for t in range(TT):
                ins = group(pe, ps[:, 0, t * 2 * MH:(t + 1) * 2 * MH],
                            [(m.xT[:, k, t * P:(t + 1) * P], wab[:, k, :]) for k in range(DT)])
            ins.then_inc(ab_summed, 1)

        @block.scalar
        def _(act):
            for n in range(ROW_CHUNKS):
                for t in range(TT):
                    act.wait_ge(summed, TT * n + t + 1)
                    if n < 2:
                        act.activation(m.mixed[:, t, n * HALF:(n + 1) * HALF], ps[:, t, :], ACT.Silu
                                       ).then_inc(out, 1)
                    else:
                        act.activation(m.r_qkv[:, n - 2, t, :], ps[:, t, :], ACT.Copy).then_inc(out, 1)
            act.wait_ge(ab_summed, 1)
            act.activation(m.ab[:].rearrange("p t c -> p (t c)"), ps[:, 0, 0:TT * 2 * MH], ACT.Copy)


def stage_project_cols(nc, d, m):
    with ExitStack() as ctx:
        def sb(name, shape, dt=F32):
            return ctx.enter_context(nc.sbuf_tensor(name, shape, dt))

        def sem(name):
            return nc.alloc_semaphore(name)

        TAPS = 4
        w = sb("w_cols", [P, 2, DT, P])
        taps = sb("dn_taps", [P, QKV, TAPS])
        conv = sb("dn_conv", [P, 2, T])
        taps_loaded = sem("dn_taps_loaded")
        loaded = [sem("cols_loaded0"), sem("cols_loaded1")]
        summed = [sem("cols_summed0"), sem("cols_summed1")]
        tap3, silued = [sem("tap3_0"), sem("tap3_1")], [sem("silued0"), sem("silued1")]
        tapped = [sem("tapped0"), sem("tapped1")]
        ps = m.ps
        block = ctx.enter_context(nc.Block())

        def sums(s):
            return ps[:, 2 * s:2 * s + 2, :].rearrange("p b n -> p (b n)")

        @block.sync
        def _(sp):
            sp.dma_start(taps[:], d["dn_taps"]).then_inc(taps_loaded, 16)
            with sp.Fori(0, QKV // 2) as i:
                for s in range(2):
                    sp.wait_ge(summed[s], i)
                    sp.dma_start(w[:, s], d["w_cols"][2 * i + s]).then_inc(loaded[s], 16)

        @block.tensor
        def _(pe):
            with pe.Fori(0, QKV // 2) as i:
                for s in range(2):
                    pe.wait_ge(loaded[s], 16 * (i + 1))
                    pe.wait_ge(tapped[s], 3 * i)
                    for h in range(2):
                        ins = group(pe, ps[:, 2 * s + h, :],
                                    [(w[:, s, k, :], m.xT[:, k, h * HALF:(h + 1) * HALF]) for k in range(DT)])
                    ins.then_inc(summed[s], 1)

        @block.scalar
        def _(act):
            act.wait_ge(taps_loaded, 16)
            with act.Fori(0, QKV // 2) as i:
                for s in range(2):
                    act.wait_ge(summed[s], i + 1)
                    act.wait_ge(silued[s], i)
                    act.activation(conv[:, s, :], sums(s), ACT.Identity,
                                   scale=taps[:, ds(2 * i + s, 1), TAPS - 1]).then_inc(tap3[s], 1)
                    act.wait_ge(tap3[s], i + 1)
                    act.wait_ge(tapped[s], 3 * i + 3)
                    act.activation(m.qkv[:, ds(2 * i + s, 1), :].rearrange("p c t -> p (c t)"), conv[:, s, :],
                                   ACT.Silu).then_inc(silued[s], 1)

        @block.vector
        def _(dve):
            dve.wait_ge(taps_loaded, 16)
            with dve.Fori(0, QKV // 2) as i:
                for s in range(2):
                    dve.wait_ge(tap3[s], i + 1)
                    for back in range(1, TAPS):
                        if back > 1:
                            dve.wait_ge(tapped[s], 3 * i + back - 1)
                        dve.scalar_tensor_tensor(conv[:, s, back:T], sums(s)[:, 0:T - back],
                                                 taps[:, ds(2 * i + s, 1), TAPS - 1 - back],
                                                 conv[:, s, back:T], ALU.mult, ALU.add).then_inc(tapped[s], 1)




def heads_of(ap):
    return ap.rearrange("p (h n) -> p h n", n=MHD)


def stage_rotary_tables(nc, d, m):
    with ExitStack() as ctx:
        def sb(name, shape, dt=F32):
            return ctx.enter_context(nc.sbuf_tensor(name, shape, dt))

        def sem(name):
            return nc.alloc_semaphore(name)

        F = MHD // 2
        pos = sb("pos", [P, TT], I32)
        posf = sb("posf", [P, TT])
        freq = sb("freq", [P, F])
        angle = sb("angle", [P, TT, F])
        turns = sb("turns", [P, 2, TT, F])
        loaded, step, folded = sem("pos_loaded"), sem("angle_step"), sem("angle_folded")
        block = ctx.enter_context(nc.Block())

        @block.sync
        def _(sp):
            sp.dma_start(pos[:], d["positions"]).then_inc(loaded, 16)
            sp.dma_start(freq[:], d["freq"].partition_broadcast(P)).then_inc(loaded, 16)

        @block.vector
        def _(dve):
            dve.wait_ge(loaded, 32)
            dve.tensor_copy(posf[:], pos[:]).then_inc(step, 1)
            dve.wait_ge(step, 1)
            dve.tensor_tensor(angle[:], posf[:].unsqueeze(2).to_broadcast([P, TT, F]),
                              freq[:].unsqueeze(1).to_broadcast([P, TT, F]), ALU.mult).then_inc(step, 1)
            n = 2
            for j, (tab, lead) in enumerate(((m.sin, 0.0), (m.cos, 0.25))):
                k = turns[:, j]
                dve.wait_ge(step, n)
                dve.tensor_scalar(k, angle[:], 1.0 / TWO_PI, lead, ALU.mult, ALU.add).then_inc(step, 1)
                dve.wait_ge(step, n + 1)
                dve.tensor_scalar(k, k, ROUND, ROUND, ALU.add, ALU.subtract).then_inc(step, 1)
                n += 2
                before = angle
                for part in (PI2_A, PI2_B, PI2_C):
                    dve.wait_ge(step, n)
                    dve.scalar_tensor_tensor(tab[:], k, -part, before[:], ALU.mult, ALU.add).then_inc(step, 1)
                    before = tab
                    n += 1
                dve.wait_ge(step, n)
                dve.tensor_scalar(tab[:], tab[:], lead * TWO_PI, float(np.float32(3.1415925)), ALU.add, ALU.min
                                  ).then_inc(step, 1)
                n += 1
                dve.wait_ge(step, n)
                dve.tensor_scalar(tab[:], tab[:], -float(np.float32(3.1415925)), None, ALU.max
                                  ).then_inc(folded, 1)

        @block.scalar
        def _(act):
            act.wait_ge(folded, 1)
            act.activation(m.sin[:], m.sin[:], ACT.Sin)
            act.wait_ge(folded, 2)
            act.activation(m.cos[:], m.cos[:], ACT.Sin)


def stage_retention(nc, d, m):
    with ExitStack() as ctx:
        def sb(name, shape, dt=F32):
            return ctx.enter_context(nc.sbuf_tensor(name, shape, dt))

        def sem(name):
            return nc.alloc_semaphore(name)

        F = MHD // 2
        tables = sb("ret_tables", [P, 3, MW])
        kdecay = sb("ret_kdecay", [P, MH])
        decay, qdecay, sdecay = tables[:, 0], tables[:, 1], tables[:, 2]
        product = sb("rot_product", [P, 2, 2, MW])
        rot = sb("rot", [P, 2, MW])
        kw = sb("ret_kw", [P, MW])
        qT = sb("ret_qT", [P, MW])
        kT = sb("ret_kT", [P, MW])
        qwT = sb("ret_qwT", [P, MW])
        sT = sb("ret_sT", [P, MW])
        state = sb("ret_state", [P, MW])
        loaded = sem("ret_loaded")
        product_done = [sem("rotq_product"), sem("rotk_product")]
        rotated = [sem("q_rotated"), sem("k_rotated")]
        turned, q_out, k_out, qw_out = sem("ret_turned"), sem("ret_q_out"), sem("ret_k_out"), sem("ret_qw_out")
        kw_done, scored, decayed, grown, summed, o_out, shrunk, state_done = (
            sem("ret_" + n) for n in ("kw_done", "scored", "decayed", "grown", "summed", "o_out", "shrunk",
                                      "state_done"))
        ps = m.ps
        block = ctx.enter_context(nc.Block())

        def rotate(eng, j, n):
            x = m.r_qkv[:, j, ds(n, 1), :].rearrange("p a (h c f) -> p (a h) c f", c=2, f=F)
            xc = product[:, j, 0].rearrange("p (h c f) -> p h c f", c=2, f=F)
            xs = product[:, j, 1].rearrange("p (h c f) -> p h c f", c=2, f=F)
            out = rot[:, j].rearrange("p (h c f) -> p h c f", c=2, f=F)
            for tab, to in ((m.cos, xc), (m.sin, xs)):
                row = tab[:, ds(n, 1), :].unsqueeze(1).to_broadcast([P, MH, 2, F])
                eng.tensor_tensor(to, x, row, ALU.mult).then_inc(product_done[j], 1)
            eng.wait_ge(product_done[j], 2 * n + 2)
            eng.wait_ge(turned, n)
            eng.tensor_tensor(out[:, :, 0, :], xc[:, :, 0, :], xs[:, :, 1, :], ALU.subtract
                              ).then_inc(rotated[j], 1)
            eng.tensor_tensor(out[:, :, 1, :], xs[:, :, 0, :], xc[:, :, 1, :], ALU.add
                              ).then_inc(rotated[j], 1)

        @block.sync
        def _(sp):
            sp.dma_start(tables[:], d["ret_tables"]).then_inc(loaded, 16)
            sp.dma_start(kdecay[:], d["ret_kdecay"]).then_inc(loaded, 16)

        @block.gpsimd
        def _(pool):
            pool.wait_ge(loaded, 32)
            with pool.Fori(0, TT) as n:
                pool.wait_ge(rotated[1], 2 * n)
                rotate(pool, 1, n)
                pool.wait_ge(rotated[1], 2 * n + 2)
                pool.wait_ge(grown, n)
                pool.tensor_tensor(heads_of(kw[:]), heads_of(rot[:, 1]),
                                   kdecay[:].unsqueeze(2).to_broadcast([P, MH, MHD]), ALU.mult
                                   ).then_inc(kw_done, 1)

        @block.vector
        def _(dve):
            dve.memset(state[:], 0.0).then_inc(state_done, 1)
            dve.wait_ge(loaded, 32)
            with dve.Fori(0, TT) as n:
                dve.wait_ge(rotated[0], 2 * n)
                rotate(dve, 0, n)
                dve.wait_ge(q_out, n + 1)
                dve.wait_ge(summed, n)
                dve.tensor_tensor(qwT[:], qT[:], qdecay, ALU.mult).then_inc(qw_out, 1)
                dve.wait_ge(scored, n + 1)
                dve.tensor_tensor(sT[:], ps[:, 2, :], decay, ALU.mult).then_inc(decayed, 1)
                dve.wait_ge(summed, n + 1)
                dve.tensor_tensor(state[:], state[:], sdecay, ALU.mult).then_inc(shrunk, 1)
                dve.wait_ge(shrunk, n + 1)
                dve.wait_ge(grown, n + 1)
                dve.tensor_tensor(state[:], state[:], ps[:, 4, :], ALU.add).then_inc(state_done, 1)

        @block.tensor
        def _(pe):
            with pe.Fori(0, TT) as n:
                for j in range(2):
                    pe.wait_ge(rotated[j], 2 * n + 2)
                pe.wait_ge(q_out, n)
                pe.wait_ge(k_out, n)
                pe.wait_ge(kw_done, n + 1)
                for j in range(2):
                    for h in range(MH):
                        ins = pe.transpose(ps[:, j, h * MHD:(h + 1) * MHD], rot[:, j, h * MHD:(h + 1) * MHD],
                                           m.ident[:])
                ins.then_inc(turned, 1)
                pe.wait_ge(state_done, n + 1)
                for h in range(MH):
                    cols = slice(h * MHD, (h + 1) * MHD)
                    ins = pe.matmul(ps[:, 4, cols], kw[:, cols],
                                    m.r_qkv[:, 2, ds(n, 1), cols].rearrange("p a c -> p (a c)"),
                                    start=True, stop=True)
                ins.then_inc(grown, 1)
                pe.wait_ge(q_out, n + 1)
                pe.wait_ge(k_out, n + 1)
                pe.wait_ge(decayed, n)
                for h in range(MH):
                    cols = slice(h * MHD, (h + 1) * MHD)
                    ins = pe.matmul(ps[:, 2, cols], kT[:, cols], qT[:, cols], start=True, stop=True)
                ins.then_inc(scored, 1)
                pe.wait_ge(decayed, n + 1)
                pe.wait_ge(qw_out, n + 1)
                pe.wait_ge(o_out, n)
                for h in range(MH):
                    cols = slice(h * MHD, (h + 1) * MHD)
                    ins = group(pe, ps[:, 3, cols],
                                [(qwT[:, cols], state[:, cols]),
                                 (sT[:, cols], m.r_qkv[:, 2, ds(n, 1), cols].rearrange("p a c -> p (a c)"))])
                ins.then_inc(summed, 1)

        @block.scalar
        def _(act):
            with act.Fori(0, TT) as n:
                act.wait_ge(turned, n + 1)
                act.wait_ge(scored, n)
                act.wait_ge(qw_out, n)
                act.activation(qT[:], ps[:, 0, :], ACT.Copy).then_inc(q_out, 1)
                act.activation(kT[:], ps[:, 1, :], ACT.Copy).then_inc(k_out, 1)
                act.wait_ge(summed, n + 1)
                act.activation(m.r_qkv[:, 0, ds(n, 1), :].rearrange("p a c -> p (a c)"), ps[:, 3, :], ACT.Copy
                               ).then_inc(o_out, 1)


def stage_head_norm(nc, d, m, name, raw, scratch, gate, weight):
    with ExitStack() as ctx:
        G = sum(r.shape[1] for r in raw)
        ss = ctx.enter_context(nc.sbuf_tensor(name + "_ss", [P, G], F32))
        inv = ctx.enter_context(nc.sbuf_tensor(name + "_inv", [P, G], F32))
        w = ctx.enter_context(nc.sbuf_tensor(name + "_w", [P, MHD], F32))
        squared, summed, meaned, rooted, inverted, loaded, scaled, weighed = (
            nc.alloc_semaphore(name + "_" + n)
            for n in ("squared", "summed", "meaned", "rooted", "inverted", "loaded", "scaled", "weighed"))
        at = [sum(r.shape[1] for r in raw[:n]) for n in range(len(raw) + 1)]
        block = ctx.enter_context(nc.Block())

        @block.sync
        def _(sp):
            if weight is not None:
                sp.dma_start(w[:], weight.partition_broadcast(P)).then_inc(loaded, 16)

        @block.scalar
        def _(act):
            for n, r in enumerate(raw):
                act.activation(scratch[n], r, ACT.Square).then_inc(squared, 1)
            act.wait_ge(meaned, 1)
            act.activation(ss[:], ss[:], ACT.Sqrt).then_inc(rooted, 1)

        @block.vector
        def _(dve):
            for n, r in enumerate(raw):
                dve.wait_ge(squared, n + 1)
                dve.tensor_reduce(ss[:, at[n]:at[n + 1]], scratch[n], AX_X, ALU.add).then_inc(summed, 1)
            dve.wait_ge(summed, len(raw))
            dve.tensor_scalar(ss[:], ss[:], 1.0 / MHD, EPS, ALU.mult, ALU.add).then_inc(meaned, 1)
            dve.wait_ge(rooted, 1)
            dve.reciprocal(inv[:], ss[:]).then_inc(inverted, 1)
            dve.wait_ge(inverted, 1)
            for n, r in enumerate(raw):
                by = inv[:, at[n]:at[n + 1]].unsqueeze(2).to_broadcast([P, r.shape[1], MHD])
                dve.tensor_tensor(r, r, by, ALU.mult).then_inc(scaled, 1)
            if weight is not None:
                dve.wait_ge(loaded, 16)
                for n, r in enumerate(raw):
                    dve.wait_ge(scaled, n + 1)
                    dve.tensor_tensor(r, r, w[:].unsqueeze(1).to_broadcast([P, r.shape[1], MHD]), ALU.mult
                                      ).then_inc(weighed, 1)
            for n, r in enumerate(raw):
                dve.wait_ge(scaled if weight is None else weighed, n + 1)
                dve.tensor_tensor(gate[n], gate[n], r, ALU.mult)




def per_head(ap):
    return ap.unsqueeze(2).to_broadcast([P, MH, MHD])


def over_heads(ap):
    return ap.unsqueeze(1).to_broadcast([P, MH, MHD])


def stage_delta_gates(nc, d, m):
    with ExitStack() as ctx:
        def sb(name, shape, dt=F32):
            return ctx.enter_context(nc.sbuf_tensor(name, shape, dt))

        def sem(name):
            return nc.alloc_semaphore(name)

        rows = sb("dn_rows", [P, 2, MH])
        z = sb("dn_z", [P, TT, MH])
        zmin = sb("dn_zmin", [P, TT, MH])
        soft = sb("dn_soft", [P, TT, MH])
        square = sb("dn_square", [P, 2, T])
        loaded, step, exped, summed, sums_read, coef = (sem("dg_" + n) for n in (
            "loaded", "step", "exped", "summed", "sums_read", "coef"))
        NORMED = 2 * MH
        pick = sb("l2_pick", [P, NORMED, NORMED])
        spread = sb("l2_spread", [NORMED, NORMED, P])
        root = sb("l2_root", [NORMED, T])
        squared, square_summed, rooting, rooted, inverted, spread_out, normed = (sem("l2_" + n) for n in (
            "squared", "summed", "rooting", "rooted", "inverted", "spread_out", "normed"))
        picks_loaded = sem("l2_picks_loaded")
        ps = m.ps
        shape = [P, TT, MH]
        N = TT * MH
        block = ctx.enter_context(nc.Block())

        def flat(t):
            return t[:].rearrange("p t h -> p (t h)")

        @block.sync
        def _(sp):
            sp.dma_start(rows[:, 0, :], d["dt_bias"].partition_broadcast(P)).then_inc(loaded, 16)
            sp.dma_start(rows[:, 1, :], d["a_log"].partition_broadcast(P)).then_inc(loaded, 16)
            sp.dma_start(pick[:], d["l2_pick"]).then_inc(picks_loaded, 16)
            sp.dma_start(spread[:], d["l2_spread"]).then_inc(picks_loaded, 16)

        @block.vector
        def _(dve):
            a = m.ab[:, :, 0:MH]
            dve.wait_ge(loaded, 32)
            dve.tensor_tensor(z[:], a, rows[:, 0, :].unsqueeze(1).to_broadcast(shape), ALU.add
                              ).then_inc(step, 1)
            dve.wait_ge(step, 1)
            dve.tensor_scalar(zmin[:], z[:], 0.0, None, ALU.min).then_inc(step, 1)
            dve.wait_ge(step, 2)
            dve.scalar_tensor_tensor(soft[:], z[:], 0.0, zmin[:], ALU.max, ALU.subtract).then_inc(step, 1)
            dve.wait_ge(exped, 3)
            dve.scalar_tensor_tensor(soft[:], z[:], 0.0, soft[:], ALU.max, ALU.add).then_inc(step, 1)
            dve.wait_ge(step, 4)
            dve.scalar_tensor_tensor(m.dn_g[:], soft[:], -1.0, rows[:, 1, :].unsqueeze(1).to_broadcast(shape),
                                     ALU.mult, ALU.mult).then_inc(step, 1)
            dve.wait_ge(summed, 1)
            dve.tensor_copy(flat(m.dn_cum), ps[:, 7, 0:N]).then_inc(sums_read, 1)
            dve.tensor_copy(flat(m.dn_last), ps[:, 7, N:2 * N]).then_inc(sums_read, 1)
            dve.wait_ge(sums_read, 2)
            dve.tensor_tensor(m.dn_tail[:], m.dn_last[:], m.dn_cum[:], ALU.subtract).then_inc(sums_read, 1)
            dve.wait_ge(exped, 7)
            dve.tensor_tensor(m.dn_bexp[:], m.dn_bexp[:], m.dn_beta[:], ALU.mult).then_inc(coef, 1)

            dve.wait_ge(square_summed, NORMED)
            dve.tensor_scalar(root[:], ps[0:NORMED, 0:2, :].rearrange("p b n -> p (b n)"), EPS, None, ALU.add
                              ).then_inc(rooting, 1)
            dve.wait_ge(rooted, 1)
            dve.reciprocal(root[:], root[:]).then_inc(inverted, 1)
            for n in range(NORMED):
                dve.wait_ge(spread_out, n + 1)
                b = 2 + 2 * (n % 2)
                dve.tensor_tensor(m.qkv[:, n, :], m.qkv[:, n, :], ps[:, b:b + 2, :].rearrange("p b n -> p (b n)"),
                                  ALU.mult).then_inc(normed, 1)

        @block.scalar
        def _(act):
            act.wait_ge(step, 3)
            act.activation(soft[:], soft[:], ACT.Exp, scale=-1.0).then_inc(exped, 1)
            act.activation(rows[:, 1, :], rows[:, 1, :], ACT.Exp).then_inc(exped, 1)
            act.wait_ge(exped, 1)
            act.activation(soft[:], soft[:], ACT.Ln, bias=1.0).then_inc(exped, 1)
            act.wait_ge(sums_read, 3)
            act.activation(m.dn_bexp[:], m.dn_cum[:], ACT.Exp).then_inc(exped, 1)
            act.activation(m.dn_tail[:], m.dn_tail[:], ACT.Exp).then_inc(exped, 1)
            act.activation(m.dn_last[:], m.dn_last[:], ACT.Exp).then_inc(exped, 1)
            act.activation(m.dn_beta[:], m.ab[:, :, MH:2 * MH], ACT.Sigmoid).then_inc(exped, 1)
            for n in range(NORMED):
                if n >= 2:
                    act.wait_ge(square_summed, n - 1)
                act.activation(square[:, n % 2, :], m.qkv[:, n, :], ACT.Square).then_inc(squared, 1)
            act.wait_ge(rooting, 1)
            act.activation(root[:], root[:], ACT.Sqrt).then_inc(rooted, 1)

        @block.tensor
        def _(pe):
            pe.wait_ge(step, 5)
            pe.matmul(ps[:, 7, 0:N], m.upto[:], flat(m.dn_g), start=True, stop=True)
            pe.matmul(ps[:, 7, N:2 * N], m.ones[:], flat(m.dn_g), start=True, stop=True).then_inc(summed, 1)
            pe.wait_ge(picks_loaded, 32)
            for n in range(NORMED):
                pe.wait_ge(squared, n + 1)
                for h in range(2):
                    ins = pe.matmul(ps[0:NORMED, h, :], pick[:, n, :], square[:, n % 2, h * HALF:(h + 1) * HALF],
                                    start=(n == 0), stop=(n == NORMED - 1))
                ins.then_inc(square_summed, 1)
            pe.wait_ge(inverted, 1)
            for n in range(NORMED):
                if n >= 2:
                    pe.wait_ge(normed, n - 1)
                for h in range(2):
                    ins = pe.matmul(ps[:, 2 + 2 * (n % 2) + h, :], spread[:, n, :],
                                    root[:, h * HALF:(h + 1) * HALF], start=True, stop=True)
                ins.then_inc(spread_out, 1)


def stage_delta(nc, d, m):
    with ExitStack() as ctx:
        def sb(name, shape, dt=F32):
            return ctx.enter_context(nc.sbuf_tensor(name, shape, dt))

        def sem(name):
            return nc.alloc_semaphore(name)

        def two(name):
            return [sem(name + "0"), sem(name + "1")]

        masks = sb("dn_masks", [P, 2 + LEVELS, P])
        cur = sb("dn_cur", [P, 2, QKV, P])
        state = sb("dn_state", [P, MW])
        zeros = sb("zero_rows", [P, D])
        zeroed, filled = sem("rows_zeroed"), sem("rows_filled")
        more = sb("dn_more", [P, 4, MW])
        tiles = [m.xT[:, k, h * HALF:(h + 1) * HALF] for k in range(DT) for h in range(2)]
        tiles += [more[:, k, :] for k in range(4)]
        names = ["y", "A", "scores", "qg", "kbg", "ktail", "vb", "M", "W", "X"]
        t = [{n: tiles[len(names) * s + k] for k, n in enumerate(names)} for s in range(2)]
        loaded, shrunk, state_done = sem("dn_loaded"), sem("dn_shrunk"), sem("dn_state_done")
        copied, stepped, spread, shifted, grown_exp = (two("dn_" + n) for n in (
            "copied", "stepped", "spread", "shifted", "grown_exp"))
        scores_exp, a_exp, kk, kq, k_turned, v_turned = (two("dn_" + n) for n in (
            "scores_exp", "a_exp", "kk", "kq", "k_turned", "v_turned"))
        a_done, scores_done, k_rows, v_rows, qg_done = (two("dn_" + n) for n in (
            "a_done", "scores_done", "k_rows", "v_rows", "qg_done"))
        masked, y_sum, y_out, w_sum, x_sum, w_done, x_done = (two("dn_" + n) for n in (
            "masked", "y_sum", "y_out", "w_sum", "x_sum", "w_done", "x_done"))
        wT_sum, wT_out, v_sum, v_out, o_sum, o_out, growth = (two("dn_" + n) for n in (
            "wT_sum", "wT_out", "v_sum", "v_out", "o_sum", "o_out", "growth"))
        ps = m.ps
        PAIRS_OF_CHUNKS = TT // 2
        block = ctx.enter_context(nc.Block())

        def bank(s, b):
            return ps[:, 4 * s + b, :]

        def head(h):
            return slice(h * MHD, (h + 1) * MHD)

        def coef(tile, n):
            return per_head(tile[:, ds(n, 1), :].rearrange("p a h -> p (a h)"))

        @block.sync
        def _(sp):
            sp.dma_start(masks[:], d["dn_masks"]).then_inc(loaded, 16)
            tail = SLOTS - SLOTS_MIN
            sp.wait_ge(zeroed, 1)
            sp.dma_start(d["y_rows"][SLOTS_MIN:, :].rearrange("(b p) n -> p b n", p=P),
                         zeros[:].unsqueeze(1).to_broadcast([P, tail // P, D])).then_inc(filled, 16)
            sp.wait_ge(filled, 16)

        @block.gpsimd
        def _(pool):
            pool.wait_ge(loaded, 16)
            with pool.Fori(0, PAIRS_OF_CHUNKS) as i:
                for s in range(2):
                    pool.wait_ge(v_turned[s], i)
                    pool.tensor_copy(cur[:, s], m.qkv[:, :, ds((2 * i + s) * P, P)]).then_inc(copied[s], 1)
                for s in range(2):
                    pool.wait_ge(grown_exp[s], i + 1)
                    pool.wait_ge(copied[s], i + 1)
                    pool.tensor_tensor(t[s]["qg"], cur[:, s, 0:MH, :].rearrange("p h n -> p (h n)"), t[s]["qg"],
                                       ALU.mult).then_inc(qg_done[s], 1)
                for level in range(LEVELS):
                    for s in range(2):
                        if level == 0:
                            pool.wait_ge(a_done[s], 2 * i + 2)
                        else:
                            pool.wait_ge(y_sum[s], LEVELS * i + level)
                            pool.wait_ge(x_done[s], (LEVELS - 1) * i + 1)
                        pool.tensor_tensor(heads_of(t[s]["M"]), heads_of(t[s]["A"]),
                                           over_heads(masks[:, 2 + level, :]), ALU.mult).then_inc(masked[s], 1)

        @block.vector
        def _(dve):
            dve.memset(state[:], 0.0).then_inc(state_done, 1)
            dve.memset(zeros[:], 0.0).then_inc(zeroed, 1)
            dve.wait_ge(loaded, 16)
            with dve.Fori(0, PAIRS_OF_CHUNKS) as i:
                for s in range(2):
                    dve.tensor_tensor(heads_of(t[s]["y"]), over_heads(m.upto), coef(m.dn_g, 2 * i + s),
                                      ALU.mult).then_inc(stepped[s], 1)
                for s in range(2):
                    dve.wait_ge(spread[s], i + 1)
                    dve.tensor_tensor(heads_of(t[s]["A"]), heads_of(bank(s, 0)), coef(m.dn_cum, 2 * i + s),
                                      ALU.subtract).then_inc(shifted[s], 1)
                for s in range(2):
                    dve.wait_ge(shifted[s], 3 * i + 1)
                    dve.tensor_tensor(heads_of(t[s]["scores"]), heads_of(t[s]["A"]), over_heads(masks[:, 0, :]),
                                      ALU.add).then_inc(shifted[s], 1)
                    dve.scalar_tensor_tensor(heads_of(t[s]["A"]), heads_of(t[s]["A"]), -1.0,
                                             over_heads(masks[:, 1, :]), ALU.mult, ALU.add
                                             ).then_inc(shifted[s], 1)
                for s in range(2):
                    dve.wait_ge(kk[s], i + 1)
                    dve.wait_ge(a_exp[s], i + 1)
                    dve.tensor_tensor(t[s]["A"], bank(s, 1), t[s]["A"], ALU.mult).then_inc(a_done[s], 1)
                for s in range(2):
                    dve.wait_ge(a_done[s], 2 * i + 1)
                    dve.tensor_tensor(heads_of(t[s]["A"]), heads_of(t[s]["A"]), coef(m.dn_beta, 2 * i + s),
                                      ALU.mult).then_inc(a_done[s], 1)
                for s in range(2):
                    dve.wait_ge(kq[s], i + 1)
                    dve.wait_ge(scores_exp[s], i + 1)
                    dve.tensor_tensor(t[s]["scores"], bank(s, 2), t[s]["scores"], ALU.mult
                                      ).then_inc(scores_done[s], 1)
                for s in range(2):
                    dve.wait_ge(k_turned[s], i + 1)
                    dve.tensor_tensor(heads_of(t[s]["kbg"]), heads_of(bank(s, 3)), coef(m.dn_bexp, 2 * i + s),
                                      ALU.mult).then_inc(k_rows[s], 1)
                    dve.tensor_tensor(heads_of(t[s]["ktail"]), heads_of(bank(s, 3)),
                                      coef(m.dn_tail, 2 * i + s), ALU.mult).then_inc(k_rows[s], 1)
                for s in range(2):
                    dve.wait_ge(v_turned[s], i + 1)
                    dve.tensor_tensor(heads_of(t[s]["vb"]), heads_of(bank(s, 3)), coef(m.dn_beta, 2 * i + s),
                                      ALU.mult).then_inc(v_rows[s], 1)
                for level in range(LEVELS):
                    for s in range(2):
                        if level == 0:
                            dve.wait_ge(y_sum[s], LEVELS * i + 1)
                            dve.tensor_tensor(heads_of(t[s]["W"]), over_heads(m.ident), heads_of(bank(s, 0)),
                                              ALU.subtract).then_inc(w_done[s], 1)
                            dve.tensor_tensor(heads_of(t[s]["X"]), over_heads(m.ident), heads_of(t[s]["M"]),
                                              ALU.subtract).then_inc(x_done[s], 1)
                            continue
                        dve.wait_ge(w_sum[s], (LEVELS - 1) * i + level)
                        dve.tensor_tensor(t[s]["W"], t[s]["W"], bank(s, 1), ALU.subtract).then_inc(w_done[s], 1)
                        if level < LEVELS - 1:
                            dve.wait_ge(x_sum[s], (LEVELS - 2) * i + level)
                            dve.tensor_tensor(t[s]["X"], t[s]["X"], bank(s, 2), ALU.subtract
                                              ).then_inc(x_done[s], 1)
                for s in range(2):
                    dve.wait_ge(o_sum[s], i + 1)
                    dve.tensor_tensor(heads_of(state[:]), heads_of(state[:]), coef(m.dn_last, 2 * i + s),
                                      ALU.mult).then_inc(shrunk, 1)
                    dve.wait_ge(shrunk, 2 * i + s + 1)
                    dve.wait_ge(growth[s], i + 1)
                    dve.tensor_tensor(state[:], state[:], bank(s, 3), ALU.add).then_inc(state_done, 1)

        @block.scalar
        def _(act):
            with act.Fori(0, PAIRS_OF_CHUNKS) as i:
                for s in range(2):
                    act.wait_ge(shifted[s], 3 * i + 1)
                    act.activation(t[s]["qg"], bank(s, 0), ACT.Exp).then_inc(grown_exp[s], 1)
                for s in range(2):
                    act.wait_ge(shifted[s], 3 * i + 3)
                    act.activation(t[s]["A"], t[s]["A"], ACT.Exp).then_inc(a_exp[s], 1)
                for s in range(2):
                    act.activation(t[s]["scores"], t[s]["scores"], ACT.Exp).then_inc(scores_exp[s], 1)
                for level in range(1, LEVELS):
                    for s in range(2):
                        act.wait_ge(y_sum[s], LEVELS * i + level + 1)
                        act.activation(t[s]["y"], bank(s, 0), ACT.Copy).then_inc(y_out[s], 1)
                for s in range(2):
                    act.wait_ge(wT_sum[s], i + 1)
                    act.activation(t[s]["y"], bank(s, 0), ACT.Copy, scale=-1.0).then_inc(wT_out[s], 1)
                for s in range(2):
                    act.wait_ge(v_sum[s], i + 1)
                    act.activation(t[s]["X"], bank(s, 1), ACT.Copy).then_inc(v_out[s], 1)
                    act.wait_ge(o_sum[s], i + 1)
                    act.activation(m.qkv[:, 0:MH, ds((2 * i + s) * P, P)], heads_of(bank(s, 2)), ACT.Copy
                                   ).then_inc(o_out[s], 1)

        @block.tensor
        def _(pe):
            with pe.Fori(0, PAIRS_OF_CHUNKS) as i:
                for s in range(2):
                    pe.wait_ge(stepped[s], i + 1)
                    pe.wait_ge(wT_out[s], i)
                    pe.matmul(bank(s, 0), m.ones[:], t[s]["y"], start=True, stop=True).then_inc(spread[s], 1)
                for s in range(2):
                    pe.wait_ge(copied[s], i + 1)
                    pe.wait_ge(v_out[s], i)
                    for h in range(MH):
                        ins = pe.matmul(bank(s, 1)[:, head(h)], cur[:, s, MH + h, :], cur[:, s, MH + h, :],
                                        start=True, stop=True)
                    ins.then_inc(kk[s], 1)
                    pe.wait_ge(o_out[s], i)
                    for h in range(MH):
                        ins = pe.matmul(bank(s, 2)[:, head(h)], cur[:, s, MH + h, :], cur[:, s, h, :],
                                        start=True, stop=True)
                    ins.then_inc(kq[s], 1)
                    pe.wait_ge(state_done, 2 * i + 1)
                    for h in range(MH):
                        ins = pe.transpose(bank(s, 3)[:, head(h)], cur[:, s, MH + h, :], m.ident[:])
                    ins.then_inc(k_turned[s], 1)
                for s in range(2):
                    pe.wait_ge(k_rows[s], 2 * i + 2)
                    for h in range(MH):
                        ins = pe.transpose(bank(s, 3)[:, head(h)], cur[:, s, 2 * MH + h, :], m.ident[:])
                    ins.then_inc(v_turned[s], 1)
                for level in range(LEVELS):
                    for s in range(2):
                        pe.wait_ge(masked[s], LEVELS * i + level + 1)
                        if level == 0:
                            pe.wait_ge(grown_exp[s], i + 1)
                        else:
                            pe.wait_ge(w_done[s], LEVELS * i + level)
                        for h in range(MH):
                            moving = m.ident[:] if level == 0 else t[s]["W"][:, head(h)]
                            ins = pe.matmul(bank(s, 0)[:, head(h)], t[s]["M"][:, head(h)], moving,
                                            start=True, stop=True)
                        ins.then_inc(y_sum[s], 1)
                    if level == 0:
                        continue
                    for s in range(2):
                        pe.wait_ge(y_out[s], (LEVELS - 1) * i + level)
                        pe.wait_ge(x_done[s], (LEVELS - 1) * i + level)
                        for h in range(MH):
                            ins = pe.matmul(bank(s, 1)[:, head(h)], t[s]["X"][:, head(h)],
                                            t[s]["y"][:, head(h)], start=True, stop=True)
                        ins.then_inc(w_sum[s], 1)
                        if level == LEVELS - 1:
                            continue
                        pe.wait_ge(scores_done[s], i + 1)
                        for h in range(MH):
                            ins = pe.matmul(bank(s, 2)[:, head(h)], t[s]["y"][:, head(h)],
                                            t[s]["X"][:, head(h)], start=True, stop=True)
                        ins.then_inc(x_sum[s], 1)
                for s in range(2):
                    pe.wait_ge(w_done[s], LEVELS * i + LEVELS)
                    for h in range(MH):
                        ins = pe.matmul(bank(s, 0)[:, head(h)], t[s]["kbg"][:, head(h)], t[s]["W"][:, head(h)],
                                        start=True, stop=True)
                    ins.then_inc(wT_sum[s], 1)
                for s in range(2):
                    pe.wait_ge(wT_out[s], i + 1)
                    pe.wait_ge(v_rows[s], i + 1)
                    pe.wait_ge(state_done, 2 * i + s + 1)
                    for h in range(MH):
                        ins = group(pe, bank(s, 1)[:, head(h)],
                                    [(t[s]["W"][:, head(h)], t[s]["vb"][:, head(h)]),
                                     (t[s]["y"][:, head(h)], state[:, head(h)])])
                    ins.then_inc(v_sum[s], 1)
                    pe.wait_ge(v_out[s], i + 1)
                    pe.wait_ge(qg_done[s], i + 1)
                    for h in range(MH):
                        ins = group(pe, bank(s, 2)[:, head(h)],
                                    [(t[s]["qg"][:, head(h)], state[:, head(h)]),
                                     (t[s]["scores"][:, head(h)], t[s]["X"][:, head(h)])])
                    ins.then_inc(o_sum[s], 1)
                    for h in range(MH):
                        ins = pe.matmul(bank(s, 3)[:, head(h)], t[s]["ktail"][:, head(h)],
                                        t[s]["X"][:, head(h)], start=True, stop=True)
                    ins.then_inc(growth[s], 1)


def stage_mix_out(nc, d, m):
    with ExitStack() as ctx:
        def sb(name, shape, dt=F32):
            return ctx.enter_context(nc.sbuf_tensor(name, shape, dt))

        def sem(name):
            return nc.alloc_semaphore(name)

        w = sb("w_mix_out", [P, NH, DT, HALF])
        part = sb("mix_part", [P, 2, HALF])
        loaded, turned, turned_out, summed, gated, added = (sem("mix_" + n) for n in (
            "loaded", "turned", "turned_out", "summed", "gated", "added"))
        gate1 = m.mod[:, 2 * D:3 * D]
        ps = m.ps
        block = ctx.enter_context(nc.Block())

        @block.sync
        def _(sp):
            for n in range(NH):
                sp.dma_start(w[:, n], d["w_mix_out"][n]).then_inc(loaded, 16)

        @block.tensor
        def _(pe):
            for t in range(TT):
                if t >= 2:
                    pe.wait_ge(turned_out, t - 1)
                turn_tile(pe, ps, 2 * (t % 2), m.mixed[:, t, :], m.ident[:]).then_inc(turned, 1)
            pe.wait_ge(loaded, 16 * NH)
            pe.wait_ge(turned_out, TT)
            for i in range(NH * TT):
                t, n = i // NH, i % NH
                if i >= 4:
                    pe.wait_ge(gated, i - 3)
                group(pe, ps[:, 4 + i % 4, :], [(m.xT[:, k, t * P:(t + 1) * P], w[:, n, k, :])
                                                for k in range(DT)]).then_inc(summed, 1)

        @block.scalar
        def _(act):
            for t in range(TT):
                act.wait_ge(turned, t + 1)
                act.activation(m.xT[:, :, t * P:(t + 1) * P], two_banks(ps, 2 * (t % 2)), ACT.Copy
                               ).then_inc(turned_out, 1)

        @block.vector
        def _(dve):
            for i in range(NH * TT):
                t, n = i // NH, i % NH
                cols = slice(n * HALF, (n + 1) * HALF)
                dve.wait_ge(summed, i + 1)
                if i >= 2:
                    dve.wait_ge(added, i - 1)
                dve.tensor_tensor(part[:, i % 2], ps[:, 4 + i % 4, :], gate1[:, cols], ALU.mult
                                  ).then_inc(gated, 1)
                dve.wait_ge(gated, i + 1)
                dve.tensor_tensor(m.res[:, t, cols], m.res[:, t, cols], part[:, i % 2], ALU.add
                                  ).then_inc(added, 1)




def stage_route(nc, d, m):
    with ExitStack() as ctx:
        def sb(name, shape, dt=F32):
            return ctx.enter_context(nc.sbuf_tensor(name, shape, dt))

        def sem(name):
            return nc.alloc_semaphore(name)

        C = GROUPS + EXPERTS
        FAR = 64.0
        w = sb("w_route", [P, DT, C])
        bias = sb("route_bias", [P, C])
        ids = sb("token_ids", [P, TT])
        iota = sb("iota", [P, 64])
        zeros = sb("zero_slots", [BLOCKS, P])
        logits = sb("logits", [P, TT, C])
        g_top, g_sum, g_prob = sb("g_top", [P, TT]), sb("g_sum", [P, TT]), sb("g_prob", [P, TT])
        g_exp = sb("g_exp", [P, TT, GROUPS])
        g_hot = sb("g_hot", [P, TT, GROUPS])
        chosen = sb("chosen", [P, TT, EXPERTS])
        e_log = sb("e_log", [P, TT, PER_GROUP])
        e_top = sb("e_top", [P, TOP, TT])
        e_hot = sb("e_hot", [P, TOP, TT, PER_GROUP])
        key = sb("route_key", [P, TT, PER_GROUP])
        key_min = sb("route_key_min", [P, TT])
        second = sb("second", [P, TT])
        hot = sb("hot", [P, TOP, TT, EXPERTS])
        both = sb("both_hot", [P, TT, EXPERTS])
        place = sb("place", [P, TT, EXPERTS])
        carry = sb("route_carry", [P, TT + 1, EXPERTS])
        blocks = sb("expert_blocks", [P, EXPERTS])
        ends = sb("expert_ends", [P, 2, EXPERTS])
        slot_f = sb("slot_f", [P, TOP, TT])
        before_end = sb("before_end", [P, BLOCKS, EXPERTS])
        owner = sb("owner_f", [P, BLOCKS])
        table = sb("slot_rows", [BLOCKS, P])
        loaded, summed, exped, ranked, slots_ready = (sem("route_" + n) for n in (
            "loaded", "summed", "exped", "ranked", "slots_ready"))
        zeroed, cleared, scattered, read_back, turned = (sem("route_" + n) for n in (
            "zeroed", "cleared", "scattered", "read_back", "turned"))
        step = sem("route_step")
        both_ready, shifted = sem("route_both_ready"), sem("route_shifted")
        ps = m.ps
        block = ctx.enter_context(nc.Block())
        SCAN = 5

        @block.sync
        def _(sp):
            sp.dma_start(w[:], d["w_route"]).then_inc(loaded, 16)
            sp.dma_start(bias[:, 0:GROUPS], d["b_group"].partition_broadcast(P)).then_inc(loaded, 16)
            sp.dma_start(bias[:, GROUPS:C], d["b_expert"].partition_broadcast(P)).then_inc(loaded, 16)
            sp.dma_start(ids[:], d["token_ids"]).then_inc(loaded, 16)
            sp.dma_start(iota[:], d["iota"].partition_broadcast(P)).then_inc(loaded, 16)
            sp.wait_ge(zeroed, 1)
            sp.dma_start(d["slot_token"].rearrange("(b p) a -> b (p a)", p=P), zeros[:]).then_inc(cleared, 16)
            sp.wait_ge(scattered, 16 * TOP * TT)
            sp.dma_start(table[:], d["slot_token"].rearrange("(b p) a -> b (p a)", p=P)).then_inc(read_back, 16)

        @block.gpsimd
        def _(pool):
            pool.wait_ge(loaded, 80)
            pool.wait_ge(cleared, 16)
            pool.wait_ge(slots_ready, 1)
            for j in range(TOP):
                for t in range(TT):
                    pool.indirect_dma_start(
                        d["slot_token"], bass.IndirectOffsetOnAxis(ap=m.slot[:, j, t:t + 1], axis=0),
                        ids[:, t:t + 1], None).then_inc(scattered, 16)

        @block.tensor
        def _(pe):
            pe.wait_ge(loaded, 80)
            for t in range(TT):
                ins = group(pe, ps[:, 0, t * C:(t + 1) * C],
                            [(m.xT[:, k, t * P:(t + 1) * P], w[:, k, :]) for k in range(DT)])
            ins.then_inc(summed, 1)
            pe.wait_ge(both_ready, 1)
            flat = both[:].rearrange("p t e -> p (t e)")
            pe.matmul(ps[:, 1, 0:TT * EXPERTS], m.before[:], flat, start=True, stop=True)
            pe.matmul(ps[:, 2, 0:TT * EXPERTS], m.ones[:], flat, start=True, stop=True).then_inc(ranked, 1)
            pe.wait_ge(read_back, 16)
            pe.transpose(ps[:, 3, 0:BLOCKS], table[:], m.ident[0:BLOCKS, 0:BLOCKS]).then_inc(turned, 1)

        @block.scalar
        def _(act):
            act.wait_ge(shifted, 1)
            act.activation(g_exp[:], g_exp[:], ACT.Exp).then_inc(exped, 1)
            act.wait_ge(shifted, 2)
            act.activation(second[:], second[:], ACT.Exp).then_inc(exped, 1)

        @block.vector
        def _(dve):
            done = 0

            def then(ins):
                nonlocal done
                done += 1
                ins.then_inc(step, 1)
                dve.wait_ge(step, done)

            def along(ap, n):
                return ap.unsqueeze(2).to_broadcast([P, TT, n])

            def row(ap, n):
                return ap.unsqueeze(1).to_broadcast([P, TT, n])

            def first_top(values, top, out, n):
                k = key[:, :, 0:n]
                then(dve.tensor_tensor(k, values, along(top, n), ALU.is_equal))
                then(dve.scalar_tensor_tensor(k, k, -FAR, row(iota[:, 0:n], n), ALU.mult, ALU.add))
                then(dve.tensor_reduce(key_min[:], k, AX_X, ALU.min))
                then(dve.tensor_tensor(out, k, along(key_min[:], n), ALU.is_equal))

            dve.memset(zeros[:], 0.0).then_inc(zeroed, 1)
            dve.wait_ge(loaded, 80)
            dve.wait_ge(summed, 1)
            then(dve.tensor_tensor(logits[:], ps[:, 0, 0:TT * C].rearrange("p (t c) -> p t c", c=C),
                                   row(bias[:], C), ALU.add))
            lg = logits[:, :, 0:GROUPS]
            then(dve.tensor_reduce(g_top[:], lg, AX_X, ALU.max))
            dve.tensor_tensor(g_exp[:], lg, along(g_top[:], GROUPS), ALU.subtract).then_inc(shifted, 1)
            first_top(lg, g_top[:], g_hot[:], GROUPS)
            le = logits[:, :, GROUPS:C].rearrange("p t (g e) -> p t g e", g=GROUPS)
            ch = chosen[:].rearrange("p t (g e) -> p t g e", g=GROUPS)
            hot_g = g_hot[:].unsqueeze(3).to_broadcast([P, TT, GROUPS, PER_GROUP])
            then(dve.tensor_tensor(ch, le, hot_g, ALU.mult))
            then(dve.tensor_reduce(e_log[:], chosen[:].rearrange("p t (g e) -> p t e g", g=GROUPS), AX_X,
                                   ALU.add))
            then(dve.tensor_reduce(e_top[:, 0, :], e_log[:], AX_X, ALU.max))
            first_top(e_log[:], e_top[:, 0, :], e_hot[:, 0], PER_GROUP)
            then(dve.scalar_tensor_tensor(e_log[:], e_hot[:, 0], MASKED, e_log[:], ALU.mult, ALU.add))
            then(dve.tensor_reduce(e_top[:, 1, :], e_log[:], AX_X, ALU.max))
            first_top(e_log[:], e_top[:, 1, :], e_hot[:, 1], PER_GROUP)
            dve.tensor_tensor(second[:], e_top[:, 1, :], e_top[:, 0, :], ALU.subtract).then_inc(shifted, 1)
            for j in range(TOP):
                h = hot[:, j].rearrange("p t (g e) -> p t g e", g=GROUPS)
                then(dve.tensor_copy(h, e_hot[:, j].unsqueeze(2).to_broadcast([P, TT, GROUPS, PER_GROUP])))
                then(dve.tensor_tensor(h, h, hot_g, ALU.mult))
            dve.tensor_tensor(both[:], hot[:, 0], hot[:, 1], ALU.add).then_inc(both_ready, 1)
            dve.wait_ge(exped, 2)
            then(dve.tensor_reduce(g_sum[:], g_exp[:], AX_X, ALU.add))
            then(dve.reciprocal(g_prob[:], g_sum[:]))
            then(dve.tensor_scalar(g_sum[:], second[:], 1.0, None, ALU.add))
            then(dve.reciprocal(g_sum[:], g_sum[:]))
            then(dve.tensor_tensor(m.gate[:, 0, :], g_prob[:], g_sum[:], ALU.mult))
            then(dve.tensor_tensor(m.gate[:, 1, :], m.gate[:, 0, :], second[:], ALU.mult))
            dve.wait_ge(ranked, 1)
            total = ps[:, 2, 0:TT * EXPERTS].rearrange("p (t e) -> p t e", e=EXPERTS)
            then(dve.memset(carry[:, 0, :], 0.0))
            for t in range(TT):
                then(dve.tensor_tensor(carry[:, t + 1, :], carry[:, t, :], total[:, t, :], ALU.add))
            then(dve.tensor_scalar(blocks[:], carry[:, TT, :], 1.0 / P, (P - 1.0) / P - 0.5 + 0.5 / P,
                                   ALU.mult, ALU.add))
            then(dve.tensor_scalar(blocks[:], blocks[:], ROUND, ROUND, ALU.add, ALU.subtract))
            then(dve.tensor_copy(ends[:, 0, :], blocks[:]))
            for n in range(SCAN):
                by, a, b = 2 ** n, ends[:, n % 2, :], ends[:, (n + 1) % 2, :]
                then(dve.tensor_copy(b[:, 0:by], a[:, 0:by]))
                then(dve.tensor_tensor(b[:, by:], a[:, by:], a[:, 0:EXPERTS - by], ALU.add))
            end, start = ends[:, SCAN % 2, :], ends[:, (SCAN + 1) % 2, :]
            then(dve.tensor_tensor(start, end, blocks[:], ALU.subtract))
            then(dve.tensor_tensor(place[:], ps[:, 1, 0:TT * EXPERTS].rearrange("p (t e) -> p t e", e=EXPERTS),
                                   carry[:, 0:TT, :], ALU.add))
            then(dve.scalar_tensor_tensor(place[:], row(start, EXPERTS), float(P), place[:], ALU.mult, ALU.add))
            for j in range(TOP):
                then(dve.tensor_tensor(hot[:, j], hot[:, j], place[:], ALU.mult))
                then(dve.tensor_reduce(slot_f[:, j, :], hot[:, j], AX_X, ALU.add))
            dve.tensor_copy(m.slot[:], slot_f[:]).then_inc(slots_ready, 1)
            then(dve.tensor_tensor(before_end[:], end.unsqueeze(1).to_broadcast([P, BLOCKS, EXPERTS]),
                                   iota[:, 0:BLOCKS].unsqueeze(2).to_broadcast([P, BLOCKS, EXPERTS]),
                                   ALU.is_le))
            then(dve.tensor_reduce(owner[:], before_end[:], AX_X, ALU.add))
            then(dve.tensor_scalar(owner[:], owner[:], float(EXPERTS - 1), None, ALU.min))
            dve.tensor_copy(m.owner[:], owner[:])
            then(dve.tensor_scalar(blocks[:], end, 0.5, 0.25 - 1.0, ALU.mult, ALU.add))
            then(dve.tensor_scalar(blocks[:], blocks[:], ROUND, ROUND, ALU.add, ALU.subtract))
            dve.tensor_copy(m.last_pair[:], blocks[:, EXPERTS - 1:EXPERTS])
            dve.memset(m.slot_token[:, BLOCKS:], 0.0)
            dve.wait_ge(turned, 1)
            dve.tensor_copy(m.slot_token[:, 0:BLOCKS], ps[:, 3, 0:BLOCKS])


def stage_experts(nc, d, m):
    with ExitStack() as ctx:
        def sb(name, shape, dt=F32):
            return ctx.enter_context(nc.sbuf_tensor(name, shape, dt))

        def sem(name):
            return nc.alloc_semaphore(name)

        def two(name):
            return [sem(name + "0"), sem(name + "1")]

        HT = DE // P
        w13 = sb("w13", [P, 2, 2, DT, DE])
        w2 = sb("w2", [P, 2, HT, D])
        spare = sb("moe_spare", [P, 1])
        index = [sb("slot_index0", [P, 1], U32), sb("slot_index1", [P, 1], U32)]
        tiles = [m.xT[:, k, :] for k in range(DT)]
        x = tiles[0:2]
        xT = [tiles[2].rearrange("p (k n) -> p k n", n=P), tiles[3].rearrange("p (k n) -> p k n", n=P)]
        y = tiles[4:6]
        hid = [tiles[6][:, 0:DE], tiles[6][:, DE:2 * DE]]
        hidT = [tiles[7][:, 0:DE], tiles[7][:, DE:2 * DE]]
        w13_loaded, w2_loaded, indexed, gathered, stored = (two("moe_" + n) for n in (
            "w13_loaded", "w2_loaded", "indexed", "gathered", "stored"))
        x_turned, x_out, up, silued, hid_done, hid_turned, hidT_out, down, y_out = (sem("moe_" + n) for n in (
            "x_turned", "x_out", "up", "silued", "hid_done", "hid_turned", "hidT_out", "down", "y_out"))
        ps = m.ps
        block = ctx.enter_context(nc.Block())

        def over_pairs(eng, body):
            last = eng.value_load(m.last_pair[0:1, 0:1], min_val=SLOTS_MIN // (2 * P) - 1,
                                  max_val=BLOCKS // 2 - 1)
            for s in range(2):
                body(0, s)
            with eng.Fori(1, last + 1) as i:
                for s in range(2):
                    body(i, s)
            return last

        def earlier(eng, sem, value):
            if not isinstance(value, int) or value > 0:
                eng.wait_ge(sem, value)

        @block.sync
        def _(sp):
            def load(i, s):
                b = 2 * i + s
                expert = sp.value_load(m.owner[0:1, ds(b, 1)], min_val=0, max_val=EXPERTS - 1)
                earlier(sp, up, 2 * (b - 1))
                sp.dma_start(w13[:, s], d["w13"][ds(expert, 1)].rearrange("a p j k n -> p (a j) k n")
                             ).then_inc(w13_loaded[s], 16)
                earlier(sp, down, 2 * (b - 1))
                sp.dma_start(w2[:, s], d["w2"][ds(expert, 1)].rearrange("a p k n -> p (a k) n")
                             ).then_inc(w2_loaded[s], 16)

            over_pairs(sp, load)

        @block.gpsimd
        def _(pool):
            def gather(b, s, nth):
                pool.tensor_copy(index[s][:], m.slot_token[:, ds(b, 1)]).then_inc(indexed[s], 1)
                pool.wait_ge(indexed[s], nth)
                pool.tensor_tensor(spare[:], m.ident[:, 0:1], m.ident[:, 1:2], ALU.add)
                pool.indirect_dma_start(x[s], None, d["h2_rows"],
                                        bass.IndirectOffsetOnAxis(ap=index[s][:], axis=0)
                                        ).then_inc(gathered[s], 16)

            def gather_ahead(i, s):
                b = 2 * i + s
                pool.wait_ge(x_turned, b + 1)
                gather(b + 2, s, i + 2)

            for s in range(2):
                gather(s, s, 1)
            last = over_pairs(pool, gather_ahead)
            for s in range(2):
                pool.wait_ge(gathered[s], 16 * last + 32)
            for s in range(2):
                pool.wait_ge(stored[s], 16 * last + 16)

        @block.tensor
        def _(pe):
            def turn_x(s, count):
                pe.wait_ge(gathered[s], 16 * count)
                turn_tile(pe, ps, 0, x[s], m.ident[:]).then_inc(x_turned, 1)

            def multiply_down(b, o, nth):
                pe.wait_ge(hidT_out, b + 1)
                pe.wait_ge(w2_loaded[o], 16 * nth)
                earlier(pe, y_out, NH * b)
                for n in range(NH):
                    group(pe, ps[:, 5 + n, :], [(hidT[o][:, k * P:(k + 1) * P],
                                                 w2[:, o, k, n * HALF:(n + 1) * HALF]) for k in range(HT)]
                          ).then_inc(down, 1)

            def step(i, s):
                o, b = 1 - s, 2 * i + s
                pe.wait_ge(w13_loaded[s], 16 * (i + 1))
                pe.wait_ge(x_out, b + 1)
                earlier(pe, hid_done, b)
                for j in range(2):
                    group(pe, ps[:, 2 + j, :], [(xT[s][:, k, :], w13[:, s, j, k, :]) for k in range(DT)]
                          ).then_inc(up, 1)
                turn_x(o, i + 1 + s)
                if not (isinstance(i, int) and b == 0):
                    multiply_down(b - 1, o, i + s)
                pe.wait_ge(hid_done, b + 1)
                earlier(pe, hidT_out, b)
                for k in range(HT):
                    ins = pe.transpose(ps[:, 4, k * P:(k + 1) * P], hid[s][:, k * P:(k + 1) * P], m.ident[:])
                ins.then_inc(hid_turned, 1)

            turn_x(0, 1)
            last = over_pairs(pe, step)
            multiply_down(2 * last + 1, 1, last + 1)

        @block.scalar
        def _(act):
            def store(b, o):
                act.wait_ge(y_out, NH * b + NH)
                act.dma_start(d["y_rows"][ds(b * P, P), :], y[o]).then_inc(stored[o], 16)

            def step(i, s):
                o, b = 1 - s, 2 * i + s
                act.wait_ge(up, 2 * b + 1)
                earlier(act, hid_turned, b - 1)
                act.activation(hid[s], ps[:, 2, :], ACT.Silu).then_inc(silued, 1)
                act.wait_ge(x_turned, b + 2)
                earlier(act, up, 2 * b)
                act.activation(xT[o], two_banks(ps, 0), ACT.Copy).then_inc(x_out, 1)
                act.wait_ge(hid_turned, b + 1)
                earlier(act, down, 2 * (b - 1))
                act.activation(hidT[s], ps[:, 4, :], ACT.Copy).then_inc(hidT_out, 1)
                if not (isinstance(i, int) and b == 0):
                    store(b - 1, o)

            act.wait_ge(x_turned, 1)
            act.activation(xT[0], two_banks(ps, 0), ACT.Copy).then_inc(x_out, 1)
            last = over_pairs(act, step)
            store(2 * last + 1, 1)

        @block.vector
        def _(dve):
            def copy_out(b, o, before):
                earlier(dve, stored[o], 16 * before)
                for n in range(NH):
                    dve.wait_ge(down, 2 * b + n + 1)
                    dve.tensor_copy(y[o][:, n * HALF:(n + 1) * HALF], ps[:, 5 + n, :]).then_inc(y_out, 1)

            def step(i, s):
                b = 2 * i + s
                dve.wait_ge(silued, b + 1)
                dve.wait_ge(up, 2 * b + 2)
                dve.tensor_tensor(hid[s], hid[s], ps[:, 3, :], ALU.mult).then_inc(hid_done, 1)
                if not (isinstance(i, int) and b == 0):
                    copy_out(b - 1, 1 - s, i - 1 + s)

            last = over_pairs(dve, step)
            copy_out(2 * last + 1, 1, last)


def stage_final(nc, d, m, out):
    with ExitStack() as ctx:
        def sb(name, shape, dt=F32):
            return ctx.enter_context(nc.sbuf_tensor(name, shape, dt))

        def sem(name):
            return nc.alloc_semaphore(name)

        y = [[sb(f"y{j}{s}", [P, D]) for s in range(2)] for j in range(TOP)]
        square = sb("fin_square", [P, D])
        ss = sb("fin_ss", [P, TT])
        inv = sb("fin_inv", [P, TT])
        w = sb("fin_w", [P, D])
        gathered = [sem("fin_gathered0"), sem("fin_gathered1")]
        loaded, first, gated, added, squared, meaned, rooted, inverted, normed, stored = (
            sem("fin_" + n) for n in ("loaded", "first", "gated", "added", "squared", "meaned",
                                      "rooted", "inverted", "normed", "stored"))
        gate2 = m.mod[:, 5 * D:6 * D]
        block = ctx.enter_context(nc.Block())

        @block.gpsimd
        def _(pool):
            for t in range(TT):
                s = t % 2
                if t >= 2:
                    pool.wait_ge(added, t - 1)
                for j in range(TOP):
                    pool.indirect_dma_start(y[j][s][:], None, d["y_rows"],
                                            bass.IndirectOffsetOnAxis(ap=m.slot[:, j, t:t + 1], axis=0)
                                            ).then_inc(gathered[s], 16)

        @block.vector
        def _(dve):
            for t in range(TT):
                s = t % 2
                dve.wait_ge(gathered[s], 16 * TOP * (t // 2 + 1))
                dve.tensor_scalar(y[0][s][:], y[0][s][:], m.gate[:, 0, t:t + 1], None, ALU.mult
                                  ).then_inc(first, 1)
                dve.wait_ge(first, t + 1)
                dve.scalar_tensor_tensor(y[0][s][:], y[1][s][:], m.gate[:, 1, t:t + 1], y[0][s][:], ALU.mult,
                                         ALU.add).then_inc(gated, 1)
                dve.wait_ge(gated, 2 * t + 1)
                dve.tensor_tensor(y[0][s][:], y[0][s][:], gate2, ALU.mult).then_inc(gated, 1)
                dve.wait_ge(gated, 2 * t + 2)
                dve.tensor_tensor(m.res[:, t, :], m.res[:, t, :], y[0][s][:], ALU.add).then_inc(added, 1)
            dve.wait_ge(squared, TT)
            dve.tensor_scalar(ss[:], ss[:], 1.0 / D, EPS, ALU.mult, ALU.add).then_inc(meaned, 1)
            dve.wait_ge(rooted, 1)
            dve.reciprocal(inv[:], ss[:]).then_inc(inverted, 1)
            dve.wait_ge(inverted, 1)
            dve.wait_ge(loaded, 16)
            for t in range(TT):
                dve.scalar_tensor_tensor(m.res[:, t, :], m.res[:, t, :], inv[:, t:t + 1], w[:], ALU.mult,
                                         ALU.mult).then_inc(normed, 1)

        @block.scalar
        def _(act):
            for t in range(TT):
                act.wait_ge(added, t + 1)
                if t:
                    act.wait_ge(squared, t)
                act.activation(square[:], m.res[:, t, :], ACT.Square, accum_out=ss[:, t:t + 1]
                               ).then_inc(squared, 1)
            act.wait_ge(meaned, 1)
            act.activation(ss[:], ss[:], ACT.Sqrt).then_inc(rooted, 1)

        @block.sync
        def _(sp):
            sp.dma_start(w[:], d["final_norm_w"].partition_broadcast(P)).then_inc(loaded, 16)
            for t in range(TT):
                sp.wait_ge(normed, t + 1)
                sp.dma_start(out[:, t, :], m.res[:, t, :]).then_inc(stored, 16)
            sp.wait_ge(stored, 16 * TT)




class Memory:
    pass


CONSTS = ["ident", "ones", "upto", "before", "ahead"]


def retention_tables():
    log_gamma = np.log1p(-(2.0 ** (-5.0 - np.arange(MH))))
    j, i = np.meshgrid(np.arange(P), np.arange(P), indexing="ij")
    scale = MHD ** -0.5
    rel = np.maximum(i - j, 0)
    decay = np.where(i >= j, np.exp(log_gamma[:, None, None] * rel), 0.0) * scale
    qdecay = np.broadcast_to(np.exp(log_gamma[:, None, None] * (i[None] + 1.0)), (MH, P, P))
    sdecay = np.broadcast_to(np.exp(log_gamma * P)[:, None, None], (MH, P, P))
    tables = np.stack([decay, qdecay, sdecay]).transpose(2, 0, 1, 3).reshape(P, 3, MW)
    kdecay = np.exp(log_gamma[None, :] * (P - 1 - np.arange(P))[:, None]) * scale
    return np.ascontiguousarray(tables, np.float32), np.ascontiguousarray(kdecay, np.float32)


def constants():
    i, j = np.meshgrid(np.arange(P), np.arange(P), indexing="ij")
    blocks = {
        "ident": i == j,
        "ones": i >= 0,
        "upto": i <= j,
        "before": i < j,
        "ahead": (j > i) * MASKED,
    }
    return np.concatenate([np.asarray(blocks[n], np.float32) for n in CONSTS], 1)


def build_program(nc, d, out):
    with ExitStack() as ctx:
        m = Memory()
        m.ps = ctx.enter_context(nc.psum_tensor("ps", [P, 8, HALF], F32))
        m.consts = ctx.enter_context(nc.sbuf_tensor("consts", [P, P * len(CONSTS)], F32))
        m.consts_loaded = ctx.enter_context(nc.semaphore("consts_loaded"))
        m.ident, m.ones, m.upto, m.before, m.ahead = (
            m.consts[:, n * P:(n + 1) * P] for n in range(len(CONSTS)))

        def sb(stack, name, shape, dt=F32, side=None):
            return stack.enter_context(nc.sbuf_tensor(name, shape, dt, side=side))

        m.ident16 = sb(ctx, "ident16", [P, P], BF16)
        m.ahead16 = sb(ctx, "ahead16", [P, P], BF16)
        m.ones16 = sb(ctx, "ones16", [P, P], BF16)
        first_block(nc, d, m, sb, ctx)
        m.mod = sb(ctx, "mod", [P, N_MOD * D])
        stage_per_layer_input(nc, d, m)
        second_block(nc, d, m, sb, out)


def first_block(nc, d, m, sb, ctx):
    right = ExitStack()
    with ExitStack() as s1:
        m.v = sb(s1, "v", [P, TT, D])
        m.res = m.v
        m.o = sb(s1, "o", [P, TT, D])
        with ExitStack() as s2:
            m.xT = sb(s2, "x0T", [P, DT, T])
            m.negc = sb(s2, "negc", [3, HEADS, T], BF16)
            with nc.cleanup_on_exit():
                stage_values(nc, d, m)
                stage_attention(nc, d, m)
        m.x_high = sb(right, "x1T_high", [P, DT, T], F32R, "right")
        m.x_low = sb(right, "x1T_low", [P, DT, T], F32R, "right")
        with nc.cleanup_on_exit():
            stage_attention_out(nc, d, m)
    with ExitStack() as s1:
        m.hT = sb(s1, "hT", [P, FT, T])
        with nc.cleanup_on_exit():
            stage_ffn_up(nc, d, m)
        right.close()
        m.res = sb(ctx, "res", [P, TT, D], F32, "right")
        m.xT = sb(ctx, "xT", [P, DT, T], F32, "right")
        with nc.cleanup_on_exit():
            stage_ffn_down(nc, d, m)


def second_block(nc, d, m, sb, out):
    with ExitStack() as s1:
        m.mixed = sb(s1, "mixed", [P, TT, D])
        m.ab = sb(s1, "ab", [P, TT, 2 * MH])
        with nc.cleanup_on_exit():
            stage_modulation(nc, d, m)
            stage_modulated_norm(nc, d, m, "norm1", False)
            with ExitStack() as s2:
                m.r_qkv = sb(s2, "r_qkv", [P, 3, TT, MW])
                stage_project_rows(nc, d, m)
                m.cos = sb(s2, "cos", [P, TT, MHD // 2])
                m.sin = sb(s2, "sin", [P, TT, MHD // 2])
                stage_rotary_tables(nc, d, m)
                stage_retention(nc, d, m)
                stage_head_norm(nc, d, m, "ret_norm", [heads_of(m.r_qkv[:, 0, t, :]) for t in range(TT)],
                                [heads_of(m.r_qkv[:, 1, t, :]) for t in range(TT)],
                                [heads_of(m.mixed[:, t, 0:MW]) for t in range(TT)], None)
        with ExitStack() as s2:
            m.qkv = sb(s2, "qkv", [P, QKV, T])
            stage_project_cols(nc, d, m)
            m.dn_g, m.dn_cum, m.dn_last, m.dn_tail, m.dn_bexp, m.dn_beta = (
                sb(s2, "dn_" + name, [P, TT, MH]) for name in ("g", "cum", "last", "tail", "bexp", "beta"))
            with nc.cleanup_on_exit():
                stage_delta_gates(nc, d, m)
                stage_delta(nc, d, m)
            stage_head_norm(nc, d, m, "dn_norm", [m.qkv[:, 0:MH, t * P:(t + 1) * P] for t in range(TT)],
                            [m.qkv[:, MH:2 * MH, t * P:(t + 1) * P] for t in range(TT)],
                            [heads_of(m.mixed[:, t, MW:2 * MW]) for t in range(TT)], d["dn_norm_w"])
        stage_mix_out(nc, d, m)
    stage_modulated_norm(nc, d, m, "norm2", True)
    with ExitStack() as s1:
        m.gate = sb(s1, "gate", [P, TOP, TT])
        m.slot = sb(s1, "slot", [P, TOP, TT], U32)
        m.owner = sb(s1, "owner", [P, BLOCKS], I32)
        m.last_pair = sb(s1, "last_pair", [P, 1], I32)
        m.slot_token = sb(s1, "slot_token", [P, BLOCKS + 2], U32)
        stage_route(nc, d, m)
        stage_experts(nc, d, m)
        stage_final(nc, d, m, out)


def delta_masks():
    i, j = np.meshgrid(np.arange(P), np.arange(P), indexing="ij")
    levels = [(i >> (n + 1) == j >> (n + 1)) & (i >> n & 1 == 1) & (j >> n & 1 == 0) for n in range(LEVELS)]
    masks = [np.where(j >= i, 0.0, MASKED), np.where(j < i, 0.0, MASKED)] + levels
    return np.ascontiguousarray(np.stack(masks, 1), np.float32)


def l2_tables():
    n = 2 * MH
    eye = np.eye(n, dtype=np.float32)
    scale = np.where(np.arange(n) < MH, MHD ** -0.5, 1.0).astype(np.float32)
    pick = np.broadcast_to(eye[None], (P, n, n))
    spread = np.broadcast_to((eye * scale)[:, :, None], (n, n, P))
    return np.ascontiguousarray(pick), np.ascontiguousarray(spread)


def cols_of(a):
    return np.ascontiguousarray(a.T.reshape(-1, P, a.shape[0]).transpose(1, 0, 2))


def rows_of(a):
    return np.ascontiguousarray(a.reshape(-1, P, a.shape[1]).transpose(1, 0, 2))


def chunks_of(w, width):
    k, n = w.shape
    return np.ascontiguousarray(w.reshape(k // P, P, n // width, width).transpose(2, 1, 0, 3))


def kernel(**inputs):
    import concourse.bacc as bacc
    import concourse.bass_utils as bass_utils

    a = {k: np.asarray(v) for k, v in inputs.items()}
    w_in, w_in2 = a["attn_w_in"][0], a["w_in_2"][0]
    tables, kdecay = retention_tables()
    l2_pick, l2_spread = l2_tables()
    arrays = {
        "x": rows_of(a["x"][0]),
        "xT": cols_of(a["x"][0]),
        "attn_w": chunks_of(w_in[:, :3 * D], HALF),
        "attn_wqk": np.ascontiguousarray(
            np.concatenate([chunks_of(w_in[:, :D], P), chunks_of(w_in[:, D:2 * D], P)], 3)),
        "attn_wf": rows_of(w_in[:, 3 * D:]),
        "attn_bf": a["attn_b_f"][0],
        "attn_w_out": chunks_of(a["attn_w_out"][0], HALF),
        "ln_mix_g": a["ln_mix_g"][0], "ln_mix_b": a["ln_mix_b"][0],
        "ln_ffn_g": a["ln_ffn_g"][0], "ln_ffn_b": a["ln_ffn_b"][0],
        "ffn_w_up": np.ascontiguousarray(np.concatenate(
            [chunks_of(a["ffn_w_up"][0][:, :FFN], P), chunks_of(a["ffn_w_up"][0][:, FFN:], P)], 3)),
        "ffn_taps": np.ascontiguousarray(a["ffn_conv_w"][0].T.reshape(FT, P, 3).transpose(1, 0, 2)),
        "ffn_bias": np.ascontiguousarray(a["ffn_conv_b"][0].reshape(FT, P).T),
        "ffn_w_down": a["ffn_w_down"][0].reshape(FT, P, D),
        "ple_w_proj": rows_of(a["ple_w_proj"][0]),
        "ple_w_gate": chunks_of(a["ple_w_gate"][0], HALF),
        "ple_b_gate": a["ple_b_gate"][0],
        "pT": cols_of(a["p"][0, 0]),
        "c": np.ascontiguousarray(a["c_2"].reshape(DT, P).T),
        "w_ada": np.ascontiguousarray(a["w_ada_2"][0].reshape(DT, P, N_MOD, D).transpose(0, 2, 1, 3)),
        "consts": constants(),
        "b_ada": a["b_ada_2"][0],
        "norm1_w": a["norm1_w_2"][0], "norm2_w": a["norm2_w_2"][0],
        "w_rows": chunks_of(np.concatenate([w_in2[:, 3 * MW:4 * MW], w_in2[:, 7 * MW:8 * MW],
                                            w_in2[:, :3 * MW]], 1), HALF),
        "w_ab": rows_of(w_in2[:, 8 * MW:]),
        "w_cols": chunks_of(w_in2[:, 4 * MW:7 * MW], P),
        "dn_taps": np.ascontiguousarray(a["conv_w_2"][0].T.reshape(QKV, P, 4).transpose(1, 0, 2)),
        "positions": np.ascontiguousarray(a["positions_2"][0].reshape(TT, P).T),
        "freq": (ROPE_THETA ** (-np.arange(0, MHD, 2, dtype=np.float32) / MHD)).astype(np.float32),
        "dt_bias": a["dt_bias_2"][0], "a_log": a["a_log_2"][0],
        "l2_pick": l2_pick, "l2_spread": l2_spread,
        "dn_masks": delta_masks(), "dn_norm_w": a["dn_norm_w_2"][0],
        "w_mix_out": chunks_of(a["w_out_2"][0], HALF),
        "w_route": rows_of(np.concatenate([a["w_group_2"][0], a["w_expert_2"][0]], 1)),
        "b_group": a["b_group_2"][0], "b_expert": a["b_expert_2"][0],
        "token_ids": np.arange(T, dtype=np.float32).reshape(TT, P).T.copy(),
        "iota": np.arange(64, dtype=np.float32),
        "w13": np.ascontiguousarray(np.stack([a["w1_2"][0], a["w3_2"][0]], 1)
                                    .reshape(EXPERTS, 2, DT, P, DE).transpose(0, 3, 1, 2, 4)),
        "w2": np.ascontiguousarray(a["w2_2"][0].reshape(EXPERTS, DE // P, P, D).transpose(0, 2, 1, 3)),
        "final_norm_w": a["final_norm_w_2"],
        "ret_tables": tables, "ret_kdecay": kdecay,
    }
    nc = bacc.Bacc("TRN2", target_bir_lowering=False, num_devices=1)
    d = {k: nc.dram_tensor("in_" + k, v.shape, mybir.dt.from_np(v.dtype), kind="ExternalInput").ap()
         for k, v in arrays.items()}
    out = nc.dram_tensor("out", (P, TT, D), F32, kind="ExternalOutput").ap()
    d["slot_token"] = nc.dram_tensor("slot_rows_dram", (SLOTS, 1), F32, kind="Internal").ap()
    d["y_rows"] = nc.dram_tensor("y_rows", (SLOTS, D), F32, kind="Internal").ap()
    d["x1_rows"] = nc.dram_tensor("x1_rows", (P, TT, D), F32, kind="Internal").ap()
    d["h2_rows"] = nc.dram_tensor("h2_rows", (T, D), F32, kind="Internal").ap()
    build_program(nc, d, out)
    r = bass_utils.run_bass_kernel_spmd(nc, [{"in_" + k: v for k, v in arrays.items()}], core_ids=[0])
    got = r.results[0]["out"]
    return np.ascontiguousarray(got.transpose(1, 0, 2)).reshape(1, T, D)
```
